# Optimizing a Trainium2 kernel written in Bass

```python
import jax, jax.numpy as jnp
from jax import lax
import numpy as np

D_MODEL = 1024
BATCH = 1
SEQ = 512
DEPTH = 1

EPS = 1e-6
NEG_INF = -1e30

N_ATTN_HEADS = 8
ATTN_HEAD_DIM = 64
ATTN_V_DIM = 2 * ATTN_HEAD_DIM
QK_WIDTH = N_ATTN_HEADS * 2 * ATTN_HEAD_DIM
ATTN_WIDTH = N_ATTN_HEADS * ATTN_V_DIM
ROT_DIM = ATTN_HEAD_DIM // 4
ROPE_THETA = 500000.0
Q_BLOCK = 128

POOL_WINDOWS = (2, 4, 8, 16)
N_POOL_GROUPS = len(POOL_WINDOWS)
POOL_WIDTH = D_MODEL
POOL_GROUP_DIM = POOL_WIDTH // N_POOL_GROUPS

IN_WIDTH = 2 * QK_WIDTH + ATTN_WIDTH + POOL_WIDTH
N_BRANCHES = 2
N_MOD = 6

PEER_HEADS = 8
N_KEYS = 128
N_EXPERTS = N_KEYS * N_KEYS
PEER_QUERY_DIM = 256
PEER_HALF = PEER_QUERY_DIM // 2
PEER_TOPK = 16
PEER_TOKEN_BLOCK = 128

kernel_name = "hybrid_pool_diffattn_peer_block"

def rms_norm(x, gain):
    xf = x.astype(jnp.float32)
    y = xf * lax.rsqrt(jnp.mean(xf * xf, axis=-1, keepdims=True) + EPS)
    return (y * gain.astype(jnp.float32)).astype(x.dtype)

def rope_partial(t, cos, sin):
    half = ROT_DIM // 2
    c = cos[:, :, None, None, :]
    s = sin[:, :, None, None, :]
    t1 = t[..., :half].astype(jnp.float32)
    t2 = t[..., half:ROT_DIM].astype(jnp.float32)
    rot = jnp.concatenate([t1 * c - t2 * s, t2 * c + t1 * s], axis=-1).astype(t.dtype)
    return jnp.concatenate([rot, t[..., ROT_DIM:]], axis=-1)

def causal_multiscale_pool(xp):
    S = xp.shape[1]
    xf = xp.astype(jnp.float32)
    cs = jnp.cumsum(xf, axis=1)
    t = jnp.arange(S)
    outs = []
    for g, w in enumerate(POOL_WINDOWS):
        csg = cs[:, :, g]
        lag = jnp.pad(csg, ((0, 0), (w, 0), (0, 0)))[:, :S]
        cnt = jnp.minimum(t + 1, w).astype(jnp.float32)[None, :, None]
        outs.append((csg - lag) / cnt - xf[:, :, g])
    return jnp.stack(outs, axis=2).astype(xp.dtype)

def diff_attention(q, k, v, lam):
    S = q.shape[1]
    scale = ATTN_HEAD_DIM ** -0.5
    outs = []
    for i in range(S // Q_BLOCK):
        lo, hi = i * Q_BLOCK, (i + 1) * Q_BLOCK
        qb, kb, vb = q[:, lo:hi], k[:, :hi], v[:, :hi]
        s = jnp.einsum('bqhcd,bkhcd->bhcqk', qb, kb).astype(jnp.float32) * scale
        mask = (lo + jnp.arange(Q_BLOCK))[:, None] >= jnp.arange(hi)[None, :]
        p = jax.nn.softmax(jnp.where(mask, s, NEG_INF), axis=-1)
        a = p[:, :, 0] - lam * p[:, :, 1]
        outs.append(jnp.einsum('bhqk,bkhd->bqhd', a.astype(vb.dtype), vb))
    return jnp.concatenate(outs, axis=1)

def _peer_block(hb, ib, gb, down, up):
    u = down[ib]
    pre = jnp.einsum('td,thkd->thk', hb, u).astype(jnp.float32)
    w = (gb * jax.nn.gelu(pre, approximate=False)).astype(hb.dtype)
    return jnp.einsum('thk,thkd->td', w, up[ib])

def peer(h, w_query, sub_keys, down, up):
    B, S, D = h.shape
    T = B * S
    hf = h.reshape(T, D)
    q = (hf @ w_query).reshape(T, PEER_HEADS, 2, PEER_HALF)
    s = jnp.einsum('thpd,pkd->thpk', q, sub_keys).astype(jnp.float32)
    sv, si = lax.top_k(s, PEER_TOPK)
    cand = (sv[:, :, 0, :, None] + sv[:, :, 1, None, :]).reshape(T, PEER_HEADS, PEER_TOPK * PEER_TOPK)
    cand_idx = (si[:, :, 0, :, None] * N_KEYS + si[:, :, 1, None, :]).reshape(T, PEER_HEADS, PEER_TOPK * PEER_TOPK)
    top_s, top_pos = lax.top_k(cand, PEER_TOPK)
    idx = jnp.take_along_axis(cand_idx, top_pos, axis=-1)
    g = jax.nn.softmax(top_s, axis=-1)
    nb = T // PEER_TOKEN_BLOCK
    out = lax.map(
        lambda a: _peer_block(a[0], a[1], a[2], down, up),
        (hf.reshape(nb, PEER_TOKEN_BLOCK, D),
         idx.reshape(nb, PEER_TOKEN_BLOCK, PEER_HEADS, PEER_TOPK),
         g.reshape(nb, PEER_TOKEN_BLOCK, PEER_HEADS, PEER_TOPK)))
    return out.reshape(B, S, D)

def setup_inputs(seed: int = 0) -> dict:
    key = jax.random.key(seed)
    ks = jax.random.split(key, 26)
    f32 = jnp.float32
    D, L = D_MODEL, DEPTH

    def nrm(k, shape, scale):
        return jax.random.normal(k, shape, f32) * scale

    return {
        'x': nrm(ks[0], (BATCH, SEQ, D), 1.0),
        'c': nrm(ks[1], (BATCH, D), 1.0),
        'positions': jax.random.randint(ks[2], (BATCH, 1), 0, 4096, jnp.int32) + jnp.arange(SEQ, dtype=jnp.int32)[None, :],
        'norm_mix_gain': 1.0 + nrm(ks[3], (L, D), 0.05),
        'norm_ffn_gain': 1.0 + nrm(ks[4], (L, D), 0.05),
        'w_ada': nrm(ks[5], (L, D, N_MOD * D), D ** -0.5),
        'b_ada': nrm(ks[6], (L, N_MOD * D), 0.02),
        'w_in': nrm(ks[7], (L, D, IN_WIDTH), D ** -0.5),
        'w_gate': nrm(ks[8], (L, D, N_BRANCHES * D), D ** -0.5),
        'b_gate': nrm(ks[9], (L, N_BRANCHES * D), 0.02),
        'pool_w': nrm(ks[10], (L, N_POOL_GROUPS, POOL_GROUP_DIM, POOL_GROUP_DIM), POOL_GROUP_DIM ** -0.5),
        'pool_scale': 1.0 + nrm(ks[11], (L, POOL_WIDTH), 0.1),
        'lambda_q1': nrm(ks[12], (L, ATTN_HEAD_DIM), 0.1),
        'lambda_k1': nrm(ks[13], (L, ATTN_HEAD_DIM), 0.1),
        'lambda_q2': nrm(ks[14], (L, ATTN_HEAD_DIM), 0.1),
        'lambda_k2': nrm(ks[15], (L, ATTN_HEAD_DIM), 0.1),
        'attn_subln_gain': 1.0 + nrm(ks[16], (L, ATTN_WIDTH), 0.05),
        'w_branch_pool': nrm(ks[17], (L, POOL_WIDTH, D), POOL_WIDTH ** -0.5),
        'w_branch_attn': nrm(ks[18], (L, ATTN_WIDTH, D), ATTN_WIDTH ** -0.5),
        'w_out': nrm(ks[19], (L, D, D), D ** -0.5),
        'peer_w_query': nrm(ks[20], (L, D, PEER_HEADS * PEER_QUERY_DIM), D ** -0.5),
        'peer_sub_keys': nrm(ks[21], (L, 2, N_KEYS, PEER_HALF), PEER_HALF ** -0.5),
        'peer_down': nrm(ks[22], (L, N_EXPERTS, D), D ** -0.5),
        'peer_up': nrm(ks[23], (L, N_EXPERTS, D), 0.3),
        'final_norm_gain': 1.0 + nrm(ks[24], (D,), 0.05),
    }

def reference(x, c, positions, norm_mix_gain, norm_ffn_gain, w_ada, b_ada, w_in, w_gate, b_gate,
              pool_w, pool_scale, lambda_q1, lambda_k1, lambda_q2, lambda_k2, attn_subln_gain,
              w_branch_pool, w_branch_attn, w_out, peer_w_query, peer_sub_keys, peer_down, peer_up,
              final_norm_gain):
    B, S, D = x.shape
    inv_freq = ROPE_THETA ** (-jnp.arange(0, ROT_DIM, 2, dtype=jnp.float32) / ROT_DIM)
    ang = positions.astype(jnp.float32)[..., None] * inv_freq
    cos, sin = jnp.cos(ang), jnp.sin(ang)
    c_act = jax.nn.silu(c)

    for l in range(DEPTH):
        mod = (c_act @ w_ada[l] + b_ada[l]).reshape(B, N_MOD, D)
        shift_m, scale_m, gate_m, shift_f, scale_f, gate_f = [mod[:, i, None, :] for i in range(N_MOD)]

        h = rms_norm(x, norm_mix_gain[l]) * (1.0 + scale_m) + shift_m
        proj = h @ w_in[l]
        q, k, v, xp = jnp.split(proj, [QK_WIDTH, 2 * QK_WIDTH, 2 * QK_WIDTH + ATTN_WIDTH], axis=-1)

        pooled = causal_multiscale_pool(xp.reshape(B, S, N_POOL_GROUPS, POOL_GROUP_DIM))
        ya = jnp.einsum('bsgc,gcd->bsgd', pooled, pool_w[l]).reshape(B, S, POOL_WIDTH) * pool_scale[l]
        y_pool = ya @ w_branch_pool[l]

        lam_init = 0.8 - 0.6 * float(np.exp(-0.3 * l))
        lam = (jnp.exp(jnp.sum(lambda_q1[l] * lambda_k1[l]).astype(jnp.float32))
               - jnp.exp(jnp.sum(lambda_q2[l] * lambda_k2[l]).astype(jnp.float32)) + lam_init)
        qh = rope_partial(q.reshape(B, S, N_ATTN_HEADS, 2, ATTN_HEAD_DIM), cos, sin)
        kh = rope_partial(k.reshape(B, S, N_ATTN_HEADS, 2, ATTN_HEAD_DIM), cos, sin)
        vh = v.reshape(B, S, N_ATTN_HEADS, ATTN_V_DIM)
        o = diff_attention(qh, kh, vh, lam)
        o = rms_norm(o, attn_subln_gain[l].reshape(N_ATTN_HEADS, ATTN_V_DIM)) * (1.0 - lam_init)
        y_attn = o.reshape(B, S, ATTN_WIDTH) @ w_branch_attn[l]

        gates = jax.nn.sigmoid(h @ w_gate[l] + b_gate[l]).reshape(B, S, N_BRANCHES, D)
        merged = gates[:, :, 0] * y_pool + gates[:, :, 1] * y_attn
        x = x + gate_m * (merged @ w_out[l])

        h2 = rms_norm(x, norm_ffn_gain[l]) * (1.0 + scale_f) + shift_f
        x = x + gate_f * peer(h2, peer_w_query[l], peer_sub_keys[l], peer_down[l], peer_up[l])

    return rms_norm(x, final_norm_gain)


_drawn_inputs = setup_inputs


def setup_inputs(seed=0):
    import zlib

    import numpy as np

    out = dict(_drawn_inputs(seed))
    spreads = {}
    factors = {'b_gate': 8.0,
     'lambda_q1': 3.389,
     'lambda_q2': 8.0,
     'lambda_k2': 3.013,
     'attn_subln_gain': 3.405,
     'norm_ffn_gain': 3.048}
    for name, (base, spread) in spreads.items():
        noise = np.random.default_rng([zlib.crc32(name.encode()), seed]).standard_normal(out[name].shape)
        drawn = base * np.exp(spread * noise) if base else spread * noise
        out[name] = __import__('jax').numpy.asarray(drawn.astype(out[name].dtype))
    for name, factor in factors.items():
        out[name] = (out[name] * factor).astype(out[name].dtype)
    return out
```

```python
import concourse.bass as bass
from concourse import mybir
from contextlib import ExitStack
import numpy as np

P = 128
D = 1024
S = 512
KT = D // P
TB = S // P
CH = 256
HEADS = 8
HD = 64
ROT = 16
WINDOWS = (2, 4, 8, 16)
PADW = 16
NKEYS = 128
PH = 8
TOPK = 16
EPS = 1e-6
LAM_INIT = 0.8 - 0.6 * float(np.exp(-0.3 * 0))
NEG = -3.0e38
MASKED = -1.0e30
MAGIC = 12582912.0
TWO_PI = (6.28125, 0.0019350051879882812, 3.0199157663446332e-07)
PI_BELOW = 3.1415925

C_ID, C_ROT, C_MASK, C_FREQ, C_INV, C_IOTA = 0, 128, 256, 384, 385, 401
C_W = 417
K_C, K_BADA, K_BGATE, K_PSCALE, K_GMIX, K_GFFN, K_SUBLN = 0, 8, 56, 72, 80, 88, 96
K_W = 104

STAGES = (("xp", 4), ("gateA", 4), ("pool", 1), ("branchP", 4), ("gateB", 4), ("q", 4), ("k", 4),
          ("v", 4), ("branchA", 4), ("out", 4), ("query", 8))


def chunk_plan():
    return [(s, c) for s, n in STAGES for c in range(n)]


CHUNKS = chunk_plan()
FIRST = {s: CHUNKS.index((s, 0)) for s, _ in STAGES}


def stream_plan():
    order = [("ada", j, r) for j in range(2) for r in range(4)]
    late = [("ada", j, r) for j in range(2, 6) for r in range(4)]
    for n in range(len(CHUNKS)):
        order.append(("w", n))
        if n >= FIRST["pool"] - 3 and late:
            order.append(late.pop(0))
    return order


STREAM = stream_plan()
AT = {item: n for n, item in enumerate(STREAM)}
RAW_SLOTS = 3


def tile_plan():
    tiles = []
    for s, c in CHUNKS:
        if s == "pool":
            tiles += [(s, n, "dve") for n in range(8)]
        elif s == "v":
            tiles += [(s, c * TB + tb, "act") for tb in range(TB)]
        else:
            who = "dve" if s in ("branchP", "branchA", "out") else "act"
            tiles += [(s, 2 * c + n, who) for n in range(2)]
    tiles += [("score", n, "act") for n in range(16)]
    tiles += [("h2tok", n, "dve") for n in range(8)]
    tiles += [("x1tok", n, "act") for n in range(8)]
    tiles += [("gaterow", n, "dve") for n in range(2)]
    return tiles


TILES = tile_plan()
TILE_AT = {(k, i): n for n, (k, i, _) in enumerate(TILES)}


def emptied(kind, index):
    n = TILE_AT[kind, index]
    who = TILES[n][2]
    return who, sum(1 for t in TILES[:n + 1] if t[2] == who)


def layer(nc, consts, chans, rows, xT_d, pos_d, subk_d, ada_d, wdram, down, up, out):
    f32, f32r = mybir.dt.float32, mybir.dt.float32r
    i32, u32 = mybir.dt.int32, mybir.dt.uint32
    ALU, ACT, AX = mybir.AluOpType, mybir.ActivationFunctionType, mybir.AxisListType

    with ExitStack() as ctx:
        def sem(name):
            return ctx.enter_context(nc.semaphore(name))

        region = ctx.enter_context(nc.sbuf_tensor("region_base", [P, 1], f32))
        base = 64
        taken = [0]

        def place(name, shape, dt, kb):
            lead = int(kb * 1024) - base
            with ExitStack() as tmp:
                if lead > 0:
                    tmp.enter_context(nc.sbuf_tensor(name + "_lead", [P, lead // 4], f32))
                t = tmp.enter_context(nc.sbuf_tensor(name, shape, dt))
            return t

        low = [0.25]

        def small(name, shape, dt=f32):
            words = int(np.prod(shape[1:]))
            t = place(name, shape, dt, low[0])
            low[0] += ((words * 4 + 63) // 64) * 64 / 1024
            assert low[0] <= 12, low[0]
            return t

        cst = small("cst", [P, C_W])
        chan = small("chan", [P, K_W])
        ones = small("ones", [P, P])
        subk = small("subk", [P, 2, NKEYS])
        rope_cos = small("rope_cos", [P, S])
        rope_sin = small("rope_sin", [P, S])
        cact = small("cact", [P, KT])
        modc = small("modc", [P, 48])
        scaleA = small("scaleA", [P, KT])
        scaleF = small("scaleF", [P, KT])
        eps_t = small("eps_t", [P, 1])
        neglam = small("neglam", [P, 1])
        lamt = small("lamt", [P, 4])
        att_max = small("att_max", [P, 2, 2])
        att_bias = small("att_bias", [P, 2, 2])
        att_sum = small("att_sum", [P, 2, 2])
        att_rec = small("att_rec", [P, 2, 2])
        att_neg = small("att_neg", [P, 2])
        ident = cst[:, C_ID:C_ID + P]
        rotm = cst[:, C_ROT:C_ROT + P]
        mask = cst[:, C_MASK:C_MASK + P]

        raw = place("raw", [P, RAW_SLOTS, KT * CH], f32, 12)
        whi = place("whi", [P, 2, KT, CH], f32r, 36)
        wlo = place("wlo", [P, 2, KT, CH], f32r, 52)
        hT_hi = place("hT_hi", [P, KT, S], f32r, 68)
        hT_lo = place("hT_lo", [P, KT, S], f32r, 84)
        xT = place("xT", [P, KT, S], f32, 100)
        r1_hi = place("r1_hi", [P, KT, S], f32r, 100)
        r1_lo = place("r1_lo", [P, KT, S], f32r, 116)
        qT = place("qT", [P, HEADS, S], f32, 100)
        kT = place("kT", [P, HEADS, S], f32, 116)
        sq1 = place("sq1", [P, KT, S], f32, 132)
        rope_w = place("rope_w", [P, 4, S], f32, 148)
        pos_i = place("pos_i", [P, S], i32, 156)
        lam_w = place("lam_w", [P, 4, HD], f32, 158)
        lam_p = place("lam_p", [P, HD], f32, 159)
        pool_w = place("pool_w", [P, 2, PADW + S], f32, 132)
        pool_y = place("pool_y", [P, 2, S], f32, 137)
        pool_e = place("pool_e", [P, 16], f32, 141)
        ya_hi = place("ya_hi", [P, KT, S], f32r, 132)
        ya_lo = place("ya_lo", [P, KT, S], f32r, 148)
        v_t = place("v_t", [P, TB, D], f32, 132)
        sigB = place("sigB", [P, KT, S], f32, 148)
        tmp1 = place("tmp1", [P, KT, S], f32, 164)
        xpT = place("xpT", [P, KT, PADW + S], f32, 164)
        q_raw = place("q_raw", [P, 2, S], f32, 164)
        q_tmp = place("q_tmp", [P, 2, S], f32, 168)
        oT = place("oT", [P, HEADS, S], f32, 164)
        xR = place("xR", [P, KT, S], f32, 164)
        sq2 = place("sq2", [P, KT, S], f32, 164)
        mergedP = place("mergedP", [P, KT, S], f32, 181)
        acc_ada = place("acc_ada", [P, 2, D], f32, 197)
        rms1 = place("rms1", [P, S], f32, 205)
        prob = place("prob", [P, 2, 2, S], f32, 68)
        comb = place("comb", [P, 2, S], f32, 76)
        combT = place("combT", [P, 2, S], f32, 80)
        sqo = place("sqo", [P, HEADS, S], f32, 84)
        tmpo = place("tmpo", [P, KT, S], f32, 132)
        x1T = place("x1T", [P, KT, S], f32, 132)
        h2T = place("h2T", [P, KT, S], f32, 148)
        q2T = place("q2T", [P, 2 * PH, S], f32, 68)
        NS = TB * PH + 1
        s_all = place("s_all", [P, NS, 2 * NKEYS], f32, 12)
        gate_row = place("gate_row", [P, D], f32, 45)
        gain_row = place("gain_row", [P, D], f32, 49)
        h2cur = place("h2cur", [P, D], f32, 53)
        accum = place("accum", [P, D], f32, 57)
        yrow = place("yrow", [P, D], f32, 61)
        d_ring = place("d_ring", [P, 8, D], f32, 68)
        x1tok = place("x1tok", [P, TB, D], f32, 100)
        h2tok = place("h2tok", [P, TB, D], f32, 116)
        u_ring = place("u_ring", [P, 8, D], f32, 164)
        at = [132.0]

        def scratch(name, shape, dt=f32):
            t = place(name, shape, dt, at[0])
            at[0] += ((int(np.prod(shape[1:])) * 4 + 63) // 64) * 64 / 1024
            assert at[0] <= 164
            return t

        bias_row = scratch("bias_row", [P, D])
        junk = scratch("junk", [P, D])
        s_cur = scratch("s_cur", [P, 2, 2, NKEYS])
        s_left = scratch("s_left", [P, 2, NKEYS])
        top_v = scratch("top_v", [P, 2, TOPK])
        top_i = scratch("top_i", [P, 2, TOPK], u32)
        top_f = scratch("top_f", [P, 2, TOPK])
        cand = scratch("cand", [P, TOPK, TOPK])
        cand_left = scratch("cand_left", [P, TOPK * TOPK])
        best = scratch("best", [P, TOPK])
        best_at = scratch("best_at", [P, TOPK], u32)
        best_ab = scratch("best_ab", [P, 2, TOPK], u32)
        best_f = scratch("best_f", [P, 2, TOPK])
        onehot = scratch("onehot", [P, 2, TOPK, TOPK])
        picked = scratch("picked", [P, 2, TOPK])
        idx = scratch("idx", [P, 2, TOPK], i32)
        logit = scratch("logit", [P, 2, TOPK])
        expo = scratch("expo", [P, 2, TOPK])
        expsum = scratch("expsum", [P, 2])
        exprec = scratch("exprec", [P, 1])
        share = scratch("share", [P, TOPK])
        pre = scratch("pre", [P, 2, TOPK])
        gel = scratch("gel", [P, 2, TOPK])
        wexp = scratch("wexp", [P, TOPK])
        fin_ss = scratch("fin_ss", [P, 3])

        bank = ctx.enter_context(nc.psum_tensor("bank", [P, 8, S], f32))

        const_in = sem("const_in")
        pos_in = sem("pos_in")
        xT_in = sem("xT_in")
        xR_in = sem("xR_in")
        row_in = sem("row_in")
        raw_in = [sem(f"raw_in{n}") for n in range(RAW_SLOTS)]
        raw_free = sem("raw_free")
        hi_ready = sem("hi_ready")
        lo_ready = sem("lo_ready")
        tile_ready = sem("tile_ready")
        act_emptied = sem("act_emptied")
        dve_emptied = sem("dve_emptied")
        cact_ready = sem("cact_ready")
        ones_ready = sem("ones_ready")
        ada_acc = sem("ada_acc")
        ada_col = sem("ada_col")
        ada_done = sem("ada_done")
        sq_ready = sem("sq_ready")
        mean_ready = sem("mean_ready")
        root_ready = sem("root_ready")
        root_used = sem("root_used")
        part_ready = sem("part_ready")
        ahi_ready = sem("ahi_ready")
        alo_ready = sem("alo_ready")
        sin_arg = sem("sin_arg")
        sin_done = sem("sin_done")
        lam_arg = sem("lam_arg")
        lam_exp = sem("lam_exp")
        rot_ready = sem("rot_ready")
        rot_used = sem("rot_used")
        sc_ready = sem("sc_ready")
        max_ready = sem("max_ready")
        prob_ready = sem("prob_ready")
        comb_ready = sem("comb_ready")
        tr_ready = sem("tr_ready")
        trs_ready = sem("trs_ready")
        pv_ready = sem("pv_ready")
        o_ready = sem("o_ready")
        x1_ready = sem("x1_ready")
        h2_ready = sem("h2_ready")
        pads = sem("pads")
        s_ready = sem("s_ready")
        route_done = sem("route_done")
        exp_done = sem("exp_done")
        h2c_ready = sem("h2c_ready")
        dot_groups = sem("dot_groups")
        sum_groups = sem("sum_groups")
        gel_done = sem("gel_done")
        pool_step = sem("pool_step")
        dve_step = sem("dve_step")
        d_in = [sem(f"d_in{n}") for n in range(8)]
        u_in = [sem(f"u_in{n}") for n in range(8)]
        y_ready = sem("y_ready")
        ss_ready = sem("ss_ready")
        out_ready = sem("out_ready")
        out_stored = sem("out_stored")
        y_free = sem("y_free")

        block = ctx.enter_context(nc.Block())

        def wait_emptied(eng, kind, index):
            who, n = emptied(kind, index)
            eng.wait_ge(act_emptied if who == "act" else dve_emptied, n)

        def raw_arrived(eng, n):
            eng.wait_ge(raw_in[n % RAW_SLOTS], 16 * (n // RAW_SLOTS + 1))

        def raw_w(n):
            return raw[:, AT["w", n] % RAW_SLOTS, :].rearrange("p (k n) -> p k n", k=KT)

        N_OP = dict(norm1=0, pooled=8, ya=16, o=24, merged=32, norm2=40)
        N_MEAN = dict(norm1=0, o=1, norm2=1 + HEADS)
        UNITS = [(h, qb) for h in range(HEADS) for qb in range(TB)]

        @block.sync
        def _(sp):
            sp.dma_start(cst[:, :], consts).then_inc(const_in, 16)
            sp.dma_start(chan[:, :], chans).then_inc(const_in, 16)
            sp.dma_start(xT[:, :, :], xT_d).then_inc(xT_in, 16)
            for n, item in enumerate(STREAM):
                if n >= RAW_SLOTS:
                    sp.wait_ge(raw_free, n - RAW_SLOTS + 1)
                if item[0] == "ada":
                    src = ada_d[item[1], item[2]]
                else:
                    src = wdram[CHUNKS[item[1]][0]][CHUNKS[item[1]][1]]
                sp.dma_start(raw[:, n % RAW_SLOTS, :], src).then_inc(raw_in[n % RAW_SLOTS], 16)
                if n == 2:
                    sp.dma_start(pos_i[:, :], pos_d).then_inc(pos_in, 16)
                    sp.dma_start(subk[:, :, :], subk_d).then_inc(pos_in, 16)
                    sp.dma_start(lam_w[:, :, :], rows[:, 2 * D:2 * D + 4 * HD]).then_inc(pos_in, 16)
                if item == ("w", FIRST["branchA"] + 1):
                    sp.wait_ge(part_ready, 24)
                    sp.dma_start(xR[:, :, :], xT_d).then_inc(xR_in, 16)
            sp.wait_ge(tile_ready, TILE_AT["gaterow", 1] + 1)
            sp.dma_start(gain_row[:, :], rows[:, 0:D]).then_inc(row_in, 16)
            sp.dma_start(bias_row[:, :], rows[:, D:2 * D]).then_inc(row_in, 16)
            sp.sem_inc(y_free, 1)
            with sp.Fori(0, TB) as tb:
                sp.wait_ge(out_ready, tb + 1)
                sp.dma_start(out[bass.ds(tb, 1), :, :].rearrange("a p d -> (a p) d"), yrow[:, :])\
                  .then_inc(out_stored, 16)
                sp.wait_ge(out_stored, 16 * tb + 16)
                sp.sem_inc(y_free, 1)
            sp.wait_ge(out_stored, 16 * TB)

        @block.tensor
        def _(pe):
            def mm3(dst, lhi, llo, rhi, rlo, first, last):
                pe.matmul(dst, lhi, rhi, start=first, stop=False)
                pe.matmul(dst, lhi, rlo, start=False, stop=False)
                return pe.matmul(dst, llo, rhi, start=False, stop=last)

            def free_bank(t):
                if t >= 4:
                    wait_emptied(pe, *TILES[t - 4][:2])

            def mean(rhs):
                for k in range(len(rhs)):
                    last = pe.matmul(bank[:, 6, :], ones[:, :], rhs[k], start=(k == 0),
                                     stop=(k == len(rhs) - 1))
                last.then_inc(mean_ready, 1)

            def ada_columns(j):
                pe.wait_ge(ada_acc, j + 1)
                if j:
                    pe.wait_ge(ada_done, j)
                for m in range(KT):
                    last = pe.matmul(bank[:, 7, m:m + 1], acc_ada[:, j % 2, m * P:(m + 1) * P],
                                     ones[:, 0:1], start=True, stop=True)
                last.then_inc(ada_col, 1)

            def rotate(n):
                pe.wait_ge(act_emptied, emptied("q", 0)[1] + n)
                if n >= 2:
                    pe.wait_ge(rot_used, n - 1)
                pe.matmul(bank[:, 4 + n % 2, :], rotm, q_raw[:, n % 2, :], start=True, stop=True)\
                  .then_inc(rot_ready, 1)

            pe.wait_ge(const_in, 32)
            pe.wait_ge(ones_ready, 1)
            pe.wait_ge(sq_ready, 8)
            mean([sq1[:, k, :] for k in range(KT)])
            ada_columns(0)
            ada_columns(1)

            ada_before = {}
            for item, n in AT.items():
                if item[0] == "ada" and item[1] >= 2 and item[2] == 3:
                    ada_before[STREAM[n - 1][1]] = item[1]

            def attention():
                def scores(u):
                    h, qb = UNITS[u]
                    par, n = u % 2, (qb + 1) * P
                    if u >= 2:
                        pe.wait_ge(prob_ready, 2 * (u - 1))
                    else:
                        wait_emptied(pe, "v", 4 * TB - 1)
                    for c in range(2):
                        last = pe.matmul(bank[:, 2 * par + c, 0:n],
                                         qT[c * HD:(c + 1) * HD, h, qb * P:(qb + 1) * P],
                                         kT[c * HD:(c + 1) * HD, h, 0:n], start=True, stop=True)
                    last.then_inc(sc_ready, 1)

                def values(u):
                    h, qb = UNITS[u]
                    pe.wait_ge(trs_ready, u + 1)
                    if qb == 0 and h >= 2:
                        pe.wait_ge(o_ready, h - 1)
                    for kb in range(qb + 1):
                        last = pe.matmul(bank[:, 6 + h % 2, qb * P:(qb + 1) * P],
                                         v_t[:, kb, h * P:(h + 1) * P],
                                         combT[:, u % 2, kb * P:(kb + 1) * P],
                                         start=(kb == 0), stop=(kb == qb))
                    last.then_inc(pv_ready, 1)

                pe.wait_ge(rot_used, 2 * HEADS)
                scores(0)
                for u, (h, qb) in enumerate(UNITS):
                    if u + 1 < len(UNITS):
                        scores(u + 1)
                    if u >= 1:
                        values(u - 1)
                    pe.wait_ge(comb_ready, u + 1)
                    if u >= 2:
                        pe.wait_ge(trs_ready, u - 1)
                    for kb in range(qb + 1):
                        last = pe.transpose(bank[:, 4 + u % 2, kb * P:(kb + 1) * P],
                                            comb[:, u % 2, kb * P:(kb + 1) * P], ident)
                    last.then_inc(tr_ready, 1)
                values(len(UNITS) - 1)
                for h in range(HEADS):
                    pe.wait_ge(sq_ready, 8 + h + 1)
                    pe.wait_ge(root_ready, N_MEAN["o"] + h)
                    mean([sqo[:, h, :]])

            def norm2_mean():
                pe.wait_ge(sq_ready, 24)
                pe.wait_ge(root_ready, N_MEAN["norm2"])
                mean([sq2[:, k, :] for k in range(KT)])

            t = 0
            for n, (stage, c) in enumerate(CHUNKS):
                if n in ada_before:
                    ada_columns(ada_before[n])
                if stage == "branchA" and c == 0:
                    attention()
                if stage == "query" and c == 0:
                    norm2_mean()
                if c == 0:
                    ready = {"xp": "norm1", "pool": "pooled", "branchP": "ya", "branchA": "o",
                             "out": "merged", "query": "norm2"}.get(stage)
                    if ready:
                        pe.wait_ge(alo_ready, N_OP[ready] + 8)
                pe.wait_ge(hi_ready, n + 1)
                pe.wait_ge(lo_ready, n + 1)
                wh, wl = whi[:, n % 2], wlo[:, n % 2]
                ah, al = {"pool": (r1_hi, r1_lo), "branchP": (ya_hi, ya_lo), "branchA": (r1_hi, r1_lo),
                          "query": (r1_hi, r1_lo)}.get(stage, (hT_hi, hT_lo))
                if stage == "pool":
                    for g in range(4):
                        for m in range(2):
                            free_bank(t)
                            for k in range(2):
                                kk = 2 * g + k
                                last = mm3(bank[:, t % 4, :], wh[:, kk, m * P:(m + 1) * P],
                                           wl[:, kk, m * P:(m + 1) * P], ah[:, kk, :], al[:, kk, :],
                                           k == 0, k == 1)
                            last.then_inc(tile_ready, 1)
                            t += 1
                elif stage == "v":
                    for tb in range(TB):
                        free_bank(t)
                        for k in range(KT):
                            last = mm3(bank[:, t % 4, 0:CH], ah[:, k, tb * P:(tb + 1) * P],
                                       al[:, k, tb * P:(tb + 1) * P], wh[:, k, :], wl[:, k, :],
                                       k == 0, k == KT - 1)
                        last.then_inc(tile_ready, 1)
                        t += 1
                else:
                    for m in range(2):
                        free_bank(t)
                        for k in range(KT):
                            last = mm3(bank[:, t % 4, :], wh[:, k, m * P:(m + 1) * P],
                                       wl[:, k, m * P:(m + 1) * P], ah[:, k, :], al[:, k, :],
                                       k == 0, k == KT - 1)
                        last.then_inc(tile_ready, 1)
                        t += 1
                if stage in ("q", "k") or (stage == "v" and c == 0):
                    done = 2 * (n - FIRST["q"])
                    for r in range(max(0, done - 2), done):
                        rotate(r)
            for n in range(16):
                tb, g = n // 4, n % 4
                free_bank(t)
                if n == 0:
                    pe.wait_ge(pos_in, 48)
                    wait_emptied(pe, "query", 15)
                for j in range(4):
                    hp = 4 * g + j
                    last = pe.matmul(bank[:, t % 4, j * P:(j + 1) * P], q2T[:, hp, tb * P:(tb + 1) * P],
                                     subk[:, hp % 2, :], start=True, stop=True)
                last.then_inc(tile_ready, 1)
                t += 1
            for src in (h2T, x1T):
                if src is h2T:
                    pe.wait_ge(h2_ready, 8)
                for n in range(8):
                    tb, half = n // 2, n % 2
                    free_bank(t)
                    for j in range(4):
                        last = pe.transpose(bank[:, t % 4, j * P:(j + 1) * P],
                                            src[:, 4 * half + j, tb * P:(tb + 1) * P], ident)
                    last.then_inc(tile_ready, 1)
                    t += 1
            for n in range(2):
                free_bank(t)
                pe.matmul(bank[:, t % 4, :], ones[:, :], acc_ada[:, 1, n * S:(n + 1) * S],
                          start=True, stop=True).then_inc(tile_ready, 1)
                t += 1

        def w_done(eng, n):
            stage, c = CHUNKS[n]
            last = {"pool": 7, "v": c * TB + TB - 1}.get(stage, 2 * c + 1)
            eng.wait_ge(tile_ready, TILE_AT[stage, last] + 1)

        @block.scalar
        def _(act):
            def whi_make(n):
                if n >= len(CHUNKS):
                    return
                raw_arrived(act, AT["w", n])
                if n >= 2:
                    w_done(act, n - 2)
                act.activation(whi[:, n % 2], raw_w(n), ACT.Copy).then_inc(hi_ready, 1)

            def tile(kind, i):
                t = TILE_AT[kind, i]
                act.wait_ge(tile_ready, t + 1)
                return bank[:, t % 4, :]

            def root(n, scale):
                act.wait_ge(mean_ready, n + 1)
                if n:
                    act.wait_ge(root_used, n)
                act.activation(rms1[:, :], bank[:, 6, :], ACT.Sqrt, bias=eps_t[:, :], scale=scale)\
                   .then_inc(root_ready, 1)

            act.wait_ge(const_in, 32)
            act.activation(cact[:, :], chan[:, K_C:K_C + KT], ACT.Silu).then_inc(cact_ready, 1)
            act.wait_ge(xT_in, 16)
            for k in range(KT):
                act.activation(sq1[:, k, :], xT[:, k, :], ACT.Square).then_inc(sq_ready, 1)
            act.wait_ge(ones_ready, 1)
            root(0, 1.0 / D)
            whi_make(0)
            for k in range(KT):
                act.wait_ge(part_ready, k + 1)
                act.activation(hT_hi[:, k, :], tmp1[:, k, :], ACT.Identity, bias=modc[:, k:k + 1])\
                   .then_inc(ahi_ready, 1)
            for n in range(2):
                act.wait_ge(sin_arg, n + 1)
                act.activation((rope_sin, rope_cos)[n][:, :], rope_w[:, 2 + n, :], ACT.Sin)\
                   .then_inc(sin_done, 1)
            act.wait_ge(lam_arg, 1)
            act.activation(lamt[:, 2:4], lamt[:, 0:2], ACT.Exp).then_inc(lam_exp, 1)

            def attention():
                def exps(u):
                    h, qb = UNITS[u]
                    par, n = u % 2, (qb + 1) * P
                    act.wait_ge(max_ready, u + 1)
                    if u >= 2:
                        act.wait_ge(comb_ready, u - 1)
                    for c in range(2):
                        act.activation(prob[:, par, c, 0:n], bank[:, 2 * par + c, 0:n], ACT.Exp,
                                       bias=att_bias[:, par, c:c + 1], scale=HD ** -0.5,
                                       accum_out=att_sum[:, par, c:c + 1]).then_inc(prob_ready, 1)

                exps(0)
                for u, (h, qb) in enumerate(UNITS):
                    if u + 1 < len(UNITS):
                        exps(u + 1)
                    act.wait_ge(tr_ready, u + 1)
                    if u >= 2:
                        act.wait_ge(pv_ready, u - 1)
                    act.activation(combT[:, u % 2, 0:(qb + 1) * P], bank[:, 4 + u % 2, 0:(qb + 1) * P],
                                   ACT.Copy).then_inc(trs_ready, 1)
                    if qb == 0 and h:
                        act.wait_ge(pv_ready, u)
                        act.activation(oT[:, h - 1, :], bank[:, 6 + (h - 1) % 2, :], ACT.Copy)\
                           .then_inc(o_ready, 1)
                act.wait_ge(pv_ready, len(UNITS))
                act.activation(oT[:, HEADS - 1, :], bank[:, 6 + (HEADS - 1) % 2, :], ACT.Copy)\
                   .then_inc(o_ready, 1)
                act.drain()
                for h in range(HEADS):
                    act.activation(sqo[:, h, :], oT[:, h, :], ACT.Square).then_inc(sq_ready, 1)
                for h in range(HEADS):
                    root(N_MEAN["o"] + h, 1.0 / P)
                    if h:
                        split_o(h - 1)
                split_o(HEADS - 1)

            def split_o(h):
                act.wait_ge(part_ready, 16 + h + 1)
                act.activation(r1_hi[:, h, :], tmpo[:, h, :], ACT.Copy).then_inc(ahi_ready, 1)

            for n, (stage, c) in enumerate(CHUNKS):
                whi_make(n + 1)
                if stage == "branchA" and c == 0:
                    attention()
                if stage == "xp":
                    if c == 0:
                        act.wait_ge(pads, 1)
                    for m in range(2):
                        act.activation(xpT[:, 2 * c + m, PADW:], tile(stage, 2 * c + m), ACT.Copy)\
                           .then_inc(act_emptied, 1)
                elif stage in ("gateA", "gateB"):
                    dst, col = (mergedP, 0) if stage == "gateA" else (sigB, KT)
                    for m in range(2):
                        i = 2 * c + m
                        act.activation(dst[:, i, :], tile(stage, i), ACT.Sigmoid,
                                       bias=chan[:, K_BGATE + col + i:K_BGATE + col + i + 1])\
                           .then_inc(act_emptied, 1)
                        if stage == "gateA":
                            act.wait_ge(part_ready, 8 + i + 1)
                            act.activation(r1_hi[:, i, :], pool_y[:, i % 2, :], ACT.Copy)\
                               .then_inc(ahi_ready, 1)
                elif stage == "pool":
                    for i in range(8):
                        src = tile(stage, i)
                        act.activation(ya_hi[:, i, :], src, ACT.Identity, bias=0.0,
                                       scale=chan[:, K_PSCALE + i:K_PSCALE + i + 1]).then_inc(ahi_ready, 1)
                elif stage in ("q", "k"):
                    for m in range(2):
                        i = 2 * c + m + (HEADS if stage == "k" else 0)
                        src = tile(stage, 2 * c + m)
                        if i >= 2:
                            act.wait_ge(rot_used, i - 1)
                        act.activation(q_raw[:, i % 2, :], src, ACT.Copy).then_inc(act_emptied, 1)
                elif stage == "v":
                    for tb in range(TB):
                        act.activation(v_t[:, tb, c * CH:(c + 1) * CH], tile(stage, c * TB + tb)[:, 0:CH],
                                       ACT.Copy).then_inc(act_emptied, 1)
                elif stage == "branchA":
                    for m in range(2):
                        i = 2 * c + m
                        act.wait_ge(part_ready, 24 + i + 1)
                        act.activation(hT_hi[:, i, :], tmpo[:, i, :], ACT.Copy).then_inc(ahi_ready, 1)
                elif stage == "out":
                    for m in range(2):
                        i = 2 * c + m
                        act.wait_ge(x1_ready, i + 1)
                        act.activation(sq2[:, i, :], x1T[:, i, :], ACT.Square).then_inc(sq_ready, 1)
                    if c == 3:
                        root(N_MEAN["norm2"], 1.0 / D)
                        for k in range(KT):
                            act.wait_ge(part_ready, 32 + k + 1)
                            act.activation(r1_hi[:, k, :], h2T[:, k, :], ACT.Identity,
                                           bias=modc[:, 24 + k:25 + k]).then_inc(ahi_ready, 1)
                elif stage == "query":
                    for m in range(2):
                        act.activation(q2T[:, 2 * c + m, :], tile(stage, 2 * c + m), ACT.Copy)\
                           .then_inc(act_emptied, 1)
            for n in range(16):
                tb, g = n // 4, n % 4
                act.activation(s_all[:, tb * PH + 2 * g:tb * PH + 2 * g + 2, :].rearrange("p a b -> p (a b)"),
                               tile("score", n), ACT.Copy).then_inc(act_emptied, 1)
            for n in range(8):
                act.activation(x1tok[:, n // 2, (n % 2) * S:(n % 2 + 1) * S], tile("x1tok", n), ACT.Copy)\
                   .then_inc(act_emptied, 1)
            act.drain()
            act.wait_ge(tile_ready, TILE_AT["gaterow", 1] + 1)
            act.activation(s_cur[:, 0].rearrange("p a b -> p (a b)"), s_all[:, 0, :], ACT.Copy)\
               .then_inc(s_ready, 1)
            wait_emptied(act, "gaterow", 1)
            with act.Fori(0, TB) as tb:
                act.activation(h2cur[:, :], h2tok[:, bass.ds(tb, 1), :].rearrange("p a d -> p (a d)"),
                               ACT.Copy).then_inc(h2c_ready, 1)
                with act.Fori(0, PH // 2) as hp:
                    for par in range(2):
                        i = tb * PH + hp * 2 + par
                        act.wait_ge(route_done, i + 1)
                        act.activation(expo[:, par], logit[:, par], ACT.Exp,
                                       accum_out=expsum[:, par:par + 1]).then_inc(exp_done, 1)
                        act.activation(s_cur[:, 1 - par].rearrange("p a b -> p (a b)"),
                                       s_all[:, bass.ds(i + 1, 1), :].rearrange("p a b -> p (a b)"),
                                       ACT.Copy).then_inc(s_ready, 1)
                        for g in range(4):
                            act.wait_ge(dot_groups, 4 * i + g + 3)
                            act.activation(gel[:, par, 4 * g:4 * g + 4], pre[:, par, 4 * g:4 * g + 4],
                                           ACT.Gelu).then_inc(gel_done, 1)
                act.wait_ge(y_ready, tb + 1)
                act.activation(junk[:, :], yrow[:, :], ACT.Square, accum_out=fin_ss[:, 0:1])
                act.drain()
                act.activation(fin_ss[:, 1:2], fin_ss[:, 0:1], ACT.Sqrt, bias=eps_t[:, :], scale=1.0 / D)\
                   .then_inc(ss_ready, 1)

        @block.vector
        def _(dve):
            def ada_chunk(j, r):
                n = AT["ada", j, r]
                raw_arrived(dve, n)
                if j >= 2 and r == 0:
                    dve.wait_ge(ada_col, j - 1)
                acc = acc_ada[:, j % 2, :]
                for k in range(2):
                    src = raw[:, n % RAW_SLOTS, k * D:(k + 1) * D]
                    col = cact[:, 2 * r + k:2 * r + k + 1]
                    if r == 0 and k == 0:
                        last = dve.tensor_scalar(acc, src, col, None, ALU.mult)
                    else:
                        last = dve.scalar_tensor_tensor(acc, src, col, acc, ALU.mult, ALU.add)
                    if k == 0:
                        dve.drain()
                last.then_inc(raw_free, 1)
                dve.drain()
                if r == 3:
                    dve.sem_inc(ada_acc, 1)

            def ada_finish(j):
                dve.wait_ge(ada_col, j + 1)
                dve.tensor_tensor(modc[:, j * KT:(j + 1) * KT], bank[:, 7, 0:KT],
                                  chan[:, K_BADA + j * KT:K_BADA + (j + 1) * KT], ALU.add)\
                   .then_inc(ada_done, 1)

            def wlo_make(n):
                if n >= len(CHUNKS):
                    return
                dve.wait_ge(hi_ready, n + 1)
                dve.tensor_tensor(wlo[:, n % 2], raw_w(n), whi[:, n % 2].bitcast(f32), ALU.subtract)\
                   .then_inc(lo_ready, 1)

            def follow(n):
                if n >= len(CHUNKS):
                    return
                wlo_make(n)
                dve.drain()
                dve.sem_inc(raw_free, 1)
                at_ = AT["w", n] + 1
                if at_ < len(STREAM) and STREAM[at_][0] == "ada":
                    _, j, r = STREAM[at_]
                    if r == 0 and j >= 3:
                        ada_finish(j - 1)
                    ada_chunk(j, r)
                    if j == 5 and r == 3:
                        ada_finish(5)

            def tile(kind, i):
                t = TILE_AT[kind, i]
                dve.wait_ge(tile_ready, t + 1)
                return bank[:, t % 4, :]

            def inverse_root(n):
                dve.wait_ge(root_ready, n + 1)
                dve.reciprocal(rms1[:, :], rms1[:, :])
                dve.drain()

            def lo_part(dst, src, hi, count, scalar=None, op=ALU.add):
                dve.wait_ge(ahi_ready, count)
                if scalar is None:
                    ins = dve.tensor_tensor(dst, src, hi.bitcast(f32), ALU.subtract)
                else:
                    ins = dve.scalar_tensor_tensor(dst, src, scalar, hi.bitcast(f32), op, ALU.subtract)
                return ins.then_inc(alo_ready, 1)

            dve.memset(ones[:, :], 1.0)
            dve.memset(eps_t[:, :], EPS)
            dve.drain()
            dve.sem_inc(ones_ready, 1)
            dve.wait_ge(cact_ready, 1)
            for j in range(2):
                for r in range(4):
                    ada_chunk(j, r)
            ada_finish(0)
            ada_finish(1)
            dve.drain()
            dve.scalar_tensor_tensor(scaleA[:, :], modc[:, KT:2 * KT], 1.0, chan[:, K_GMIX:K_GMIX + KT],
                                     ALU.add, ALU.mult)
            inverse_root(0)
            for k in range(KT):
                dve.scalar_tensor_tensor(tmp1[:, k, :], xT[:, k, :], scaleA[:, k:k + 1], rms1[:, :],
                                         ALU.mult, ALU.mult).then_inc(part_ready, 1)
            dve.sem_inc(root_used, 1)
            follow(0)
            for k in range(KT):
                lo_part(hT_lo[:, k, :], tmp1[:, k, :], hT_hi[:, k, :], k + 1, modc[:, k:k + 1])
            dve.drain()
            dve.memset(xpT[:, :, 0:PADW], 0.0)
            dve.memset(pool_w[:, :, 0:PADW], 0.0)
            dve.drain()
            dve.sem_inc(pads, 1)
            dve.wait_ge(pos_in, 48)
            ang, turns = rope_w[:, 0, :], rope_w[:, 1, :]
            dve.tensor_copy(turns, pos_i[:, :])
            dve.drain()
            dve.tensor_scalar(ang, turns, cst[:, C_FREQ:C_FREQ + 1], None, ALU.mult)
            dve.drain()
            for n, shift in ((0, 0.0), (1, 0.25)):
                arg = rope_w[:, 2 + n, :]
                dve.tensor_scalar(turns, ang, 1.0 / (2 * np.pi), shift, ALU.mult, ALU.add)
                dve.drain()
                dve.tensor_scalar(turns, turns, MAGIC, None, ALU.add)
                dve.drain()
                dve.tensor_scalar(turns, turns, -MAGIC, None, ALU.add)
                dve.drain()
                dve.scalar_tensor_tensor(arg, turns, -TWO_PI[0], ang, ALU.mult, ALU.add)
                for part in TWO_PI[1:]:
                    dve.drain()
                    dve.scalar_tensor_tensor(arg, turns, -part, arg, ALU.mult, ALU.add)
                dve.drain()
                if n:
                    dve.tensor_scalar(arg, arg, np.pi / 2, None, ALU.add)
                    dve.drain()
                dve.tensor_scalar(arg, arg, PI_BELOW, -PI_BELOW, ALU.min, ALU.max).then_inc(sin_arg, 1)
                dve.drain()
            for n in range(2):
                dve.tensor_tensor(lam_p[:, :], lam_w[:, 2 * n, :], lam_w[:, 2 * n + 1, :], ALU.mult)
                dve.drain()
                dve.tensor_reduce(lamt[:, n:n + 1], lam_p[:, :], AX.X, ALU.add)
                dve.drain()
            dve.sem_inc(lam_arg, 1)
            dve.wait_ge(lam_exp, 1)
            dve.tensor_tensor(neglam[:, :], lamt[:, 3:4], lamt[:, 2:3], ALU.subtract)
            dve.drain()
            dve.tensor_scalar(neglam[:, :], neglam[:, :], -LAM_INIT, None, ALU.add)

            def pooling(i):
                w = WINDOWS[i // 2]
                if i == 0:
                    wait_emptied(dve, "xp", 7)
                x = xpT[:, i, :]
                src, n = x, 1
                while n < w:
                    dst = pool_w[:, (n.bit_length() - 1) % 2, :]
                    dve.tensor_tensor(dst[:, PADW:], src[:, PADW:], src[:, PADW - n:PADW + S - n], ALU.add)
                    dve.drain()
                    src, n = dst, 2 * n
                y = pool_y[:, i % 2, :]
                if i >= 2:
                    dve.wait_ge(ahi_ready, 8 + i - 1)
                dve.scalar_tensor_tensor(y, src[:, PADW:], 1.0 / w, x[:, PADW:], ALU.mult, ALU.subtract)
                dve.tensor_tensor(pool_e[:, 0:w - 1], src[:, PADW:PADW + w - 1],
                                  cst[:, C_INV:C_INV + w - 1], ALU.mult)
                dve.drain()
                dve.tensor_tensor(y[:, 0:w - 1], pool_e[:, 0:w - 1], x[:, PADW:PADW + w - 1], ALU.subtract)\
                   .then_inc(part_ready, 1)
                dve.drain()
                lo_part(r1_lo[:, i, :], y, r1_hi[:, i, :], 8 + i + 1)

            def attention():
                def maxima(u):
                    h, qb = UNITS[u]
                    par, n = u % 2, (qb + 1) * P
                    dve.wait_ge(sc_ready, u + 1)
                    sc = bank[:, 2 * par:2 * par + 2, 0:n]
                    dve.tensor_tensor(sc[:, :, qb * P:n], sc[:, :, qb * P:n],
                                      mask.unsqueeze(1).broadcast_to([P, 2, P]), ALU.add)
                    dve.drain()
                    dve.tensor_reduce(att_max[:, par, :], sc, AX.X, ALU.max)
                    dve.drain()
                    dve.tensor_scalar(att_bias[:, par, :], att_max[:, par, :], -(HD ** -0.5), None, ALU.mult)\
                       .then_inc(max_ready, 1)

                maxima(0)
                for u, (h, qb) in enumerate(UNITS):
                    if u + 1 < len(UNITS):
                        maxima(u + 1)
                    par, n = u % 2, (qb + 1) * P
                    dve.wait_ge(prob_ready, 2 * (u + 1))
                    dve.reciprocal(att_rec[:, par, :], att_sum[:, par, :])
                    dve.drain()
                    dve.tensor_tensor(att_neg[:, par:par + 1], att_rec[:, par, 1:2], neglam[:, :], ALU.mult)
                    dve.drain()
                    if u >= 2:
                        dve.wait_ge(tr_ready, u - 1)
                    dve.tensor_scalar(comb[:, par, 0:n], prob[:, par, 1, 0:n], att_neg[:, par:par + 1],
                                      None, ALU.mult)
                    dve.drain()
                    dve.scalar_tensor_tensor(comb[:, par, 0:n], prob[:, par, 0, 0:n],
                                             att_rec[:, par, 0:1], comb[:, par, 0:n],
                                             ALU.mult, ALU.add).then_inc(comb_ready, 1)
                for h in range(HEADS):
                    inverse_root(N_MEAN["o"] + h)
                    dve.scalar_tensor_tensor(tmpo[:, h, :], oT[:, h, :],
                                             chan[:, K_SUBLN + h:K_SUBLN + h + 1], rms1[:, :],
                                             ALU.mult, ALU.mult)
                    dve.drain()
                    dve.sem_inc(root_used, 1)
                    dve.tensor_scalar(tmpo[:, h, :], tmpo[:, h, :], 1.0 - LAM_INIT, None, ALU.mult)\
                       .then_inc(part_ready, 1)
                    dve.drain()
                    lo_part(r1_lo[:, h, :], tmpo[:, h, :], r1_hi[:, h, :], 24 + h + 1)

            for n, (stage, c) in enumerate(CHUNKS):
                if n + 1 < len(CHUNKS):
                    follow(n + 1)
                if stage == "branchA" and c == 0:
                    attention()
                if stage == "gateA":
                    for m in range(2):
                        pooling(2 * c + m)
                elif stage == "pool":
                    for i in range(8):
                        src = tile(stage, i)
                        lo_part(ya_lo[:, i, :], src, ya_hi[:, i, :], 16 + i + 1,
                                chan[:, K_PSCALE + i:K_PSCALE + i + 1], ALU.mult)
                        dve.drain()
                        dve.sem_inc(dve_emptied, 1)
                elif stage == "branchP":
                    for m in range(2):
                        i = 2 * c + m
                        src = tile(stage, i)
                        wait_emptied(dve, "gateA", i)
                        dve.tensor_tensor(mergedP[:, i, :], src, mergedP[:, i, :], ALU.mult)\
                           .then_inc(dve_emptied, 1)
                elif stage in ("q", "k") or (stage == "v" and c == 0):
                    done = 2 * (n - FIRST["q"])
                    for r in range(max(0, done - 2), done):
                        dve.wait_ge(rot_ready, r + 1)
                        if r == 0:
                            dve.wait_ge(sin_done, 2)
                        dst = (qT if r < HEADS else kT)[:, r % HEADS, :]
                        dve.tensor_tensor(q_tmp[:, 0, :], q_raw[:, r % 2, :], rope_cos[:, :], ALU.mult)
                        dve.tensor_tensor(q_tmp[:, 1, :], bank[:, 4 + r % 2, :], rope_sin[:, :], ALU.mult)
                        dve.drain()
                        dve.tensor_tensor(dst, q_tmp[:, 0, :], q_tmp[:, 1, :], ALU.add)\
                           .then_inc(rot_used, 1)
                        dve.drain()
                elif stage == "branchA":
                    for m in range(2):
                        i = 2 * c + m
                        src = tile(stage, i)
                        dve.tensor_tensor(tmpo[:, i, :], src, sigB[:, i, :], ALU.mult)\
                           .then_inc(dve_emptied, 1)
                        dve.drain()
                        dve.tensor_tensor(tmpo[:, i, :], tmpo[:, i, :], mergedP[:, i, :], ALU.add)\
                           .then_inc(part_ready, 1)
                        dve.drain()
                        lo_part(hT_lo[:, i, :], tmpo[:, i, :], hT_hi[:, i, :], 32 + i + 1)
                elif stage == "out":
                    if c == 0:
                        dve.wait_ge(xR_in, 16)
                    for m in range(2):
                        i = 2 * c + m
                        src = tile(stage, i)
                        dve.scalar_tensor_tensor(x1T[:, i, :], src, modc[:, 16 + i:17 + i], xR[:, i, :],
                                                 ALU.mult, ALU.add).then_inc(dve_emptied, 1)
                        dve.drain()
                        dve.sem_inc(x1_ready, 1)
                    if c == 3:
                        dve.scalar_tensor_tensor(scaleF[:, :], modc[:, 32:40], 1.0,
                                                 chan[:, K_GFFN:K_GFFN + KT], ALU.add, ALU.mult)
                        inverse_root(N_MEAN["norm2"])
                        for k in range(KT):
                            dve.scalar_tensor_tensor(h2T[:, k, :], x1T[:, k, :], scaleF[:, k:k + 1],
                                                     rms1[:, :], ALU.mult, ALU.mult).then_inc(part_ready, 1)
                        for k in range(KT):
                            lo_part(r1_lo[:, k, :], h2T[:, k, :], r1_hi[:, k, :], 40 + k + 1,
                                    modc[:, 24 + k:25 + k])
                        for k in range(KT):
                            dve.tensor_scalar(h2T[:, k, :], h2T[:, k, :], modc[:, 24 + k:25 + k], None,
                                              ALU.add).then_inc(h2_ready, 1)
            for n in range(8):
                dve.tensor_copy(h2tok[:, n // 2, (n % 2) * S:(n % 2 + 1) * S], tile("h2tok", n))\
                   .then_inc(dve_emptied, 1)
            for n in range(2):
                src = tile("gaterow", n)
                if n == 0:
                    dve.wait_ge(row_in, 32)
                dve.tensor_tensor(gate_row[:, n * S:(n + 1) * S], src, bias_row[:, n * S:(n + 1) * S],
                                  ALU.add).then_inc(dve_emptied, 1)
            wait_emptied(dve, "score", 15)
            dve.memset(s_all[:, NS - 1, :], 0.0)
            dve.drain()
            dve.sem_inc(dot_groups, 2)
            dve.sem_inc(sum_groups, 2)

            iota = cst[:, C_IOTA:C_IOTA + TOPK]

            def top16(vals, at_, src, left):
                dve.max(vals[:, 0:8], src)
                dve.drain()
                dve.max_index(at_[:, 0:8], vals[:, 0:8], src)
                dve.match_replace(left, vals[:, 0:8], src, NEG)
                dve.drain()
                dve.max(vals[:, 8:16], left)
                dve.drain()
                dve.max_index(at_[:, 8:16], vals[:, 8:16], left)

            def route(par):
                for half in range(2):
                    top16(top_v[:, half], top_i[:, half], s_cur[:, par, half], s_left[:, half])
                dve.drain()
                dve.tensor_copy(top_f[:, :, :], top_i[:, :, :])
                dve.tensor_tensor(cand[:, :, :], top_v[:, 0].unsqueeze(2).broadcast_to([P, TOPK, TOPK]),
                                  top_v[:, 1].unsqueeze(1).broadcast_to([P, TOPK, TOPK]), ALU.add)
                dve.drain()
                top16(best, best_at, cand[:, :, :].rearrange("p a b -> p (a b)"), cand_left[:, :])
                dve.drain()
                dve.tensor_scalar(best_ab[:, 0], best_at[:, :], 4, None, ALU.logical_shift_right)
                dve.tensor_scalar(best_ab[:, 1], best_at[:, :], TOPK - 1, None, ALU.bitwise_and)
                dve.tensor_scalar(logit[:, par], best[:, :], best[:, 0:1], None, ALU.subtract)
                dve.drain()
                dve.tensor_copy(best_f[:, :, :], best_ab[:, :, :])
                dve.drain()
                for half in range(2):
                    dve.tensor_tensor(onehot[:, half], best_f[:, half].unsqueeze(2).broadcast_to([P, TOPK, TOPK]),
                                      iota.unsqueeze(1).broadcast_to([P, TOPK, TOPK]), ALU.is_equal)
                dve.drain()
                for half in range(2):
                    dve.tensor_tensor(onehot[:, half], onehot[:, half],
                                      top_f[:, half].unsqueeze(1).broadcast_to([P, TOPK, TOPK]), ALU.mult)
                dve.drain()
                dve.tensor_reduce(picked[:, :, :], onehot[:, :, :, :], AX.X, ALU.add)
                dve.drain()
                dve.scalar_tensor_tensor(idx[:, par], picked[:, 0], float(NKEYS), picked[:, 1],
                                         ALU.mult, ALU.add).then_inc(route_done, 1)

            dve.wait_ge(s_ready, 1)
            route(0)
            with dve.Fori(0, TB) as tb:
                dve.memset(accum[:, :], 0.0)
                dve.wait_ge(h2c_ready, tb + 1)
                dve.sem_inc(dve_step, 1)
                with dve.Fori(0, PH // 2) as hp:
                    for par in range(2):
                        i = tb * PH + hp * 2 + par
                        dve.wait_ge(s_ready, i + 2)
                        dve.sem_inc(dve_step, 1)
                        route(1 - par)
                        dve.wait_ge(exp_done, i + 1)
                        dve.reciprocal(exprec[:, :], expsum[:, par:par + 1])
                        dve.drain()
                        dve.tensor_scalar(share[:, :], expo[:, par], exprec[:, :], None, ALU.mult)

                        def dots(g):
                            for k in range(4):
                                slot = (g % 2) * 4 + k
                                dve.drain()
                                dve.wait_ge(d_in[slot], 16 * (2 * i + g // 2) + 16)
                                last = dve.tensor_tensor_reduce(
                                    out=junk[:, :], in0=d_ring[:, slot, :], in1=h2cur[:, :], scale=1.0,
                                    scalar=0.0, op0=ALU.mult, op1=ALU.add,
                                    accum_out=pre[:, par, 4 * g + k:4 * g + k + 1])
                            last.then_inc(dot_groups, 1)

                        def sums(g):
                            dve.wait_ge(gel_done, 4 * i + g + 1)
                            dve.tensor_tensor(wexp[:, 4 * g:4 * g + 4], gel[:, par, 4 * g:4 * g + 4],
                                              share[:, 4 * g:4 * g + 4], ALU.mult)
                            for k in range(4):
                                slot = (g % 2) * 4 + k
                                dve.drain()
                                dve.wait_ge(u_in[slot], 16 * (2 * i + g // 2) + 16)
                                last = dve.scalar_tensor_tensor(
                                    accum[:, :], u_ring[:, slot, :], wexp[:, 4 * g + k:4 * g + k + 1],
                                    accum[:, :], ALU.mult, ALU.add)
                            last.then_inc(sum_groups, 1)

                        dots(0)
                        for g in range(1, 4):
                            dots(g)
                            sums(g - 1)
                        sums(3)
                dve.drain()
                dve.wait_ge(y_free, tb + 1)
                dve.tensor_tensor(yrow[:, :], accum[:, :], gate_row[:, :], ALU.mult)
                dve.drain()
                dve.tensor_tensor(yrow[:, :], yrow[:, :],
                                  x1tok[:, bass.ds(tb, 1), :].rearrange("p a d -> p (a d)"), ALU.add)\
                   .then_inc(y_ready, 1)
                dve.wait_ge(ss_ready, tb + 1)
                dve.reciprocal(fin_ss[:, 2:3], fin_ss[:, 1:2])
                dve.drain()
                dve.scalar_tensor_tensor(yrow[:, :], yrow[:, :], fin_ss[:, 2:3], gain_row[:, :],
                                         ALU.mult, ALU.mult).then_inc(out_ready, 1)

        @block.gpsimd
        def _(pool):
            with pool.Fori(0, TB * PH // 2) as it:
                for par in range(2):
                    i = it * 2 + par

                    def fetch(ring, table, arrived, freed, g):
                        pool.wait_ge(freed, 4 * i + g + 1)
                        pool.sem_inc(pool_step, 1)
                        for k in range(4):
                            slot = (g % 2) * 4 + k
                            pool.indirect_dma_start(
                                out=ring[:, slot, :], out_offset=None, in_=table,
                                in_offset=bass.IndirectOffsetOnAxis(ap=idx[:, par, 4 * g + k:4 * g + k + 1],
                                                                    axis=0)).then_inc(arrived[slot], 16)

                    pool.wait_ge(route_done, i + 1)
                    pool.sem_inc(pool_step, 1)
                    fetch(d_ring, down, d_in, dot_groups, 0)
                    for g in range(1, 4):
                        fetch(d_ring, down, d_in, dot_groups, g)
                        fetch(u_ring, up, u_in, sum_groups, g - 1)
                    fetch(u_ring, up, u_in, sum_groups, 3)


def constants():
    c = np.zeros((P, C_W), np.float32)
    c[:, C_ID:C_ID + P] = np.eye(P)
    inv = (500000.0 ** (-np.arange(0, ROT, 2) / ROT)).astype(np.float32)
    for p in range(P):
        r = p % HD
        if r < ROT // 2:
            c[p + ROT // 2, C_ROT + p] = -1.0
        elif r < ROT:
            c[p - ROT // 2, C_ROT + p] = 1.0
        if r < ROT:
            c[p, C_FREQ] = inv[r % (ROT // 2)]
    c[:, C_MASK:C_MASK + P] = np.where(np.arange(P)[:, None] >= np.arange(P)[None, :], 0.0, MASKED)
    c[:, C_INV:C_INV + 16] = 1.0 / np.arange(1, 17)
    c[:, C_IOTA:C_IOTA + TOPK] = np.arange(TOPK)
    return c


def kernel(**inputs):
    import concourse.bacc as bacc
    from concourse.bass_utils import run_bass_kernel_spmd

    a = {k: np.asarray(v) for k, v in inputs.items()}

    def chunks(w):
        n = w.shape[1]
        return np.ascontiguousarray(w.reshape(KT, P, n // CH, CH).transpose(2, 1, 0, 3).reshape(n // CH, P, KT * CH))

    def columns(v):
        return v.reshape(-1, P).T

    w_in, w_gate = a["w_in"][0], a["w_gate"][0]
    arrays = {
        "consts": constants(),
        "chans": np.ascontiguousarray(np.concatenate(
            [columns(a[k].reshape(-1)) for k in ("c", "b_ada", "b_gate", "pool_scale", "norm_mix_gain",
                                                 "norm_ffn_gain", "attn_subln_gain")], axis=1)),
        "rows": np.ascontiguousarray(np.broadcast_to(np.concatenate(
            [a["final_norm_gain"], a["b_ada"][0, 5 * D:], a["lambda_q1"][0], a["lambda_k1"][0],
             a["lambda_q2"][0], a["lambda_k2"][0]])[None, :], (P, 2 * D + 4 * HD))),
        "xT": np.ascontiguousarray(a["x"][0].T.reshape(KT, P, S).transpose(1, 0, 2)),
        "pos": np.ascontiguousarray(np.broadcast_to(a["positions"], (P, S))),
        "subk": np.ascontiguousarray(a["peer_sub_keys"][0].transpose(2, 0, 1)),
        "ada": np.ascontiguousarray(a["w_ada"][0].reshape(4, 2, P, 6, D).transpose(3, 0, 2, 1, 4)
                                    .reshape(6, 4, P, 2 * D)),
        "w_xp": chunks(w_in[:, 3 * D:]), "w_q": chunks(w_in[:, :D]), "w_k": chunks(w_in[:, D:2 * D]),
        "w_v": chunks(w_in[:, 2 * D:3 * D]), "w_gateA": chunks(w_gate[:, :D]),
        "w_gateB": chunks(w_gate[:, D:]),
        "w_pool": np.ascontiguousarray(a["pool_w"][0].reshape(4, 2, P, CH).transpose(2, 0, 1, 3)
                                       .reshape(1, P, KT * CH)),
        "w_branchP": chunks(a["w_branch_pool"][0]), "w_branchA": chunks(a["w_branch_attn"][0]),
        "w_out": chunks(a["w_out"][0]), "w_query": chunks(a["peer_w_query"][0]),
        "down": np.ascontiguousarray(a["peer_down"][0]), "up": np.ascontiguousarray(a["peer_up"][0]),
    }
    nc = bacc.Bacc("TRN2", target_bir_lowering=False, num_devices=1)
    t = {k: nc.dram_tensor("in_" + k, v.shape, mybir.dt.from_np(v.dtype), kind="ExternalInput").ap()
         for k, v in arrays.items()}
    out = nc.dram_tensor("out", (TB, P, D), mybir.dt.float32, kind="ExternalOutput").ap()
    wdram = {s: t["w_" + s] for s, _ in STAGES}
    layer(nc, t["consts"], t["chans"], t["rows"], t["xT"], t["pos"], t["subk"], t["ada"], wdram,
          t["down"], t["up"], out)
    r = run_bass_kernel_spmd(nc, [{"in_" + k: v for k, v in arrays.items()}], core_ids=[0])
    return r.results[0]["out"].reshape(1, S, D)
```

```python
import concourse.bass as bass
from concourse import mybir
from contextlib import ExitStack
import numpy as np

P = 128
D = 1024
S = 512
KT = D // P
TB = S // P
CH = 256
HEADS = 8
HD = 64
ROT = 16
WINDOWS = (2, 4, 8, 16)
PADW = 16
NKEYS = 128
PH = 8
TOPK = 16
EPS = 1e-6
LAM_INIT = 0.8 - 0.6 * float(np.exp(-0.3 * 0))
DTB = 3
DT = DTB * P
ET = 128
UN = 8
BT = 8
GC = 32
NEG = -3.0e38
MASKED = -1.0e30
MAGIC = 12582912.0
TWO_PI = (6.28125, 0.0019350051879882812, 3.0199157663446332e-07)
PI_BELOW = 3.1415925

C_ID, C_ROT, C_MASK, C_FREQ, C_INV, C_IOTA = 0, 128, 256, 384, 385, 401
C_W = 401 + 128
K_C, K_BADA, K_BGATE, K_PSCALE, K_GMIX, K_GFFN, K_SUBLN = 0, 8, 56, 72, 80, 88, 96
K_W = 104

STAGES = (("xp", 4), ("gateA", 4), ("pool", 1), ("branchP", 4), ("gateB", 4), ("q", 4), ("k", 4),
          ("v", 4), ("branchA", 4), ("out", 4), ("query", 8))


def chunk_plan():
    return [(s, c) for s, n in STAGES for c in range(n)]


CHUNKS = chunk_plan()
FIRST = {s: CHUNKS.index((s, 0)) for s, _ in STAGES}


def stream_plan():
    order = [("ada", j, r) for j in range(2) for r in range(4)]
    late = [("ada", j, r) for j in range(2, 6) for r in range(4)]
    for n in range(len(CHUNKS)):
        order.append(("w", n))
        if n >= FIRST["pool"] - 3 and late:
            order.append(late.pop(0))
    return order


STREAM = stream_plan()
AT = {item: n for n, item in enumerate(STREAM)}
RAW_SLOTS = 3


def tile_plan():
    tiles = []
    for s, c in CHUNKS:
        if s == "pool":
            tiles += [(s, n, "dve") for n in range(8)]
        elif s == "v":
            tiles += [(s, c * TB + tb, "act") for tb in range(TB)]
        else:
            who = "dve" if s in ("branchP", "branchA", "out") else "act"
            tiles += [(s, 2 * c + n, who) for n in range(2)]
    tiles += [("score", n, "act") for n in range(16)]
    tiles += [("h2tok", n, "dve") for n in range(2)]
    tiles += [("x1tok", n, "act") for n in range(8)]
    tiles += [("gaterow", n, "dve") for n in range(2)]
    return tiles


TILES = tile_plan()
TILE_AT = {(k, i): n for n, (k, i, _) in enumerate(TILES)}


def emptied(kind, index):
    n = TILE_AT[kind, index]
    who = TILES[n][2]
    return who, sum(1 for t in TILES[:n + 1] if t[2] == who)


def layer(nc, consts, chans, rows, xT_d, pos_d, subk_d, ada_d, wdram, downT, down, up, gmat, x1d, out):
    f32, f32r = mybir.dt.float32, mybir.dt.float32r
    i32, u32 = mybir.dt.int32, mybir.dt.uint32
    ALU, ACT, AX = mybir.AluOpType, mybir.ActivationFunctionType, mybir.AxisListType

    with ExitStack() as ctx:
        def sem(name):
            return ctx.enter_context(nc.semaphore(name))

        region = ctx.enter_context(nc.sbuf_tensor("region_base", [P, 1], f32))
        base = 64
        taken = [0]

        def place(name, shape, dt, kb):
            lead = int(kb * 1024) - base
            with ExitStack() as tmp:
                if lead > 0:
                    tmp.enter_context(nc.sbuf_tensor(name + "_lead", [P, lead // 4], f32))
                t = tmp.enter_context(nc.sbuf_tensor(name, shape, dt))
            return t

        low = [0.25]

        def small(name, shape, dt=f32):
            words = int(np.prod(shape[1:]))
            t = place(name, shape, dt, low[0])
            low[0] += ((words * 4 + 63) // 64) * 64 / 1024
            assert low[0] <= 12, low[0]
            return t

        cst = small("cst", [P, C_W])
        chan = small("chan", [P, K_W])
        ones = small("ones", [P, P])
        subk = small("subk", [P, 2, NKEYS])
        rope_cos = small("rope_cos", [P, S])
        rope_sin = small("rope_sin", [P, S])
        cact = small("cact", [P, KT])
        modc = small("modc", [P, 48])
        scaleA = small("scaleA", [P, KT])
        scaleF = small("scaleF", [P, KT])
        eps_t = small("eps_t", [P, 1])
        neglam = small("neglam", [P, 1])
        lamt = small("lamt", [P, 4])
        att_max = small("att_max", [P, 2, 2])
        att_bias = small("att_bias", [P, 2, 2])
        att_sum = small("att_sum", [P, 2, 2])
        att_rec = small("att_rec", [P, 2, 2])
        att_neg = small("att_neg", [P, 2])
        ident = cst[:, C_ID:C_ID + P]
        rotm = cst[:, C_ROT:C_ROT + P]
        mask = cst[:, C_MASK:C_MASK + P]

        raw = place("raw", [P, RAW_SLOTS, KT * CH], f32, 12)
        whi = place("whi", [P, 2, KT, CH], f32r, 36)
        wlo = place("wlo", [P, 2, KT, CH], f32r, 52)
        hT_hi = place("hT_hi", [P, KT, S], f32r, 68)
        hT_lo = place("hT_lo", [P, KT, S], f32r, 84)
        xT = place("xT", [P, KT, S], f32, 100)
        r1_hi = place("r1_hi", [P, KT, S], f32r, 100)
        r1_lo = place("r1_lo", [P, KT, S], f32r, 116)
        qT = place("qT", [P, HEADS, S], f32, 100)
        kT = place("kT", [P, HEADS, S], f32, 116)
        sq1 = place("sq1", [P, KT, S], f32, 132)
        rope_w = place("rope_w", [P, 4, S], f32, 148)
        pos_i = place("pos_i", [P, S], i32, 156)
        lam_w = place("lam_w", [P, 4, HD], f32, 158)
        lam_p = place("lam_p", [P, HD], f32, 159)
        pool_w = place("pool_w", [P, 2, PADW + S], f32, 132)
        pool_y = place("pool_y", [P, 2, S], f32, 137)
        pool_e = place("pool_e", [P, 16], f32, 141)
        ya_hi = place("ya_hi", [P, KT, S], f32r, 132)
        ya_lo = place("ya_lo", [P, KT, S], f32r, 148)
        v_t = place("v_t", [P, TB, D], f32, 132)
        sigB = place("sigB", [P, KT, S], f32, 148)
        tmp1 = place("tmp1", [P, KT, S], f32, 164)
        xpT = place("xpT", [P, KT, PADW + S], f32, 164)
        q_raw = place("q_raw", [P, 2, S], f32, 164)
        q_tmp = place("q_tmp", [P, 2, S], f32, 168)
        oT = place("oT", [P, HEADS, S], f32, 164)
        xR = place("xR", [P, KT, S], f32, 164)
        sq2 = place("sq2", [P, KT, S], f32, 164)
        mergedP = place("mergedP", [P, KT, S], f32, 181)
        acc_ada = place("acc_ada", [P, 2, D], f32, 197)
        rms1 = place("rms1", [P, S], f32, 205)
        prob = place("prob", [P, 2, 2, S], f32, 68)
        comb = place("comb", [P, 2, S], f32, 76)
        combT = place("combT", [P, 2, S], f32, 80)
        rms_o = place("rms_o", [P, 2, S], f32, 68)
        sqo = place("sqo", [P, HEADS, S], f32, 84)
        tmpo = place("tmpo", [P, KT, S], f32, 132)
        x1T = place("x1T", [P, KT, S], f32, 132)
        h2T = place("h2T", [P, KT, S], f32, 148)
        q2T = place("q2T", [P, 2 * PH, S], f32, 68)
        s_all = place("s_all", [P, TB, 2 * PH, NKEYS], f32, 12)
        gstage = place("gstage", [P, 2, ET, GC], f32, 44)
        ohJ = place("ohJ", [P, 2, BT, P], f32r, 76)
        ohI_hi = place("ohI_hi", [P, 2, BT, P], f32r, 84)
        ohI_lo = place("ohI_lo", [P, 2, BT, P], f32r, 92)
        s_cur = place("s_cur", [P, 2 * PH, NKEYS], f32, 132)
        s_left = place("s_left", [P, 2 * PH, NKEYS], f32, 140)
        cand = place("cand", [P, PH, TOPK, TOPK], f32, 148)
        cand_left = place("cand_left", [P, PH, TOPK * TOPK], f32, 156)
        onehot = place("onehot", [P, 2, PH, TOPK, TOPK], f32, 164)
        x1stage = place("x1stage", [P, TB, D], f32, 164)
        draw = place("draw", [P, 4, D], f32, 12)
        uraw = place("uraw", [P, 4, D], f32, 28)
        dhi = place("dhi", [P, 2, KT, P], f32r, 44)
        dlo = place("dlo", [P, 2, KT, P], f32r, 52)
        uhi = place("uhi", [P, 2, D], f32r, 60)
        ulo = place("ulo", [P, 2, D], f32r, 68)
        gtile = place("gtile", [P, 2, DT // GC, 4 * GC], f32, 76)
        ge = place("ge", [P, 2, DT], f32, 88)
        wf = place("wf", [P, 2, DT], f32, 91)
        w_hi = place("w_hi", [P, 2, DT], f32r, 94)
        w_lo = place("w_lo", [P, 2, DT], f32r, 97)
        d_ring = place("d_ring", [P, 4, D], f32, 132)
        u_ring = place("u_ring", [P, 8, D], f32, 148)
        yrow = place("yrow", [P, TB, D], f32, 132)
        x1tok = place("x1tok", [P, TB, D], f32, 12)
        gain_row = place("gain_row", [P, D], f32, 28)
        bias_row = place("bias_row", [P, D], f32, 132)
        at = [181.0]

        def scratch(name, shape, dt=f32):
            t = place(name, shape, dt, at[0])
            at[0] += ((int(np.prod(shape[1:])) * 4 + 63) // 64) * 64 / 1024
            assert at[0] <= 207, at
            return t

        h2row = scratch("h2row", [P, D])
        gate_row = scratch("gate_row", [P, D])
        idx3 = scratch("idx3", [P, P + UN], i32)
        share3 = scratch("share3", [P, P])
        picked = scratch("picked", [P, 3, P])
        ijT = scratch("ijT", [P, 2, P])
        gT_hi = scratch("gT_hi", [P, P], f32r)
        gT_lo = scratch("gT_lo", [P, P], f32r)
        zeros = scratch("zeros", [P, S], f32r)
        assert at[0] <= 197, at
        at = [197.0]
        top_v = scratch("top_v", [P, PH, 2, TOPK])
        top_i = scratch("top_i", [P, PH, 2, TOPK], u32)
        top_f = scratch("top_f", [P, PH, 2, TOPK])
        best = scratch("best", [P, PH, TOPK])
        best_at = scratch("best_at", [P, PH, TOPK], u32)
        best_ab = scratch("best_ab", [P, 2, PH, TOPK], u32)
        best_f = scratch("best_f", [P, 2, PH, TOPK])
        logit = scratch("logit", [P, PH, TOPK])
        expo = scratch("expo", [P, PH, TOPK])
        expsum = scratch("expsum", [P, PH])
        accum = place("accum", [P, D], f32, 197)
        junk = place("junk", [P, D], f32, 201)
        at = [205.0]
        idxc = scratch("idxc", [P, UN], i32)
        sh8 = scratch("sh8", [P, UN])
        pre3 = scratch("pre3", [P, UN])
        gel3 = scratch("gel3", [P, UN])
        wexp = scratch("wexp", [P, UN])
        fin_ss = scratch("fin_ss", [P, 3, TB])

        bank = ctx.enter_context(nc.psum_tensor("bank", [P, 8, S], f32))

        const_in = sem("const_in")
        pos_in = sem("pos_in")
        xT_in = sem("xT_in")
        xR_in = sem("xR_in")
        row_in = sem("row_in")
        raw_in = [sem(f"raw_in{n}") for n in range(RAW_SLOTS)]
        raw_free = sem("raw_free")
        hi_ready = sem("hi_ready")
        lo_ready = sem("lo_ready")
        tile_ready = sem("tile_ready")
        act_emptied = sem("act_emptied")
        dve_emptied = sem("dve_emptied")
        cact_ready = sem("cact_ready")
        ones_ready = sem("ones_ready")
        ada_acc = sem("ada_acc")
        ada_col = sem("ada_col")
        ada_done = sem("ada_done")
        sq_ready = sem("sq_ready")
        mean_ready = sem("mean_ready")
        root_ready = sem("root_ready")
        root_used = sem("root_used")
        part_ready = sem("part_ready")
        ahi_ready = sem("ahi_ready")
        alo_ready = sem("alo_ready")
        sin_arg = sem("sin_arg")
        sin_done = sem("sin_done")
        lam_arg = sem("lam_arg")
        lam_exp = sem("lam_exp")
        rot_ready = sem("rot_ready")
        rot_used = sem("rot_used")
        sc_ready = sem("sc_ready")
        max_ready = sem("max_ready")
        prob_ready = sem("prob_ready")
        comb_ready = sem("comb_ready")
        tr_ready = sem("tr_ready")
        trs_ready = sem("trs_ready")
        pv_ready = sem("pv_ready")
        o_ready = sem("o_ready")
        x1sq_ready = sem("x1sq_ready")
        h2_ready = sem("h2_ready")
        pads = sem("pads")
        x1_stored = sem("x1_stored")
        cur_ready = sem("cur_ready")
        logit_ready = sem("logit_ready")
        exp_done = sem("exp_done")
        picked_ready = sem("picked_ready")
        pickT_ready = sem("pickT_ready")
        pickTs_ready = sem("pickTs_ready")
        gTlo_ready = sem("gTlo_ready")
        ohJ_ready = sem("ohJ_ready")
        ohI_ready = sem("ohI_ready")
        gmm = sem("gmm")
        gbank_free = sem("gbank_free")
        stage_full = sem("stage_full")
        stage_free = sem("stage_free")
        g_stored = sem("g_stored")
        idx_ready = sem("idx_ready")
        draw_free = sem("draw_free")
        uraw_free = sem("uraw_free")
        draw_in = [sem(f"draw_in{n}") for n in range(4)]
        uraw_in = [sem(f"uraw_in{n}") for n in range(4)]
        dhi_ready = sem("dhi_ready")
        dlo_ready = sem("dlo_ready")
        uhi_ready = sem("uhi_ready")
        ulo_ready = sem("ulo_ready")
        g_in = [sem(f"g_in{n}") for n in range(2)]
        g_free = sem("g_free")
        pre_done = sem("pre_done")
        up_done = sem("up_done")
        ge_ready = sem("ge_ready")
        wf_ready = sem("wf_ready")
        whi_ready = sem("whi_ready")
        wlo_ready = sem("wlo_ready")
        psum_done = sem("psum_done")
        idxc_ready = sem("idxc_ready")
        pool_step = sem("pool_step")
        dve_step = sem("dve_step")
        d_in = [sem(f"d_in{n}") for n in range(4)]
        u_in = [sem(f"u_in{n}") for n in range(8)]
        dot_done = sem("dot_done")
        sum_done = sem("sum_done")
        gel3_ready = sem("gel3_ready")
        x1b_in = sem("x1b_in")
        y_ready = sem("y_ready")
        ss_ready = sem("ss_ready")
        out_ready = sem("out_ready")
        out_stored = sem("out_stored")

        block = ctx.enter_context(nc.Block())

        def wait_emptied(eng, kind, index):
            who, n = emptied(kind, index)
            eng.wait_ge(act_emptied if who == "act" else dve_emptied, n)

        def raw_arrived(eng, n):
            eng.wait_ge(raw_in[n % RAW_SLOTS], 16 * (n // RAW_SLOTS + 1))

        def raw_w(n):
            return raw[:, AT["w", n] % RAW_SLOTS, :].rearrange("p (k n) -> p k n", k=KT)

        N_OP = dict(norm1=0, pooled=8, ya=16, o=24, merged=32, norm2=40)
        N_MEAN = dict(norm1=0, o=1, norm2=1 + HEADS)
        UNITS = [(h, qb) for h in range(HEADS) for qb in range(TB)]

        @block.sync
        def _(sp):
            sp.dma_start(cst[:, :], consts).then_inc(const_in, 16)
            sp.dma_start(chan[:, :], chans).then_inc(const_in, 16)
            sp.dma_start(xT[:, :, :], xT_d).then_inc(xT_in, 16)
            for n, item in enumerate(STREAM):
                if n >= RAW_SLOTS:
                    sp.wait_ge(raw_free, n - RAW_SLOTS + 1)
                if item[0] == "ada":
                    src = ada_d[item[1], item[2]]
                else:
                    src = wdram[CHUNKS[item[1]][0]][CHUNKS[item[1]][1]]
                sp.dma_start(raw[:, n % RAW_SLOTS, :], src).then_inc(raw_in[n % RAW_SLOTS], 16)
                if n == 2:
                    sp.dma_start(pos_i[:, :], pos_d).then_inc(pos_in, 16)
                    sp.dma_start(subk[:, :, :], subk_d).then_inc(pos_in, 16)
                    sp.dma_start(lam_w[:, :, :], rows[:, 2 * D:2 * D + 4 * HD]).then_inc(pos_in, 16)
                if item == ("w", FIRST["branchA"] + 1):
                    sp.wait_ge(part_ready, 24)
                    sp.dma_start(xR[:, :, :], xT_d).then_inc(xR_in, 16)
            wait_emptied(sp, "h2tok", 1)
            wait_emptied(sp, "x1tok", 7)
            sp.dma_start(bias_row[:, :], rows[:, D:2 * D]).then_inc(row_in, 16)
            sp.dma_start(x1d, x1stage[:, :, :]).then_inc(x1_stored, 16)
            sp.sem_inc(stage_free, 2)
            with sp.Fori(0, DTB) as tb:
                for c in range(P // GC):
                    n = tb * (P // GC) + c
                    sp.wait_ge(stage_full, n + 1)
                    sp.dma_start(gmat[bass.ds(n, 1)].rearrange("a p i t -> (a p) i t"), gstage[:, c % 2])\
                      .then_inc(g_stored, 16)
                    sp.wait_ge(g_stored, 16 * n + 16)
                    sp.sem_inc(stage_free, 1)
            sp.wait_ge(idx_ready, 1)
            sp.wait_ge(g_stored, 16 * DTB * P // GC)

            def raw_tiles(i, slot, both=True):
                sp.wait_ge(draw_free, i + 1)
                sp.dma_start(draw[:, slot, :], downT[bass.ds(i, 1)].rearrange("a p n -> (a p) n"))\
                  .then_inc(draw_in[slot], 16)
                if both:
                    sp.wait_ge(uraw_free, i + 1)
                    sp.dma_start(uraw[:, slot, :], up[bass.ds(i * P, P), :]).then_inc(uraw_in[slot], 16)

            with sp.Fori(0, ET // UN) as it:
                for e in range(UN):
                    raw_tiles(it * UN + e, e % 4)
                    if e % 4 == 0:
                        half = e // 4
                        sp.wait_ge(g_free, 2 * it + half + 1)
                        sp.dma_start(gtile[:, half],
                                     gmat[:, :, bass.ds(it * UN + e, 4), :]
                                     .rearrange("c p i t -> p c (i t)")).then_inc(g_in[half], 16)
            for n in range(2):
                sp.wait_ge(draw_free, ET + n + 1)
                sp.dma_start(draw[:, n, :], downT[n]).then_inc(draw_in[n], 16)
            sp.wait_ge(uraw_free, ET + 1)
            sp.dma_start(uraw[:, 0, :], up[0:P, :]).then_inc(uraw_in[0], 16)
            sp.wait_ge(draw_free, 4 + ET + 2)
            sp.wait_ge(uraw_free, 4 + ET + 1)
            sp.wait_ge(x1_stored, 16)
            sp.dma_start(x1tok[:, :, :], x1d).then_inc(x1b_in, 16)
            sp.dma_start(gain_row[:, :], rows[:, 0:D]).then_inc(x1b_in, 16)
            for tb in range(TB):
                sp.wait_ge(out_ready, tb + 1)
                sp.dma_start(out[tb], yrow[:, tb, :]).then_inc(out_stored, 16)
            sp.wait_ge(out_stored, 16 * TB)

        @block.tensor
        def _(pe):
            def mm3(dst, lhi, llo, rhi, rlo, first, last):
                pe.matmul(dst, lhi, rhi, start=first, stop=False)
                pe.matmul(dst, lhi, rlo, start=False, stop=False)
                return pe.matmul(dst, llo, rhi, start=False, stop=last)

            def free_bank(t):
                if t >= 4:
                    wait_emptied(pe, *TILES[t - 4][:2])

            def mean(rhs, b=6):
                for k in range(len(rhs)):
                    last = pe.matmul(bank[:, b, :], ones[:, :], rhs[k], start=(k == 0),
                                     stop=(k == len(rhs) - 1))
                last.then_inc(mean_ready, 1)

            def ada_columns(j):
                pe.wait_ge(ada_acc, j + 1)
                if j:
                    pe.wait_ge(ada_done, j)
                for m in range(KT):
                    last = pe.matmul(bank[:, 7, m:m + 1], acc_ada[:, j % 2, m * P:(m + 1) * P],
                                     ones[:, 0:1], start=True, stop=True)
                last.then_inc(ada_col, 1)

            def rotate(n):
                pe.wait_ge(act_emptied, emptied("q", 0)[1] + n)
                if n >= 2:
                    pe.wait_ge(rot_used, n - 1)
                pe.matmul(bank[:, 4 + n % 2, :], rotm, q_raw[:, n % 2, :], start=True, stop=True)\
                  .then_inc(rot_ready, 1)

            pe.wait_ge(const_in, 32)
            pe.wait_ge(ones_ready, 1)
            pe.wait_ge(sq_ready, 8)
            mean([sq1[:, k, :] for k in range(KT)])
            ada_columns(0)
            ada_columns(1)

            ada_before = {}
            for item, n in AT.items():
                if item[0] == "ada" and item[1] >= 2 and item[2] == 3:
                    ada_before[STREAM[n - 1][1]] = item[1]

            def attention():
                def scores(u):
                    h, qb = UNITS[u]
                    par, n = u % 2, (qb + 1) * P
                    if u >= 2:
                        pe.wait_ge(prob_ready, 2 * (u - 1))
                    else:
                        wait_emptied(pe, "v", 4 * TB - 1)
                    for c in range(2):
                        last = pe.matmul(bank[:, 2 * par + c, 0:n],
                                         qT[c * HD:(c + 1) * HD, h, qb * P:(qb + 1) * P],
                                         kT[c * HD:(c + 1) * HD, h, 0:n], start=True, stop=True)
                    last.then_inc(sc_ready, 1)

                def values(u):
                    h, qb = UNITS[u]
                    pe.wait_ge(trs_ready, u + 1)
                    if qb == 0 and h >= 2:
                        pe.wait_ge(o_ready, h - 1)
                    for kb in range(qb + 1):
                        last = pe.matmul(bank[:, 6 + h % 2, qb * P:(qb + 1) * P],
                                         v_t[:, kb, h * P:(h + 1) * P],
                                         combT[:, u % 2, kb * P:(kb + 1) * P],
                                         start=(kb == 0), stop=(kb == qb))
                    last.then_inc(pv_ready, 1)

                pe.wait_ge(rot_used, 2 * HEADS)
                scores(0)
                scores(1)
                for u, (h, qb) in enumerate(UNITS):
                    pe.wait_ge(comb_ready, u + 1)
                    if u >= 2:
                        pe.wait_ge(trs_ready, u - 1)
                    for kb in range(qb + 1):
                        last = pe.transpose(bank[:, 4 + u % 2, kb * P:(kb + 1) * P],
                                            comb[:, u % 2, kb * P:(kb + 1) * P], ident)
                    last.then_inc(tr_ready, 1)
                    if u + 2 < len(UNITS):
                        scores(u + 2)
                    values(u)
                for h in range(HEADS):
                    pe.wait_ge(sq_ready, 8 + h + 1)
                    if h >= 2:
                        pe.wait_ge(root_ready, N_MEAN["o"] + h - 1)
                    mean([sqo[:, h, :]], h % 2)

            def norm2_mean():
                pe.wait_ge(x1sq_ready, 1)
                mean([sq2[:, 0, :]])

            t = 0
            for n, (stage, c) in enumerate(CHUNKS):
                if n in ada_before:
                    ada_columns(ada_before[n])
                if stage == "branchA" and c == 0:
                    attention()
                if stage == "query" and c == 0:
                    norm2_mean()
                if c == 0:
                    ready = {"xp": "norm1", "pool": "pooled", "branchP": "ya", "branchA": "o",
                             "out": "merged", "query": "norm2"}.get(stage)
                    if ready:
                        pe.wait_ge(alo_ready, N_OP[ready] + 8)
                pe.wait_ge(hi_ready, n + 1)
                pe.wait_ge(lo_ready, n + 1)
                wh, wl = whi[:, n % 2], wlo[:, n % 2]
                ah, al = {"pool": (r1_hi, r1_lo), "branchP": (ya_hi, ya_lo), "branchA": (r1_hi, r1_lo),
                          "query": (r1_hi, r1_lo)}.get(stage, (hT_hi, hT_lo))
                if stage == "pool":
                    for g in range(4):
                        for m in range(2):
                            free_bank(t)
                            for k in range(2):
                                kk = 2 * g + k
                                last = mm3(bank[:, t % 4, :], wh[:, kk, m * P:(m + 1) * P],
                                           wl[:, kk, m * P:(m + 1) * P], ah[:, kk, :], al[:, kk, :],
                                           k == 0, k == 1)
                            last.then_inc(tile_ready, 1)
                            t += 1
                elif stage == "v":
                    for tb in range(TB):
                        free_bank(t)
                        for k in range(KT):
                            last = mm3(bank[:, t % 4, 0:CH], ah[:, k, tb * P:(tb + 1) * P],
                                       al[:, k, tb * P:(tb + 1) * P], wh[:, k, :], wl[:, k, :],
                                       k == 0, k == KT - 1)
                        last.then_inc(tile_ready, 1)
                        t += 1
                else:
                    for m in range(2):
                        free_bank(t)
                        for k in range(KT):
                            last = mm3(bank[:, t % 4, :], wh[:, k, m * P:(m + 1) * P],
                                       wl[:, k, m * P:(m + 1) * P], ah[:, k, :], al[:, k, :],
                                       k == 0, k == KT - 1)
                        last.then_inc(tile_ready, 1)
                        t += 1
                if stage in ("q", "k") or (stage == "v" and c == 0):
                    done = 2 * (n - FIRST["q"])
                    for r in range(max(0, done - 2), done):
                        rotate(r)
            for n in range(16):
                tb, g = n // 4, n % 4
                free_bank(t)
                if n == 0:
                    pe.wait_ge(pos_in, 48)
                    wait_emptied(pe, "query", 15)
                for j in range(4):
                    hp = 4 * g + j
                    last = pe.matmul(bank[:, t % 4, j * P:(j + 1) * P], q2T[:, hp, tb * P:(tb + 1) * P],
                                     subk[:, hp % 2, :], start=True, stop=True)
                last.then_inc(tile_ready, 1)
                t += 1
            pe.wait_ge(h2_ready, 8)
            for src, tiles in ((h2T, [6, 7]), (x1T, list(range(8)))):
                for n in tiles:
                    tb, half = n // 2, n % 2
                    free_bank(t)
                    for j in range(4):
                        last = pe.transpose(bank[:, t % 4, j * P:(j + 1) * P],
                                            src[:, 4 * half + j, tb * P:(tb + 1) * P], ident)
                    last.then_inc(tile_ready, 1)
                    t += 1
            for n in range(2):
                free_bank(t)
                pe.matmul(bank[:, t % 4, :], ones[:, :], acc_ada[:, 1, n * S:(n + 1) * S],
                          start=True, stop=True).then_inc(tile_ready, 1)
                t += 1
            wait_emptied(pe, "gaterow", 1)
            pe.sem_inc(gmm, 2)
            with pe.Fori(0, DTB) as tb:
                pe.wait_ge(picked_ready, tb + 1)
                for n in range(3):
                    last = pe.transpose(bank[:, 4, n * P:(n + 1) * P], picked[:, n, :], ident)
                last.then_inc(pickT_ready, 1)
                for b in range(P // BT):
                    par = b % 2
                    pe.wait_ge(ohJ_ready, tb * (P // BT) + b + 1)
                    pe.wait_ge(ohI_ready, tb * (P // BT) + b + 1)
                    pe.wait_ge(gbank_free, tb * (P // BT) + b + 1)
                    for n in range(BT):
                        dst = bank[:, 2 * par + n // 4, (n % 4) * P:(n % 4 + 1) * P]
                        pe.matmul(dst, ohJ[:, par, n, :], ohI_hi[:, par, n, :], start=True, stop=False)
                        last = pe.matmul(dst, ohJ[:, par, n, :], ohI_lo[:, par, n, :], start=False, stop=True)
                    last.then_inc(gmm, 1)
            pe.wait_ge(gbank_free, 2 + DTB * P // BT)
            pe.wait_ge(idx_ready, 1)
            for b in range(2 * DTB):
                pe.matmul(bank[:, b, :], zeros[:, 0:P], zeros[:, :], start=True, stop=False)
            pe.sem_inc(up_done, 1)

            def down_products(par):
                for k in range(KT):
                    last = mm3(bank[:, 6 + par, 0:DT], dhi[:, par, k, :], dlo[:, par, k, :],
                               r1_hi[:, k, 0:DT], r1_lo[:, k, 0:DT], k == 0, k == KT - 1)
                last.then_inc(pre_done, 1)

            pe.wait_ge(dlo_ready, 1)
            down_products(0)
            with pe.Fori(0, ET // UN) as it:
                for e in range(UN):
                    i, par = it * UN + e, e % 2
                    pe.wait_ge(dlo_ready, i + 2)
                    down_products(1 - par)
                    pe.wait_ge(wlo_ready, i + 1)
                    pe.wait_ge(ulo_ready, i + 1)
                    for tb in range(DTB):
                        lh, ll = (x[:, par, tb * P:(tb + 1) * P] for x in (w_hi, w_lo))
                        for half in range(2):
                            rh, rl = (x[:, par, half * S:(half + 1) * S] for x in (uhi, ulo))
                            last = mm3(bank[:, 2 * tb + half, :], lh, ll, rh, rl, False, False)
                    last.then_inc(up_done, 1)
            for b in range(2 * DTB):
                last = pe.matmul(bank[:, b, :], zeros[:, 0:P], zeros[:, :], start=False, stop=True)
            last.then_inc(psum_done, 1)

        def w_done(eng, n):
            stage, c = CHUNKS[n]
            last = {"pool": 7, "v": c * TB + TB - 1}.get(stage, 2 * c + 1)
            eng.wait_ge(tile_ready, TILE_AT[stage, last] + 1)

        @block.scalar
        def _(act):
            def whi_make(n):
                if n >= len(CHUNKS):
                    return
                raw_arrived(act, AT["w", n])
                if n >= 2:
                    w_done(act, n - 2)
                act.activation(whi[:, n % 2], raw_w(n), ACT.Copy).then_inc(hi_ready, 1)

            def tile(kind, i):
                t = TILE_AT[kind, i]
                act.wait_ge(tile_ready, t + 1)
                return bank[:, t % 4, :]

            def root(n, scale, b=6, dst=rms1[:, :], ahead=0):
                act.wait_ge(mean_ready, n + 1)
                if n > ahead:
                    act.wait_ge(root_used, n - ahead)
                act.activation(dst, bank[:, b, :], ACT.Sqrt, bias=eps_t[:, :], scale=scale)\
                   .then_inc(root_ready, 1)

            act.wait_ge(const_in, 32)
            act.activation(cact[:, :], chan[:, K_C:K_C + KT], ACT.Silu).then_inc(cact_ready, 1)
            act.wait_ge(xT_in, 16)
            for k in range(KT):
                act.activation(sq1[:, k, :], xT[:, k, :], ACT.Square).then_inc(sq_ready, 1)
            act.wait_ge(ones_ready, 1)
            root(0, 1.0 / D)
            whi_make(0)
            for k in range(KT):
                act.wait_ge(part_ready, k + 1)
                act.activation(hT_hi[:, k, :], tmp1[:, k, :], ACT.Identity, bias=modc[:, k:k + 1])\
                   .then_inc(ahi_ready, 1)
            for n in range(2):
                act.wait_ge(sin_arg, n + 1)
                act.activation((rope_sin, rope_cos)[n][:, :], rope_w[:, 2 + n, :], ACT.Sin)\
                   .then_inc(sin_done, 1)
            act.wait_ge(lam_arg, 1)
            act.activation(lamt[:, 2:4], lamt[:, 0:2], ACT.Exp).then_inc(lam_exp, 1)

            def attention():
                def exps(u):
                    h, qb = UNITS[u]
                    par, n = u % 2, (qb + 1) * P
                    act.wait_ge(max_ready, u + 1)
                    if u >= 2:
                        act.wait_ge(comb_ready, u - 1)
                    for c in range(2):
                        act.activation(prob[:, par, c, 0:n], bank[:, 2 * par + c, 0:n], ACT.Exp,
                                       bias=att_bias[:, par, c:c + 1], scale=HD ** -0.5,
                                       accum_out=att_sum[:, par, c:c + 1]).then_inc(prob_ready, 1)

                exps(0)
                exps(1)
                for u, (h, qb) in enumerate(UNITS):
                    act.wait_ge(tr_ready, u + 1)
                    if u >= 2:
                        act.wait_ge(pv_ready, u - 1)
                    act.activation(combT[:, u % 2, 0:(qb + 1) * P], bank[:, 4 + u % 2, 0:(qb + 1) * P],
                                   ACT.Copy).then_inc(trs_ready, 1)
                    if qb == 0 and h:
                        act.wait_ge(pv_ready, u)
                        act.activation(oT[:, h - 1, :], bank[:, 6 + (h - 1) % 2, :], ACT.Copy)\
                           .then_inc(o_ready, 1)
                    if u + 2 < len(UNITS):
                        exps(u + 2)
                act.wait_ge(pv_ready, len(UNITS))
                act.activation(oT[:, HEADS - 1, :], bank[:, 6 + (HEADS - 1) % 2, :], ACT.Copy)\
                   .then_inc(o_ready, 1)
                act.drain()
                for h in range(HEADS):
                    act.activation(sqo[:, h, :], oT[:, h, :], ACT.Square).then_inc(sq_ready, 1)
                for h in range(HEADS):
                    root(N_MEAN["o"] + h, 1.0 / P, h % 2, rms_o[:, h % 2, :], min(h, 1))
                    if h:
                        split_o(h - 1)
                split_o(HEADS - 1)

            def split_o(h):
                act.wait_ge(part_ready, 16 + h + 1)
                act.activation(r1_hi[:, h, :], tmpo[:, h, :], ACT.Copy).then_inc(ahi_ready, 1)

            for n, (stage, c) in enumerate(CHUNKS):
                whi_make(n + 1)
                if stage == "branchA" and c == 0:
                    attention()
                if stage == "xp":
                    if c == 0:
                        act.wait_ge(pads, 1)
                    for m in range(2):
                        act.activation(xpT[:, 2 * c + m, PADW:], tile(stage, 2 * c + m), ACT.Copy)\
                           .then_inc(act_emptied, 1)
                elif stage in ("gateA", "gateB"):
                    dst, col = (mergedP, 0) if stage == "gateA" else (sigB, KT)
                    for m in range(2):
                        i = 2 * c + m
                        act.activation(dst[:, i, :], tile(stage, i), ACT.Sigmoid,
                                       bias=chan[:, K_BGATE + col + i:K_BGATE + col + i + 1])\
                           .then_inc(act_emptied, 1)
                        if stage == "gateA":
                            act.wait_ge(part_ready, 8 + i + 1)
                            act.activation(r1_hi[:, i, :], pool_y[:, i % 2, :], ACT.Copy)\
                               .then_inc(ahi_ready, 1)
                elif stage == "pool":
                    for i in range(8):
                        src = tile(stage, i)
                        act.activation(ya_hi[:, i, :], src, ACT.Identity, bias=0.0,
                                       scale=chan[:, K_PSCALE + i:K_PSCALE + i + 1]).then_inc(ahi_ready, 1)
                elif stage in ("q", "k"):
                    for m in range(2):
                        i = 2 * c + m + (HEADS if stage == "k" else 0)
                        src = tile(stage, 2 * c + m)
                        if i >= 2:
                            act.wait_ge(rot_used, i - 1)
                        act.activation(q_raw[:, i % 2, :], src, ACT.Copy).then_inc(act_emptied, 1)
                elif stage == "v":
                    for tb in range(TB):
                        act.activation(v_t[:, tb, c * CH:(c + 1) * CH], tile(stage, c * TB + tb)[:, 0:CH],
                                       ACT.Copy).then_inc(act_emptied, 1)
                elif stage == "branchA":
                    for m in range(2):
                        i = 2 * c + m
                        act.wait_ge(part_ready, 24 + i + 1)
                        act.activation(hT_hi[:, i, :], tmpo[:, i, :], ACT.Copy).then_inc(ahi_ready, 1)
                elif stage == "out":
                    if c == 3:
                        root(N_MEAN["norm2"], 1.0 / D)
                        for k in range(KT):
                            act.wait_ge(part_ready, 32 + k + 1)
                            act.activation(r1_hi[:, k, :], h2T[:, k, :], ACT.Identity,
                                           bias=modc[:, 24 + k:25 + k]).then_inc(ahi_ready, 1)
                elif stage == "query":
                    for m in range(2):
                        act.activation(q2T[:, 2 * c + m, :], tile(stage, 2 * c + m), ACT.Copy)\
                           .then_inc(act_emptied, 1)
            for n in range(16):
                tb, g = n // 4, n % 4
                act.activation(s_all[:, tb, 4 * g:4 * g + 4, :].rearrange("p a b -> p (a b)"),
                               tile("score", n), ACT.Copy).then_inc(act_emptied, 1)
            for n in range(8):
                act.activation(x1stage[:, n // 2, (n % 2) * S:(n % 2 + 1) * S], tile("x1tok", n), ACT.Copy)\
                   .then_inc(act_emptied, 1)
            act.sem_inc(gbank_free, 2)
            wait_emptied(act, "gaterow", 1)

            def softmax_part(src, n):
                act.activation(s_cur[:, :, :].rearrange("p a b -> p (a b)"), src, ACT.Copy)\
                   .then_inc(cur_ready, 1)
                act.wait_ge(logit_ready, n + 1)
                act.activation(expo[:, :, :], logit[:, :, :], ACT.Exp).then_inc(exp_done, 1)

            act.drain()
            with act.Fori(0, DTB) as tb:
                softmax_part(s_all[:, bass.ds(tb, 1)].rearrange("p c a b -> p (c a b)"), tb)
                act.wait_ge(pickT_ready, tb + 1)
                act.activation(ijT[:, :, :].rearrange("p a b -> p (a b)"), bank[:, 4, 0:2 * P], ACT.Copy)
                act.activation(gT_hi[:, :], bank[:, 4, 2 * P:3 * P], ACT.Copy).then_inc(pickTs_ready, 1)
                for b in range(P // BT):
                    n, par = tb * (P // BT) + b, b % 2
                    if b % 4 == 0:
                        act.wait_ge(stage_free, tb * (P // GC) + b // 4 + 1)
                    act.wait_ge(gmm, n + 3)
                    for q in range(2):
                        t0 = BT * (b % 4) + 4 * q
                        last = act.activation(
                            gstage[:, (b // 4) % 2, :, t0:t0 + 4].rearrange("p i t -> p t i"),
                            bank[:, 2 * par + q, :].rearrange("p (t i) -> p t i", t=4), ACT.Copy)
                    last.then_inc(gbank_free, 1)
                    if b % 4 == 3:
                        act.drain()
                        act.sem_inc(stage_full, 1)
            softmax_part(s_all[:, DTB].rearrange("p a b -> p (a b)"), DTB)

            def down_hi(n, slot, par):
                act.wait_ge(draw_in[slot], n)
                act.activation(dhi[:, par].rearrange("p a b -> p (a b)"), draw[:, slot, :], ACT.Copy)\
                   .then_inc(dhi_ready, 1)

            def up_hi(n, slot, par):
                act.wait_ge(uraw_in[slot], n)
                act.activation(uhi[:, par, :], uraw[:, slot, :], ACT.Copy).then_inc(uhi_ready, 1)

            down_hi(16, 0, 0)
            down_hi(16, 1, 1)
            up_hi(16, 0, 0)
            with act.Fori(0, ET // UN) as it:
                for e in range(UN):
                    i, par = it * UN + e, e % 2
                    act.wait_ge(pre_done, i + 1)
                    act.activation(ge[:, par, :], bank[:, 6 + par, 0:DT], ACT.Gelu).then_inc(ge_ready, 1)
                    down_hi(32 * it + 16 * ((e + 2) // 4 + 1), (e + 2) % 4, par)
                    act.wait_ge(wf_ready, i + 1)
                    act.activation(w_hi[:, par, :], wf[:, par, :], ACT.Copy).then_inc(whi_ready, 1)
                    act.wait_ge(up_done, i + 1)
                    up_hi(32 * it + 16 * ((e + 1) // 4 + 1), (e + 1) % 4, 1 - par)
                    act.wait_ge(dot_done, i + 5)
                    act.activation(gel3[:, e:e + 1], pre3[:, e:e + 1], ACT.Gelu).then_inc(gel3_ready, 1)
            for tb in (3, 0, 1, 2):
                act.wait_ge(y_ready, (tb + 1) % TB + 1)
                act.activation(junk[:, :], yrow[:, tb, :], ACT.Square, accum_out=fin_ss[:, 0, tb:tb + 1])
                act.drain()
            act.activation(fin_ss[:, 1, :], fin_ss[:, 0, :], ACT.Sqrt, bias=eps_t[:, :], scale=1.0 / D)\
               .then_inc(ss_ready, 1)

        @block.vector
        def _(dve):
            def ada_chunk(j, r):
                n = AT["ada", j, r]
                raw_arrived(dve, n)
                if j >= 2 and r == 0:
                    dve.wait_ge(ada_col, j - 1)
                acc = acc_ada[:, j % 2, :]
                for k in range(2):
                    src = raw[:, n % RAW_SLOTS, k * D:(k + 1) * D]
                    col = cact[:, 2 * r + k:2 * r + k + 1]
                    if r == 0 and k == 0:
                        last = dve.tensor_scalar(acc, src, col, None, ALU.mult)
                    else:
                        last = dve.scalar_tensor_tensor(acc, src, col, acc, ALU.mult, ALU.add)
                    if k == 0:
                        dve.drain()
                last.then_inc(raw_free, 1)
                dve.drain()
                if r == 3:
                    dve.sem_inc(ada_acc, 1)

            def ada_finish(j):
                dve.wait_ge(ada_col, j + 1)
                dve.tensor_tensor(modc[:, j * KT:(j + 1) * KT], bank[:, 7, 0:KT],
                                  chan[:, K_BADA + j * KT:K_BADA + (j + 1) * KT], ALU.add)\
                   .then_inc(ada_done, 1)

            def wlo_make(n):
                if n >= len(CHUNKS):
                    return
                dve.wait_ge(hi_ready, n + 1)
                dve.tensor_tensor(wlo[:, n % 2], raw_w(n), whi[:, n % 2].bitcast(f32), ALU.subtract)\
                   .then_inc(lo_ready, 1)

            def follow(n):
                if n >= len(CHUNKS):
                    return
                wlo_make(n)
                dve.drain()
                dve.sem_inc(raw_free, 1)
                at_ = AT["w", n] + 1
                if at_ < len(STREAM) and STREAM[at_][0] == "ada":
                    _, j, r = STREAM[at_]
                    if r == 0 and j >= 3:
                        ada_finish(j - 1)
                    ada_chunk(j, r)
                    if j == 5 and r == 3:
                        ada_finish(5)

            def tile(kind, i):
                t = TILE_AT[kind, i]
                dve.wait_ge(tile_ready, t + 1)
                return bank[:, t % 4, :]

            def inverse_root(n, dst=rms1[:, :]):
                dve.wait_ge(root_ready, n + 1)
                dve.reciprocal(dst, dst)
                dve.drain()

            def lo_part(dst, src, hi, count, scalar=None, op=ALU.add):
                dve.wait_ge(ahi_ready, count)
                if scalar is None:
                    ins = dve.tensor_tensor(dst, src, hi.bitcast(f32), ALU.subtract)
                else:
                    ins = dve.scalar_tensor_tensor(dst, src, scalar, hi.bitcast(f32), op, ALU.subtract)
                return ins.then_inc(alo_ready, 1)

            dve.memset(ones[:, :], 1.0)
            dve.memset(eps_t[:, :], EPS)
            dve.drain()
            dve.sem_inc(ones_ready, 1)
            dve.wait_ge(cact_ready, 1)
            for j in range(2):
                for r in range(4):
                    ada_chunk(j, r)
            ada_finish(0)
            ada_finish(1)
            dve.drain()
            dve.scalar_tensor_tensor(scaleA[:, :], modc[:, KT:2 * KT], 1.0, chan[:, K_GMIX:K_GMIX + KT],
                                     ALU.add, ALU.mult)
            inverse_root(0)
            for k in range(KT):
                dve.scalar_tensor_tensor(tmp1[:, k, :], xT[:, k, :], scaleA[:, k:k + 1], rms1[:, :],
                                         ALU.mult, ALU.mult).then_inc(part_ready, 1)
            dve.sem_inc(root_used, 1)
            follow(0)
            for k in range(KT):
                lo_part(hT_lo[:, k, :], tmp1[:, k, :], hT_hi[:, k, :], k + 1, modc[:, k:k + 1])
            dve.drain()
            dve.memset(xpT[:, :, 0:PADW], 0.0)
            dve.memset(pool_w[:, :, 0:PADW], 0.0)
            dve.drain()
            dve.sem_inc(pads, 1)
            dve.wait_ge(pos_in, 48)
            ang, turns = rope_w[:, 0, :], rope_w[:, 1, :]
            dve.tensor_copy(turns, pos_i[:, :])
            dve.drain()
            dve.tensor_scalar(ang, turns, cst[:, C_FREQ:C_FREQ + 1], None, ALU.mult)
            dve.drain()
            for n, shift in ((0, 0.0), (1, 0.25)):
                arg = rope_w[:, 2 + n, :]
                dve.tensor_scalar(turns, ang, 1.0 / (2 * np.pi), shift, ALU.mult, ALU.add)
                dve.drain()
                dve.tensor_scalar(turns, turns, MAGIC, None, ALU.add)
                dve.drain()
                dve.tensor_scalar(turns, turns, -MAGIC, None, ALU.add)
                dve.drain()
                dve.scalar_tensor_tensor(arg, turns, -TWO_PI[0], ang, ALU.mult, ALU.add)
                for part in TWO_PI[1:]:
                    dve.drain()
                    dve.scalar_tensor_tensor(arg, turns, -part, arg, ALU.mult, ALU.add)
                dve.drain()
                if n:
                    dve.tensor_scalar(arg, arg, np.pi / 2, None, ALU.add)
                    dve.drain()
                dve.tensor_scalar(arg, arg, PI_BELOW, -PI_BELOW, ALU.min, ALU.max).then_inc(sin_arg, 1)
                dve.drain()
            for n in range(2):
                dve.tensor_tensor(lam_p[:, :], lam_w[:, 2 * n, :], lam_w[:, 2 * n + 1, :], ALU.mult)
                dve.drain()
                dve.tensor_reduce(lamt[:, n:n + 1], lam_p[:, :], AX.X, ALU.add)
                dve.drain()
            dve.sem_inc(lam_arg, 1)
            dve.wait_ge(lam_exp, 1)
            dve.tensor_tensor(neglam[:, :], lamt[:, 3:4], lamt[:, 2:3], ALU.subtract)
            dve.drain()
            dve.tensor_scalar(neglam[:, :], neglam[:, :], -LAM_INIT, None, ALU.add)

            def pooling(i):
                w = WINDOWS[i // 2]
                if i == 0:
                    wait_emptied(dve, "xp", 7)
                x = xpT[:, i, :]
                src, n = x, 1
                while n < w:
                    dst = pool_w[:, (n.bit_length() - 1) % 2, :]
                    dve.tensor_tensor(dst[:, PADW:], src[:, PADW:], src[:, PADW - n:PADW + S - n], ALU.add)
                    dve.drain()
                    src, n = dst, 2 * n
                y = pool_y[:, i % 2, :]
                if i >= 2:
                    dve.wait_ge(ahi_ready, 8 + i - 1)
                dve.scalar_tensor_tensor(y, src[:, PADW:], 1.0 / w, x[:, PADW:], ALU.mult, ALU.subtract)
                dve.tensor_tensor(pool_e[:, 0:w - 1], src[:, PADW:PADW + w - 1],
                                  cst[:, C_INV:C_INV + w - 1], ALU.mult)
                dve.drain()
                dve.tensor_tensor(y[:, 0:w - 1], pool_e[:, 0:w - 1], x[:, PADW:PADW + w - 1], ALU.subtract)\
                   .then_inc(part_ready, 1)
                dve.drain()
                lo_part(r1_lo[:, i, :], y, r1_hi[:, i, :], 8 + i + 1)

            def attention():
                def maxima(u):
                    h, qb = UNITS[u]
                    par, n = u % 2, (qb + 1) * P
                    dve.wait_ge(sc_ready, u + 1)
                    sc = bank[:, 2 * par:2 * par + 2, 0:n]
                    dve.tensor_tensor(sc[:, :, qb * P:n], sc[:, :, qb * P:n],
                                      mask.unsqueeze(1).broadcast_to([P, 2, P]), ALU.add)
                    dve.drain()
                    dve.tensor_reduce(att_max[:, par, :], sc, AX.X, ALU.max)
                    dve.drain()
                    dve.tensor_scalar(att_bias[:, par, :], att_max[:, par, :], -(HD ** -0.5), None, ALU.mult)\
                       .then_inc(max_ready, 1)

                maxima(0)
                maxima(1)
                for u, (h, qb) in enumerate(UNITS):
                    par, n = u % 2, (qb + 1) * P
                    dve.wait_ge(prob_ready, 2 * (u + 1))
                    dve.reciprocal(att_rec[:, par, :], att_sum[:, par, :])
                    dve.drain()
                    dve.tensor_tensor(att_neg[:, par:par + 1], att_rec[:, par, 1:2], neglam[:, :], ALU.mult)
                    dve.drain()
                    if u >= 2:
                        dve.wait_ge(tr_ready, u - 1)
                    dve.tensor_scalar(comb[:, par, 0:n], prob[:, par, 1, 0:n], att_neg[:, par:par + 1],
                                      None, ALU.mult)
                    dve.drain()
                    dve.scalar_tensor_tensor(comb[:, par, 0:n], prob[:, par, 0, 0:n],
                                             att_rec[:, par, 0:1], comb[:, par, 0:n],
                                             ALU.mult, ALU.add).then_inc(comb_ready, 1)
                    if u + 2 < len(UNITS):
                        maxima(u + 2)
                for h in range(HEADS):
                    inverse_root(N_MEAN["o"] + h, rms_o[:, h % 2, :])
                    dve.scalar_tensor_tensor(tmpo[:, h, :], oT[:, h, :],
                                             chan[:, K_SUBLN + h:K_SUBLN + h + 1], rms_o[:, h % 2, :],
                                             ALU.mult, ALU.mult)
                    dve.drain()
                    dve.sem_inc(root_used, 1)
                    dve.tensor_scalar(tmpo[:, h, :], tmpo[:, h, :], 1.0 - LAM_INIT, None, ALU.mult)\
                       .then_inc(part_ready, 1)
                    dve.drain()
                    lo_part(r1_lo[:, h, :], tmpo[:, h, :], r1_hi[:, h, :], 24 + h + 1)

            for n, (stage, c) in enumerate(CHUNKS):
                if n + 1 < len(CHUNKS):
                    follow(n + 1)
                if stage == "branchA" and c == 0:
                    attention()
                if stage == "gateA":
                    for m in range(2):
                        pooling(2 * c + m)
                elif stage == "pool":
                    for i in range(8):
                        src = tile(stage, i)
                        lo_part(ya_lo[:, i, :], src, ya_hi[:, i, :], 16 + i + 1,
                                chan[:, K_PSCALE + i:K_PSCALE + i + 1], ALU.mult)
                        dve.drain()
                        dve.sem_inc(dve_emptied, 1)
                elif stage == "branchP":
                    for m in range(2):
                        i = 2 * c + m
                        src = tile(stage, i)
                        wait_emptied(dve, "gateA", i)
                        dve.tensor_tensor(mergedP[:, i, :], src, mergedP[:, i, :], ALU.mult)\
                           .then_inc(dve_emptied, 1)
                elif stage in ("q", "k") or (stage == "v" and c == 0):
                    done = 2 * (n - FIRST["q"])
                    for r in range(max(0, done - 2), done):
                        dve.wait_ge(rot_ready, r + 1)
                        if r == 0:
                            dve.wait_ge(sin_done, 2)
                        dst = (qT if r < HEADS else kT)[:, r % HEADS, :]
                        dve.tensor_tensor(q_tmp[:, 0, :], q_raw[:, r % 2, :], rope_cos[:, :], ALU.mult)
                        dve.tensor_tensor(q_tmp[:, 1, :], bank[:, 4 + r % 2, :], rope_sin[:, :], ALU.mult)
                        dve.drain()
                        dve.tensor_tensor(dst, q_tmp[:, 0, :], q_tmp[:, 1, :], ALU.add)\
                           .then_inc(rot_used, 1)
                        dve.drain()
                elif stage == "branchA":
                    for m in range(2):
                        i = 2 * c + m
                        src = tile(stage, i)
                        dve.tensor_tensor(tmpo[:, i, :], src, sigB[:, i, :], ALU.mult)\
                           .then_inc(dve_emptied, 1)
                        dve.drain()
                        dve.tensor_tensor(tmpo[:, i, :], tmpo[:, i, :], mergedP[:, i, :], ALU.add)\
                           .then_inc(part_ready, 1)
                        dve.drain()
                        lo_part(hT_lo[:, i, :], tmpo[:, i, :], hT_hi[:, i, :], 32 + i + 1)
                elif stage == "out":
                    if c == 0:
                        dve.wait_ge(xR_in, 16)
                    for m in range(2):
                        i = 2 * c + m
                        src = tile(stage, i)
                        dve.scalar_tensor_tensor(x1T[:, i, :], src, modc[:, 16 + i:17 + i], xR[:, i, :],
                                                 ALU.mult, ALU.add).then_inc(dve_emptied, 1)
                        dve.drain()
                        dst = sq2[:, min(i, 1), :]
                        dve.tensor_tensor(dst, x1T[:, i, :], x1T[:, i, :], ALU.mult)
                        dve.drain()
                        if i:
                            dve.tensor_tensor(sq2[:, 0, :], sq2[:, 0, :], dst, ALU.add)
                            dve.drain()
                        if i == KT - 1:
                            dve.sem_inc(x1sq_ready, 1)
                    if c == 3:
                        dve.scalar_tensor_tensor(scaleF[:, :], modc[:, 32:40], 1.0,
                                                 chan[:, K_GFFN:K_GFFN + KT], ALU.add, ALU.mult)
                        inverse_root(N_MEAN["norm2"])
                        for k in range(KT):
                            dve.scalar_tensor_tensor(h2T[:, k, :], x1T[:, k, :], scaleF[:, k:k + 1],
                                                     rms1[:, :], ALU.mult, ALU.mult).then_inc(part_ready, 1)
                        for k in range(KT):
                            lo_part(r1_lo[:, k, :], h2T[:, k, :], r1_hi[:, k, :], 40 + k + 1,
                                    modc[:, 24 + k:25 + k])
                        for k in range(KT):
                            dve.tensor_scalar(h2T[:, k, :], h2T[:, k, :], modc[:, 24 + k:25 + k], None,
                                              ALU.add).then_inc(h2_ready, 1)
            for n in range(2):
                dve.tensor_copy(h2row[:, n * S:(n + 1) * S], tile("h2tok", n)).then_inc(dve_emptied, 1)
            for n in range(2):
                src = tile("gaterow", n)
                if n == 0:
                    dve.wait_ge(row_in, 16)
                dve.tensor_tensor(gate_row[:, n * S:(n + 1) * S], src, bias_row[:, n * S:(n + 1) * S],
                                  ALU.add).then_inc(dve_emptied, 1)
            dve.memset(zeros[:, :].bitcast(f32), 0.0)
            dve.memset(idx3[:, P:P + UN], 0)
            dve.wait_ge(x1_stored, 16)
            iota = cst[:, C_IOTA:C_IOTA + P]
            grid = [P, PH, TOPK, TOPK]

            def top16(vals, at_, src, left):
                rows_ = range(len(src))
                for n in rows_:
                    dve.max(vals[n][:, 0:8], src[n])
                dve.drain()
                for n in rows_:
                    dve.max_index(at_[n][:, 0:8], vals[n][:, 0:8], src[n])
                    dve.match_replace(left[n], vals[n][:, 0:8], src[n], NEG)
                dve.drain()
                for n in rows_:
                    dve.max(vals[n][:, 8:16], left[n])
                dve.drain()
                for n in rows_:
                    dve.max_index(at_[n][:, 8:16], vals[n][:, 8:16], left[n])
                dve.drain()

            def route(n):
                hp = [(h, half) for h in range(PH) for half in range(2)]
                top16([top_v[:, h, x] for h, x in hp], [top_i[:, h, x] for h, x in hp],
                      [s_cur[:, 2 * h + x] for h, x in hp], [s_left[:, 2 * h + x] for h, x in hp])
                dve.tensor_copy(top_f[:, :, :, :], top_i[:, :, :, :])
                dve.tensor_tensor(cand[:, :, :, :], top_v[:, :, 0].unsqueeze(3).broadcast_to(grid),
                                  top_v[:, :, 1].unsqueeze(2).broadcast_to(grid), ALU.add)
                dve.drain()
                top16([best[:, h] for h in range(PH)], [best_at[:, h] for h in range(PH)],
                      [cand[:, h].rearrange("p a b -> p (a b)") for h in range(PH)],
                      [cand_left[:, h] for h in range(PH)])
                dve.tensor_tensor(logit[:, :, :], best[:, :, :],
                                  best[:, :, 0:1].broadcast_to([P, PH, TOPK]), ALU.subtract)\
                   .then_inc(logit_ready, 1)
                dve.tensor_scalar(best_ab[:, 0], best_at[:, :, :], 4, None, ALU.logical_shift_right)
                dve.tensor_scalar(best_ab[:, 1], best_at[:, :, :], TOPK - 1, None, ALU.bitwise_and)
                dve.drain()
                dve.tensor_copy(best_f[:, :, :, :], best_ab[:, :, :, :])
                dve.drain()
                for x in range(2):
                    dve.tensor_tensor(onehot[:, x], best_f[:, x].unsqueeze(3).broadcast_to(grid),
                                      iota[:, 0:TOPK].unsqueeze(1).unsqueeze(1).broadcast_to(grid),
                                      ALU.is_equal)
                dve.drain()
                for x in range(2):
                    dve.tensor_tensor(onehot[:, x], onehot[:, x],
                                      top_f[:, :, x].unsqueeze(2).broadcast_to(grid), ALU.mult)
                dve.drain()
                for x in range(2):
                    dve.tensor_reduce(picked[:, x, :].rearrange("p (a b) -> p a b", a=PH), onehot[:, x],
                                      AX.X, ALU.add)
                dve.wait_ge(exp_done, n + 1)
                dve.tensor_reduce(expsum[:, :], expo[:, :, :], AX.X, ALU.add)
                dve.drain()
                dve.reciprocal(expsum[:, :], expsum[:, :])
                dve.drain()
                return dve.tensor_tensor(picked[:, 2, :].rearrange("p (a b) -> p a b", a=PH),
                                         expo[:, :, :], expsum[:, :].unsqueeze(2)
                                         .broadcast_to([P, PH, TOPK]), ALU.mult)

            with dve.Fori(0, DTB) as tb:
                dve.wait_ge(cur_ready, tb + 1)
                dve.sem_inc(dve_step, 1)
                route(tb).then_inc(picked_ready, 1)
                dve.wait_ge(pickTs_ready, tb + 1)
                dve.tensor_tensor(gT_lo[:, :], bank[:, 4, 2 * P:3 * P], gT_hi[:, :].bitcast(f32),
                                  ALU.subtract).then_inc(gTlo_ready, 1)
                dve.drain()
                for b in range(P // BT):
                    par = b % 2
                    dve.wait_ge(gmm, tb * (P // BT) + b + 1)
                    for n in range(BT):
                        t0 = b * BT + n
                        for dst, g in ((ohI_hi, gT_hi), (ohI_lo, gT_lo)):
                            last = dve.tensor_scalar(dst[:, par, n, :], iota, ijT[:, 0, t0:t0 + 1],
                                                     g[:, t0:t0 + 1].bitcast(f32), ALU.is_equal, ALU.mult)
                    last.then_inc(ohI_ready, 1)
            dve.wait_ge(cur_ready, DTB + 1)
            route(DTB)
            dve.drain()
            dve.scalar_tensor_tensor(idx3[:, 0:P], picked[:, 0, :], float(NKEYS), picked[:, 1, :],
                                     ALU.mult, ALU.add)
            dve.tensor_copy(share3[:, :], picked[:, 2, :])
            dve.memset(accum[:, :], 0.0)
            dve.drain()
            dve.sem_inc(idx_ready, 1)
            for s_, n in ((draw_free, 4), (uraw_free, 4), (g_free, 2), (dot_done, 4), (sum_done, 8)):
                dve.sem_inc(s_, n)

            def down_lo(n, slot, par):
                dve.wait_ge(dhi_ready, n + 1)
                dve.tensor_tensor(dlo[:, par].rearrange("p a b -> p (a b)"), draw[:, slot, :],
                                  dhi[:, par].rearrange("p a b -> p (a b)").bitcast(f32), ALU.subtract)\
                   .then_inc(dlo_ready, 1)

            def up_lo(n, slot, par):
                dve.wait_ge(uhi_ready, n + 1)
                dve.tensor_tensor(ulo[:, par, :], uraw[:, slot, :], uhi[:, par, :].bitcast(f32),
                                  ALU.subtract).then_inc(ulo_ready, 1)

            down_lo(0, 0, 0)
            down_lo(1, 1, 1)
            up_lo(0, 0, 0)
            dve.drain()
            dve.sem_inc(draw_free, 2)
            dve.sem_inc(uraw_free, 1)
            with dve.Fori(0, ET // UN) as it:
                dve.tensor_copy(sh8[:, :], share3[:, bass.ds(it * UN, UN)])
                for e in range(UN):
                    i, par = it * UN + e, e % 2

                    def summed(k):
                        dve.wait_ge(gel3_ready, it * UN + k + 1)
                        dve.tensor_tensor(wexp[:, k:k + 1], gel3[:, k:k + 1], sh8[:, k:k + 1], ALU.mult)
                        dve.drain()
                        dve.wait_ge(u_in[k], 16 * it + 16)
                        dve.scalar_tensor_tensor(accum[:, :], u_ring[:, k, :], wexp[:, k:k + 1],
                                                 accum[:, :], ALU.mult, ALU.add).then_inc(sum_done, 1)

                    dve.wait_ge(ge_ready, i + 1)
                    if e % 4 == 0:
                        dve.wait_ge(g_in[e // 4], 16 * it + 16)
                    dve.tensor_tensor(wf[:, par, :].rearrange("p (c t) -> p c t", t=GC),
                                      ge[:, par, :].rearrange("p (c t) -> p c t", t=GC),
                                      gtile[:, e // 4, :, (e % 4) * GC:(e % 4 + 1) * GC], ALU.mult)\
                       .then_inc(wf_ready, 1)
                    down_lo(i + 2, (e + 2) % 4, par)
                    dve.wait_ge(whi_ready, i + 1)
                    dve.tensor_tensor(w_lo[:, par, :], wf[:, par, :], w_hi[:, par, :].bitcast(f32),
                                      ALU.subtract).then_inc(wlo_ready, 1)
                    dve.drain()
                    dve.sem_inc(draw_free, 1)
                    if e % 4 == 3:
                        dve.sem_inc(g_free, 1)
                    dve.wait_ge(d_in[e % 4], 32 * it + 16 * (e // 4 + 1))
                    dve.tensor_tensor_reduce(out=junk[:, :], in0=d_ring[:, e % 4, :], in1=h2row[:, :],
                                             scale=1.0, scalar=0.0, op0=ALU.mult, op1=ALU.add,
                                             accum_out=pre3[:, e:e + 1]).then_inc(dot_done, 1)
                    up_lo(i + 1, (e + 1) % 4, 1 - par)
                    dve.drain()
                    dve.sem_inc(uraw_free, 1)
                    if e:
                        summed(e - 1)
                    if e == UN - 1:
                        summed(e)
            dve.drain()
            dve.wait_ge(x1b_in, 32)
            dve.wait_ge(psum_done, 1)
            for tb in (3, 0, 1, 2):
                src = accum[:, :] if tb == 3 else bank[:, 2 * tb:2 * tb + 2, :].rearrange("p a b -> p (a b)")
                dve.tensor_tensor(yrow[:, tb, :], src, gate_row[:, :], ALU.mult)
                dve.drain()
                dve.tensor_tensor(yrow[:, tb, :], yrow[:, tb, :], x1tok[:, tb, :], ALU.add)\
                   .then_inc(y_ready, 1)
            dve.wait_ge(ss_ready, 1)
            dve.reciprocal(fin_ss[:, 2, :], fin_ss[:, 1, :])
            dve.drain()
            for tb in range(TB):
                dve.scalar_tensor_tensor(yrow[:, tb, :], yrow[:, tb, :], fin_ss[:, 2, tb:tb + 1],
                                         gain_row[:, :], ALU.mult, ALU.mult).then_inc(out_ready, 1)

        @block.gpsimd
        def _(pool):
            iota = cst[:, C_IOTA:C_IOTA + P]
            with pool.Fori(0, DTB) as tb:
                pool.wait_ge(pickTs_ready, tb + 1)
                pool.sem_inc(pool_step, 1)
                for b in range(P // BT):
                    pool.wait_ge(gmm, tb * (P // BT) + b + 1)
                    pool.sem_inc(pool_step, 1)
                    for n in range(BT):
                        t0 = b * BT + n
                        last = pool.tensor_scalar(ohJ[:, b % 2, n, :], iota, ijT[:, 1, t0:t0 + 1], None,
                                                  ALU.is_equal)
                    last.then_inc(ohJ_ready, 1)
            pool.wait_ge(idx_ready, 1)
            pool.tensor_copy(idxc[:, :], idx3[:, 0:UN]).then_inc(idxc_ready, 1)
            with pool.Fori(0, ET // UN) as it:
                pool.wait_ge(idxc_ready, it + 1)
                pool.sem_inc(pool_step, 1)
                for e in range(UN):
                    for ring, slot, table, arrived, freed in (
                            (d_ring, e % 4, down, d_in, dot_done), (u_ring, e, up, u_in, sum_done)):
                        pool.wait_ge(freed, it * UN + e + 1)
                        pool.sem_inc(pool_step, 1)
                        pool.indirect_dma_start(
                            out=ring[:, slot, :], out_offset=None, in_=table,
                            in_offset=bass.IndirectOffsetOnAxis(ap=idxc[:, e:e + 1], axis=0))\
                            .then_inc(arrived[slot], 16)
                for slot in range(4):
                    pool.wait_ge(d_in[slot], 32 * it + 32)
                for slot in range(UN):
                    pool.wait_ge(u_in[slot], 16 * it + 16)
                pool.sem_inc(pool_step, 1)
                pool.tensor_copy(idxc[:, :], idx3[:, bass.ds((it + 1) * UN, UN)]).then_inc(idxc_ready, 1)


def constants():
    c = np.zeros((P, C_W), np.float32)
    c[:, C_ID:C_ID + P] = np.eye(P)
    inv = (500000.0 ** (-np.arange(0, ROT, 2) / ROT)).astype(np.float32)
    for p in range(P):
        r = p % HD
        if r < ROT // 2:
            c[p + ROT // 2, C_ROT + p] = -1.0
        elif r < ROT:
            c[p - ROT // 2, C_ROT + p] = 1.0
        if r < ROT:
            c[p, C_FREQ] = inv[r % (ROT // 2)]
    c[:, C_MASK:C_MASK + P] = np.where(np.arange(P)[:, None] >= np.arange(P)[None, :], 0.0, MASKED)
    c[:, C_INV:C_INV + 16] = 1.0 / np.arange(1, 17)
    c[:, C_IOTA:C_IOTA + P] = np.arange(P)
    return c


def kernel(**inputs):
    import concourse.bacc as bacc
    from concourse.bass_utils import run_bass_kernel_spmd

    a = {k: np.asarray(v) for k, v in inputs.items()}

    def chunks(w):
        n = w.shape[1]
        return np.ascontiguousarray(w.reshape(KT, P, n // CH, CH).transpose(2, 1, 0, 3).reshape(n // CH, P, KT * CH))

    def columns(v):
        return v.reshape(-1, P).T

    w_in, w_gate = a["w_in"][0], a["w_gate"][0]
    arrays = {
        "consts": constants(),
        "chans": np.ascontiguousarray(np.concatenate(
            [columns(a[k].reshape(-1)) for k in ("c", "b_ada", "b_gate", "pool_scale", "norm_mix_gain",
                                                 "norm_ffn_gain", "attn_subln_gain")], axis=1)),
        "rows": np.ascontiguousarray(np.broadcast_to(np.concatenate(
            [a["final_norm_gain"], a["b_ada"][0, 5 * D:], a["lambda_q1"][0], a["lambda_k1"][0],
             a["lambda_q2"][0], a["lambda_k2"][0]])[None, :], (P, 2 * D + 4 * HD))),
        "xT": np.ascontiguousarray(a["x"][0].T.reshape(KT, P, S).transpose(1, 0, 2)),
        "pos": np.ascontiguousarray(np.broadcast_to(a["positions"], (P, S))),
        "subk": np.ascontiguousarray(a["peer_sub_keys"][0].transpose(2, 0, 1)),
        "ada": np.ascontiguousarray(a["w_ada"][0].reshape(4, 2, P, 6, D).transpose(3, 0, 2, 1, 4)
                                    .reshape(6, 4, P, 2 * D)),
        "w_xp": chunks(w_in[:, 3 * D:]), "w_q": chunks(w_in[:, :D]), "w_k": chunks(w_in[:, D:2 * D]),
        "w_v": chunks(w_in[:, 2 * D:3 * D]), "w_gateA": chunks(w_gate[:, :D]),
        "w_gateB": chunks(w_gate[:, D:]),
        "w_pool": np.ascontiguousarray(a["pool_w"][0].reshape(4, 2, P, CH).transpose(2, 0, 1, 3)
                                       .reshape(1, P, KT * CH)),
        "w_branchP": chunks(a["w_branch_pool"][0]), "w_branchA": chunks(a["w_branch_attn"][0]),
        "w_out": chunks(a["w_out"][0]), "w_query": chunks(a["peer_w_query"][0]),
        "downT": np.ascontiguousarray(a["peer_down"][0].reshape(ET, P, KT, P).transpose(0, 3, 2, 1)
                                      .reshape(ET, P, D)),
        "down": np.ascontiguousarray(a["peer_down"][0]), "up": np.ascontiguousarray(a["peer_up"][0]),
    }
    nc = bacc.Bacc("TRN2", target_bir_lowering=False, num_devices=1)
    t = {k: nc.dram_tensor("in_" + k, v.shape, mybir.dt.from_np(v.dtype), kind="ExternalInput").ap()
         for k, v in arrays.items()}
    gmat = nc.dram_tensor("gmat", (DT // GC, P, ET, GC), mybir.dt.float32, kind="Internal").ap()
    x1d = nc.dram_tensor("x1d", (P, TB, D), mybir.dt.float32, kind="Internal").ap()
    out = nc.dram_tensor("out", (TB, P, D), mybir.dt.float32, kind="ExternalOutput").ap()
    wdram = {s: t["w_" + s] for s, _ in STAGES}
    layer(nc, t["consts"], t["chans"], t["rows"], t["xT"], t["pos"], t["subk"], t["ada"], wdram,
          t["downT"], t["down"], t["up"], gmat, x1d, out)
    r = run_bass_kernel_spmd(nc, [{"in_" + k: v for k, v in arrays.items()}], core_ids=[0])
    return r.results[0]["out"].reshape(1, S, D)
```

```python
import concourse.bass as bass
from concourse import mybir
from contextlib import ExitStack
import numpy as np

P = 128
D = 1024
S = 512
KT = D // P
TB = S // P
CH = 256
HEADS = 8
HD = 64
ROT = 16
WINDOWS = (2, 4, 8, 16)
PADW = 16
NKEYS = 128
PH = 8
TOPK = 16
EPS = 1e-6
LAM_INIT = 0.8 - 0.6 * float(np.exp(-0.3 * 0))
DTB = 3
DT = DTB * P
ET = 128
UN = 16
BT = 8
GC = 16
GG = 8
DN0 = 20
DNA = 10
DNB = 26
DN = DNA + DNB
DR = 3
EXP_AT = 10
EXPB_AT = 7
DROWS = 5
NEXT_AT = 10
ROWS = 45
NEG = -3.0e38
MASKED = -1.0e30
MAGIC = 12582912.0
TWO_PI = (6.28125, 0.0019350051879882812, 3.0199157663446332e-07)
PI_BELOW = 3.1415925

C_ID, C_ROT, C_MASK, C_FREQ, C_INV, C_IOTA = 0, 128, 256, 384, 385, 401
C_W = 401 + 128
K_C, K_BADA, K_BGATE, K_PSCALE, K_GMIX, K_GFFN, K_SUBLN = 0, 8, 56, 72, 80, 88, 96
K_W = 104

STAGES = (("xp", 4), ("gateA", 4), ("pool", 1), ("branchP", 4), ("gateB", 4), ("q", 4), ("k", 4),
          ("v", 4), ("branchA", 4), ("out", 4), ("query", 8))


def chunk_plan():
    return [(s, c) for s, n in STAGES for c in range(n)]


CHUNKS = chunk_plan()
FIRST = {s: CHUNKS.index((s, 0)) for s, _ in STAGES}


def stream_plan():
    order = [("ada", j, r) for j in range(2) for r in range(4)]
    late = [("ada", j, r) for j in range(2, 6) for r in range(4)]
    for n in range(len(CHUNKS)):
        order.append(("w", n))
        if n >= FIRST["pool"] - 3 and late:
            order.append(late.pop(0))
    return order


STREAM = stream_plan()
AT = {item: n for n, item in enumerate(STREAM)}
RAW_SLOTS = 3


def after_batch(b):
    first = DNA + b * DNB * BT // P
    return list(range(first, DNA + (b + 1) * DNB * BT // P))

def rows_of_batch(b):
    return list(range(3 * b - 3, 3 * b)) if b else []


def tile_plan():
    tiles = []
    for s, c in CHUNKS:
        if (s, c) == ("query", 0):
            tiles += [("x1tok", n, "act") for n in range(8)]
        if s == "pool":
            tiles += [(s, n, "dve") for n in range(8)]
        elif s == "v":
            tiles += [(s, c * TB + tb, "act") for tb in range(TB)]
        else:
            who = "dve" if s in ("branchP", "branchA", "out") else "act"
            tiles += [(s, 2 * c + n, who) for n in range(2)]
    tiles += [("h2tok", n, "dve") for n in range(2)]
    tiles += [("gaterow", n, "dve") for n in range(2)]
    tiles += [("score", n, "act") for n in range(16)]
    return tiles


TILES = tile_plan()
TILE_AT = {(k, i): n for n, (k, i, _) in enumerate(TILES)}


def emptied(kind, index):
    n = TILE_AT[kind, index]
    who = TILES[n][2]
    return who, sum(1 for t in TILES[:n + 1] if t[2] == who)


def layer(nc, consts, chans, rows, xT_d, pos_d, subk_d, ada_d, wdram, downT, down, up, gmat, ged, x1d, gated, out):
    f32, f32r = mybir.dt.float32, mybir.dt.float32r
    i32, u32 = mybir.dt.int32, mybir.dt.uint32
    ALU, ACT, AX = mybir.AluOpType, mybir.ActivationFunctionType, mybir.AxisListType

    with ExitStack() as ctx:
        def sem(name):
            return ctx.enter_context(nc.semaphore(name))

        region = ctx.enter_context(nc.sbuf_tensor("region_base", [P, 1], f32))
        base = 64
        taken = [0]

        def place(name, shape, dt, kb):
            lead = int(kb * 1024) - base
            with ExitStack() as tmp:
                if lead > 0:
                    tmp.enter_context(nc.sbuf_tensor(name + "_lead", [P, lead // 4], f32))
                t = tmp.enter_context(nc.sbuf_tensor(name, shape, dt))
            return t

        low = [0.25]

        def small(name, shape, dt=f32):
            words = int(np.prod(shape[1:]))
            t = place(name, shape, dt, low[0])
            low[0] += ((words * 4 + 63) // 64) * 64 / 1024
            assert low[0] <= 12, low[0]
            return t

        cst = small("cst", [P, C_W])
        chan = small("chan", [P, K_W])
        ones = small("ones", [P, P])
        subk = small("subk", [P, 2, NKEYS])
        rope_cos = small("rope_cos", [P, S])
        rope_sin = small("rope_sin", [P, S])
        cact = small("cact", [P, KT])
        modc = small("modc", [P, 48])
        scaleA = small("scaleA", [P, KT])
        scaleF = small("scaleF", [P, KT])
        eps_t = small("eps_t", [P, 1])
        neglam = small("neglam", [P, 1])
        lamt = small("lamt", [P, 4])
        att_max = small("att_max", [P, 2, 2])
        att_bias = small("att_bias", [P, 2, 2])
        att_sum = small("att_sum", [P, 2, 2])
        att_rec = small("att_rec", [P, 2, 2])
        att_neg = small("att_neg", [P, 2])
        gain_o = small("gain_o", [P, HEADS])
        ident = cst[:, C_ID:C_ID + P]
        rotm = cst[:, C_ROT:C_ROT + P]
        mask = cst[:, C_MASK:C_MASK + P]

        raw = place("raw", [P, RAW_SLOTS, KT * CH], f32, 12)
        whi = place("whi", [P, 2, KT, CH], f32r, 36)
        wlo = place("wlo", [P, 2, KT, CH], f32r, 52)
        hT_hi = place("hT_hi", [P, KT, S], f32r, 68)
        hT_lo = place("hT_lo", [P, KT, S], f32r, 84)
        xT = place("xT", [P, KT, S], f32, 100)
        r1_hi = place("r1_hi", [P, KT, S], f32r, 100)
        r1_lo = place("r1_lo", [P, KT, S], f32r, 116)
        qT = place("qT", [P, HEADS, S], f32, 100)
        kT = place("kT", [P, HEADS, S], f32, 116)
        sq1 = place("sq1", [P, KT, S], f32, 132)
        rope_w = place("rope_w", [P, 4, S], f32, 148)
        pos_i = place("pos_i", [P, S], i32, 156)
        lam_w = place("lam_w", [P, 4, HD], f32, 158)
        lam_p = place("lam_p", [P, HD], f32, 159)
        pool_w = place("pool_w", [P, 2, PADW + S], f32, 132)
        pool_y = place("pool_y", [P, 2, S], f32, 137)
        pool_e = place("pool_e", [P, 16], f32, 141)
        ya_hi = place("ya_hi", [P, KT, S], f32r, 132)
        ya_lo = place("ya_lo", [P, KT, S], f32r, 148)
        v_t = place("v_t", [P, TB, D], f32, 132)
        sigB = place("sigB", [P, KT, S], f32, 148)
        tmp1 = place("tmp1", [P, KT, S], f32, 164)
        xpT = place("xpT", [P, KT, PADW + S], f32, 164)
        q_raw = place("q_raw", [P, 2, S], f32, 164)
        q_tmp = place("q_tmp", [P, 2, S], f32, 168)
        oT = place("oT", [P, HEADS, S], f32, 164)
        xR = place("xR", [P, KT, S], f32, 164)
        sq2 = place("sq2", [P, KT, S], f32, 164)
        mergedP = place("mergedP", [P, KT, S], f32, 181)
        acc_ada = place("acc_ada", [P, 2, D], f32, 197)
        rms1 = place("rms1", [P, S], f32, 205)
        prob = place("prob", [P, 2, 2, S], f32, 68)
        comb = place("comb", [P, 2, S], f32, 76)
        combT = place("combT", [P, 2, S], f32, 80)
        sqo = place("sqo", [P, S], f32, 84)
        rms_o = place("rms_o", [P, HEADS, S], f32, 84)
        tmpo = place("tmpo", [P, KT, S], f32, 132)
        x1T = place("x1T", [P, KT, S], f32, 132)
        h2T = place("h2T", [P, KT, S], f32, 148)
        q2T = place("q2T", [P, 2 * PH, S], f32, 68)
        s_all = place("s_all", [P, TB, 2 * PH, NKEYS], f32, 12)
        oh_eq = place("oh_eq", [P, 2, 2, BT, P], f32r, 60)
        gstage = place("gstage", [P, 2, ET, GC], f32, 44)
        ohI_hi = place("ohI_hi", [P, 2, BT, P], f32r, 76)
        ohI_lo = place("ohI_lo", [P, 2, BT, P], f32r, 84)
        s_cur = place("s_cur", [P, 2 * PH, NKEYS], f32, 132)
        s_left = place("s_left", [P, 2 * PH, NKEYS], f32, 140)
        cand_left = place("cand_left", [P, PH, TOPK * TOPK], f32, 140)
        onehot = place("onehot", [P, PH, TOPK, TOPK], f32, 140)
        dot_junk = place("dot_junk", [P, D], f32, 140)
        cand = place("cand", [P, PH, TOPK, TOPK], f32, 148)
        draw = place("draw", [P, DR, D], f32, 156)
        dhi = place("dhi", [P, DR, KT, P], f32r, 168)
        dlo = [place(f"dlo{n}", [P, KT, P], f32r, kb) for n, kb in enumerate((92, 96, 185))]
        d_ring = [place(f"d_ring{n}", [P, D], f32, kb) for n, kb in enumerate((12, 16, 144, 148, 152))]
        x1stage = place("x1stage", [P, TB, D], f32, 164)
        uraw = place("uraw", [P, 4, D], f32, 20)
        uhi = place("uhi", [P, 4, D], f32r, 44)
        ulo = place("ulo", [P, 4, D], f32r, 60)
        gein = place("gein", [P, 4, DT], f32, 76)
        wf = place("wf", [P, 2, DT], f32, 82)
        w_hi = place("w_hi", [P, 4, DT], f32r, 85)
        w_lo = place("w_lo", [P, 4, DT], f32r, 91)
        gtile = place("gtile", [P, 2, DT // GC, GG * GC], f32, 100)
        zeros = place("zeros", [P, S], f32r, 124)
        gain_row = place("gain_row", [P, D], f32, 128)
        u_ring = place("u_ring", [P, 8, D], f32, 148)
        yrow = place("yrow", [P, TB, D], f32, 132)
        x1tok = place("x1tok", [P, TB, D], f32, 164)
        bias_row = place("bias_row", [P, D], f32, 197)
        at = [181.0]

        def scratch(name, shape, dt=f32):
            t = place(name, shape, dt, at[0])
            at[0] += ((int(np.prod(shape[1:])) * 4 + 63) // 64) * 64 / 1024
            assert at[0] <= 207, at
            return t

        h2row = scratch("h2row", [P, D])
        gate_row = scratch("gate_row", [P, D])
        idx3 = scratch("idx3", [P, P + UN], i32)
        assert 3 * ROWS <= P + UN
        share3 = scratch("share3", [P, P])
        picked = scratch("picked", [P, 3, P])
        ijT = scratch("ijT", [P, 2, P])
        gT_hi = scratch("gT_hi", [P, P], f32r)
        gT_lo = scratch("gT_lo", [P, P], f32r)
        ge = scratch("ge", [P, 2, DT])
        assert at[0] <= 197, at
        at = [197.0]
        top_v = scratch("top_v", [P, PH, 2, TOPK])
        top_i = scratch("top_i", [P, PH, 2, TOPK], u32)
        top_f = scratch("top_f", [P, PH, 2, TOPK])
        best = scratch("best", [P, PH, TOPK])
        best_at = scratch("best_at", [P, PH, TOPK], u32)
        best_ab = scratch("best_ab", [P, 2, PH, TOPK], u32)
        best_f = scratch("best_f", [P, 2, PH, TOPK])
        logit = scratch("logit", [P, PH, TOPK])
        expo = scratch("expo", [P, PH, TOPK])
        expsum = scratch("expsum", [P, PH])
        at = [204.5]
        pre3 = scratch("pre3", [P, 3 * ROWS])
        pre_s = scratch("pre_s", [P, ROWS])
        idxd = scratch("idxd", [P, ROWS], i32)
        gel3 = scratch("gel3", [P, P])
        wexp = scratch("wexp", [P, P])
        accum = place("accum", [P, D], f32, 197)
        junk = place("junk", [P, D], f32, 201)
        idxc = small("idxc", [P, UN], i32)
        wexp_s = small("wexp_s", [P, UN])
        fin_ss = small("fin_ss", [P, 3, TB])

        bank = ctx.enter_context(nc.psum_tensor("bank", [P, 8, S], f32))

        const_in = sem("const_in")
        pos_in = sem("pos_in")
        xT_in = sem("xT_in")
        xR_in = sem("xR_in")
        row_in = sem("row_in")
        raw_in = [sem(f"raw_in{n}") for n in range(RAW_SLOTS)]
        raw_free = sem("raw_free")
        hi_ready = sem("hi_ready")
        lo_ready = sem("lo_ready")
        tile_ready = sem("tile_ready")
        act_emptied = sem("act_emptied")
        dve_emptied = sem("dve_emptied")
        cact_ready = sem("cact_ready")
        ones_ready = sem("ones_ready")
        ada_acc = sem("ada_acc")
        ada_col = sem("ada_col")
        ada_done = sem("ada_done")
        sq_ready = sem("sq_ready")
        mean_ready = sem("mean_ready")
        root_ready = sem("root_ready")
        root_used = sem("root_used")
        part_ready = sem("part_ready")
        ahi_ready = sem("ahi_ready")
        alo_ready = sem("alo_ready")
        sin_arg = sem("sin_arg")
        sin_done = sem("sin_done")
        lam_arg = sem("lam_arg")
        lam_exp = sem("lam_exp")
        rot_ready = sem("rot_ready")
        rot_used = sem("rot_used")
        sc_ready = sem("sc_ready")
        max_ready = sem("max_ready")
        prob_ready = sem("prob_ready")
        comb_ready = sem("comb_ready")
        tr_ready = sem("tr_ready")
        trs_ready = sem("trs_ready")
        pv_ready = sem("pv_ready")
        meano_out = sem("meano_out")
        o_ready = sem("o_ready")
        x1sq_ready = sem("x1sq_ready")
        h2_ready = sem("h2_ready")
        pads = sem("pads")
        x1_stored = sem("x1_stored")
        gate_stored = sem("gate_stored")
        cur_ready = sem("cur_ready")
        logit_ready = sem("logit_ready")
        exp_done = sem("exp_done")
        picked_ready = sem("picked_ready")
        pickT_ready = sem("pickT_ready")
        pickTs_ready = sem("pickTs_ready")
        eq_ready = sem("eq_ready")
        ohhi_ready = sem("ohhi_ready")
        ohlo_ready = sem("ohlo_ready")
        gmm = sem("gmm")
        gbank_free = sem("gbank_free")
        g_stored = [sem(f"g_stored{n}") for n in range(2)]
        idx_ready = sem("idx_ready")
        draw_in = [sem(f"draw_in{n}") for n in range(DR)]
        uraw_in = [sem(f"uraw_in{n}") for n in range(4)]
        dhi_ready = sem("dhi_ready")
        dlo_ready = sem("dlo_ready")
        pre_done = sem("pre_done")
        ge_ready = sem("ge_ready")
        ge_stored = [sem(f"ge_stored{n}") for n in range(2)]
        ge_in = [sem(f"ge_in{n}") for n in range(4)]
        uhi_ready = sem("uhi_ready")
        ulo_ready = sem("ulo_ready")
        g_in = [sem(f"g_in{n}") for n in range(2)]
        g_free = sem("g_free")
        up_done = sem("up_done")
        wf_ready = sem("wf_ready")
        whi_ready = sem("whi_ready")
        wlo_ready = sem("wlo_ready")
        zeros_ready = sem("zeros_ready")
        psum_done = sem("psum_done")
        idxd_ready = sem("idxd_ready")
        idxc_ready = sem("idxc_ready")
        pool_step = sem("pool_step")
        dve_step = sem("dve_step")
        d_in = [sem(f"d_in{n}") for n in range(DROWS)]
        u_in = [sem(f"u_in{n}") for n in range(8)]
        dot_done = sem("dot_done")
        sum_done = sem("sum_done")
        pre3_ready = sem("pre3_ready")
        gel3_ready = sem("gel3_ready")
        rows_free = sem("rows_free")
        x1b_in = sem("x1b_in")
        y_ready = sem("y_ready")
        ss_ready = sem("ss_ready")
        out_ready = sem("out_ready")
        out_stored = sem("out_stored")

        block = ctx.enter_context(nc.Block())

        def wait_emptied(eng, kind, index):
            who, n = emptied(kind, index)
            eng.wait_ge(act_emptied if who == "act" else dve_emptied, n)

        def raw_arrived(eng, n):
            eng.wait_ge(raw_in[n % RAW_SLOTS], 16 * (n // RAW_SLOTS + 1))

        def raw_w(n):
            return raw[:, AT["w", n] % RAW_SLOTS, :].rearrange("p (k n) -> p k n", k=KT)

        N_OP = dict(norm1=0, pooled=8, ya=16, o=24, merged=32, norm2=40)
        N_MEAN = dict(norm1=0, o=1, norm2=1 + HEADS)
        UNITS = [(h, qb) for h in range(HEADS) for qb in range(TB)]

        @block.sync
        def _(sp):
            sp.dma_start(cst[:, :], consts).then_inc(const_in, 16)
            sp.dma_start(chan[:, :], chans).then_inc(const_in, 16)
            sp.dma_start(xT[:, :, :], xT_d).then_inc(xT_in, 16)
            for n, item in enumerate(STREAM):
                if n >= RAW_SLOTS:
                    sp.wait_ge(raw_free, n - RAW_SLOTS + 1)
                if item[0] == "ada":
                    src = ada_d[item[1], item[2]]
                else:
                    src = wdram[CHUNKS[item[1]][0]][CHUNKS[item[1]][1]]
                sp.dma_start(raw[:, n % RAW_SLOTS, :], src).then_inc(raw_in[n % RAW_SLOTS], 16)
                if n == 2:
                    sp.dma_start(pos_i[:, :], pos_d).then_inc(pos_in, 16)
                    sp.dma_start(subk[:, :, :], subk_d).then_inc(pos_in, 16)
                    sp.dma_start(lam_w[:, :, :], rows[:, 2 * D:2 * D + 4 * HD]).then_inc(pos_in, 16)
                if item == ("w", FIRST["query"]):
                    sp.wait_ge(ada_done, 6)
                    sp.dma_start(bias_row[:, :], rows[:, D:2 * D]).then_inc(row_in, 16)
                if item == ("w", FIRST["query"] + 5):
                    wait_emptied(sp, "x1tok", 7)
                    sp.dma_start(x1d, x1stage[:, :, :]).then_inc(x1_stored, 16)
                if item == ("w", FIRST["branchA"] + 1):
                    sp.wait_ge(part_ready, 24)
                    sp.dma_start(xR[:, :, :], xT_d).then_inc(xR_in, 16)
            wait_emptied(sp, "gaterow", 1)
            sp.dma_start(gated, gate_row[:, :]).then_inc(gate_stored, 16)
            sp.wait_ge(x1_stored, 16)

            def load_down(i, j):
                sp.wait_ge(dlo_ready, i + 1)
                sp.dma_start(draw[:, (j + 1) % DR, :], downT[bass.ds(i, 1)].rearrange("a p n -> (a p) n"))\
                  .then_inc(draw_in[(j + 1) % DR], 16)

            for i in range(DN0):
                load_down(i, i)
            with sp.Fori(0, DTB) as tb:
                for j in range(DN):
                    load_down(tb * DN + DN0 + j, DN0 + j)
            for n in range(DR):
                sp.wait_ge(dlo_ready, ET + n + 1)
                slot = (ET + n + 1) % DR
                sp.dma_start(draw[:, slot, :], downT[n]).then_inc(draw_in[slot], 16)

            def load_up(i, slot):
                sp.wait_ge(ulo_ready, i + 1)
                sp.dma_start(uraw[:, slot, :], up[bass.ds(i * P, P), :]).then_inc(uraw_in[slot], 16)

            sp.wait_ge(cur_ready, 1 + DTB)
            for n in range(4):
                load_up(n, n)
            for n in range(2):
                sp.wait_ge(ge_stored[n], 16 * ET // 2)
                sp.wait_ge(g_stored[n], 16 + 16 * DT // GC // 2)
            sp.wait_ge(gmm, 2 + DTB * P // BT)
            sp.wait_ge(pre_done, ET)

            def load_gelu(i, e, it):
                if e % GG == 0:
                    g = e // GG
                    sp.wait_ge(g_free, 2 * it + g + 1)
                    sp.dma_start(gtile[:, g % 2], gmat[:, :, bass.ds(i, GG), :]
                                 .rearrange("c p i t -> p c (i t)")).then_inc(g_in[g % 2], 16)
                sp.wait_ge(wf_ready, i + 1)
                sp.dma_start(gein[:, e % 4, :], ged[bass.ds(i, 1)].rearrange("a p n -> (a p) n"))\
                  .then_inc(ge_in[e % 4], 16)

            turns = ET // UN
            for e in range(4):
                load_gelu(e, e, 0)
            with sp.Fori(0, turns - 1) as it:
                for e in range(4, UN + 4):
                    load_gelu(it * UN + e, e, it)
                    load_up(it * UN + e, e % 4)
            for e in range(4, UN):
                i = (turns - 1) * UN + e
                load_gelu(i, e, turns - 1)
                load_up(i, e % 4)
            for n in range(2):
                sp.wait_ge(ulo_ready, ET + n + 1)
                sp.dma_start(uraw[:, n, :], up[0:P, :]).then_inc(uraw_in[n], 16)
            sp.dma_start(gain_row[:, :], rows[:, 0:D]).then_inc(x1b_in, 16)
            sp.wait_ge(sum_done, 8 + P)
            sp.dma_start(x1tok[:, :, :], x1d).then_inc(x1b_in, 16)
            sp.dma_start(gate_row[:, :], gated).then_inc(x1b_in, 16)
            for tb in range(TB):
                sp.wait_ge(out_ready, tb + 1)
                sp.dma_start(out[tb], yrow[:, tb, :]).then_inc(out_stored, 16)
            sp.wait_ge(uraw_in[1], 16 * (ET // 4 + 1))
            sp.wait_ge(out_stored, 16 * TB)

        @block.tensor
        def _(pe):
            def mm3(dst, lhi, llo, rhi, rlo, first, last):
                pe.matmul(dst, lhi, rhi, start=first, stop=False)
                pe.matmul(dst, lhi, rlo, start=False, stop=False)
                return pe.matmul(dst, llo, rhi, start=False, stop=last)

            def free_bank(t):
                if t >= 4:
                    wait_emptied(pe, *TILES[t - 4][:2])

            def mean(rhs, b=6):
                for k in range(len(rhs)):
                    last = pe.matmul(bank[:, b, :], ones[:, :], rhs[k], start=(k == 0),
                                     stop=(k == len(rhs) - 1))
                last.then_inc(mean_ready, 1)

            def ada_columns(j):
                pe.wait_ge(ada_acc, j + 1)
                if j:
                    pe.wait_ge(ada_done, j)
                for m in range(KT):
                    last = pe.matmul(bank[:, 7, m:m + 1], acc_ada[:, j % 2, m * P:(m + 1) * P],
                                     ones[:, 0:1], start=True, stop=True)
                last.then_inc(ada_col, 1)

            def rotate(n):
                pe.wait_ge(act_emptied, emptied("q", 0)[1] + n)
                if n >= 2:
                    pe.wait_ge(rot_used, n - 1)
                pe.matmul(bank[:, 4 + n % 2, :], rotm, q_raw[:, n % 2, :], start=True, stop=True)\
                  .then_inc(rot_ready, 1)

            pe.wait_ge(const_in, 32)
            pe.wait_ge(ones_ready, 1)
            pe.wait_ge(sq_ready, 8)
            mean([sq1[:, k, :] for k in range(KT)])
            ada_columns(0)
            ada_columns(1)

            ada_before = {}
            for item, n in AT.items():
                if item[0] == "ada" and item[1] >= 2 and item[2] == 3:
                    ada_before[STREAM[n - 1][1]] = item[1]

            def attention():
                def scores(u):
                    h, qb = UNITS[u]
                    par, n = u % 2, (qb + 1) * P
                    if u >= 2:
                        pe.wait_ge(prob_ready, 2 * (u - 1))
                    else:
                        wait_emptied(pe, "v", 4 * TB - 1)
                    for c in range(2):
                        last = pe.matmul(bank[:, 2 * par + c, 0:n],
                                         qT[c * HD:(c + 1) * HD, h, qb * P:(qb + 1) * P],
                                         kT[c * HD:(c + 1) * HD, h, 0:n], start=True, stop=True)
                    last.then_inc(sc_ready, 1)

                def values(u):
                    h, qb = UNITS[u]
                    pe.wait_ge(trs_ready, u + 1)
                    if qb == 0 and h >= 2:
                        pe.wait_ge(meano_out, h - 1)
                    for kb in range(qb + 1):
                        last = pe.matmul(bank[:, 6 + h % 2, qb * P:(qb + 1) * P],
                                         v_t[:, kb, h * P:(h + 1) * P],
                                         combT[:, u % 2, kb * P:(kb + 1) * P],
                                         start=(kb == 0), stop=(kb == qb))
                    last.then_inc(pv_ready, 1)

                def head_mean(h):
                    pe.wait_ge(sq_ready, 8 + h + 1)
                    pe.wait_ge(o_ready, h + 1)
                    mean([sqo[:, :]], 6 + h % 2)

                pe.wait_ge(rot_used, 2 * HEADS)
                scores(0)
                scores(1)
                for u, (h, qb) in enumerate(UNITS):
                    if u + 2 < len(UNITS):
                        scores(u + 2)
                    pe.wait_ge(comb_ready, u + 1)
                    if u >= 2:
                        pe.wait_ge(trs_ready, u - 1)
                    for kb in range(qb + 1):
                        last = pe.transpose(bank[:, 4 + u % 2, kb * P:(kb + 1) * P],
                                            comb[:, u % 2, kb * P:(kb + 1) * P], ident)
                    last.then_inc(tr_ready, 1)
                    if u:
                        values(u - 1)
                    if qb == 1 and h:
                        head_mean(h - 1)
                values(len(UNITS) - 1)
                head_mean(HEADS - 1)

            def norm2_mean():
                pe.wait_ge(x1sq_ready, 1)
                mean([sq2[:, 0, :]])

            def tokens_first(t, src, numbers):
                for n in numbers:
                    tb, half = n // 2, n % 2
                    free_bank(t)
                    for j in range(4):
                        last = pe.transpose(bank[:, t % 4, j * P:(j + 1) * P],
                                            src[:, 4 * half + j, tb * P:(tb + 1) * P], ident)
                    last.then_inc(tile_ready, 1)
                    t += 1
                return t

            t = 0
            for n, (stage, c) in enumerate(CHUNKS):
                if n in ada_before:
                    ada_columns(ada_before[n])
                if stage == "branchA" and c == 0:
                    attention()
                if stage == "query" and c == 0:
                    norm2_mean()
                    t = tokens_first(t, x1T, range(8))
                if c == 0:
                    ready = {"xp": "norm1", "pool": "pooled", "branchP": "ya", "branchA": "o",
                             "out": "merged", "query": "norm2"}.get(stage)
                    if ready:
                        pe.wait_ge(alo_ready, N_OP[ready] + 8)
                pe.wait_ge(hi_ready, n + 1)
                pe.wait_ge(lo_ready, n + 1)
                wh, wl = whi[:, n % 2], wlo[:, n % 2]
                ah, al = {"pool": (r1_hi, r1_lo), "branchP": (ya_hi, ya_lo), "branchA": (r1_hi, r1_lo),
                          "query": (r1_hi, r1_lo)}.get(stage, (hT_hi, hT_lo))
                if stage == "pool":
                    for g in range(4):
                        for m in range(2):
                            free_bank(t)
                            for k in range(2):
                                kk = 2 * g + k
                                last = mm3(bank[:, t % 4, :], wh[:, kk, m * P:(m + 1) * P],
                                           wl[:, kk, m * P:(m + 1) * P], ah[:, kk, :], al[:, kk, :],
                                           k == 0, k == 1)
                            last.then_inc(tile_ready, 1)
                            t += 1
                elif stage == "v":
                    for tb in range(TB):
                        free_bank(t)
                        for k in range(KT):
                            last = mm3(bank[:, t % 4, 0:CH], ah[:, k, tb * P:(tb + 1) * P],
                                       al[:, k, tb * P:(tb + 1) * P], wh[:, k, :], wl[:, k, :],
                                       k == 0, k == KT - 1)
                        last.then_inc(tile_ready, 1)
                        t += 1
                else:
                    for m in range(2):
                        free_bank(t)
                        for k in range(KT):
                            last = mm3(bank[:, t % 4, :], wh[:, k, m * P:(m + 1) * P],
                                       wl[:, k, m * P:(m + 1) * P], ah[:, k, :], al[:, k, :],
                                       k == 0, k == KT - 1)
                        last.then_inc(tile_ready, 1)
                        t += 1
                if stage in ("q", "k") or (stage == "v" and c == 0):
                    done = 2 * (n - FIRST["q"])
                    for r in range(max(0, done - 2), done):
                        rotate(r)
            pe.wait_ge(h2_ready, 8)
            t = tokens_first(t, h2T, [6, 7])
            for n in range(2):
                free_bank(t)
                pe.matmul(bank[:, t % 4, :], ones[:, :], acc_ada[:, 1, n * S:(n + 1) * S],
                          start=True, stop=True).then_inc(tile_ready, 1)
                t += 1
            for n in range(16):
                tb, g = n // 4, n % 4
                free_bank(t)
                if n == 0:
                    pe.wait_ge(pos_in, 48)
                    wait_emptied(pe, "query", 15)
                for j in range(4):
                    hp = 4 * g + j
                    last = pe.matmul(bank[:, t % 4, j * P:(j + 1) * P], q2T[:, hp, tb * P:(tb + 1) * P],
                                     subk[:, hp % 2, :], start=True, stop=True)
                last.then_inc(tile_ready, 1)
                t += 1
            wait_emptied(pe, "score", 15)
            wait_emptied(pe, "gaterow", 1)
            pe.sem_inc(gmm, 2)

            def down_products(i, j):
                pe.wait_ge(ge_ready, i + 1)
                pe.wait_ge(dlo_ready, i + DR + 1)
                slot = (j + 1) % DR
                for k in range(KT):
                    last = mm3(bank[:, 6 + j % 2, 0:DT], dhi[:, slot, k, :], dlo[slot][:, k, :],
                               r1_hi[:, k, 0:DT], r1_lo[:, k, 0:DT], k == 0, k == KT - 1)
                last.then_inc(pre_done, 1)

            for i in range(DN0):
                down_products(i, i)
            with pe.Fori(0, DTB) as tb:
                for j in range(DNA):
                    down_products(tb * DN + DN0 + j, DN0 + j)
                pe.wait_ge(picked_ready, tb + 1)
                for n in range(3):
                    last = pe.transpose(bank[:, 4, n * P:(n + 1) * P], picked[:, n, :], ident)
                last.then_inc(pickT_ready, 1)
                for b in range(P // BT):
                    par = b % 2
                    pe.wait_ge(ohhi_ready, tb * (P // BT) + b + 1)
                    pe.wait_ge(ohlo_ready, tb * (P // BT) + b + 1)
                    pe.wait_ge(gbank_free, tb * (P // BT) + b + 1)
                    for n in range(BT):
                        dst = bank[:, 2 * par + n // 4, (n % 4) * P:(n % 4 + 1) * P]
                        pe.matmul(dst, oh_eq[:, par, 1, n, :], ohI_hi[:, par, n, :], start=True, stop=False)
                        last = pe.matmul(dst, oh_eq[:, par, 1, n, :], ohI_lo[:, par, n, :],
                                         start=False, stop=True)
                    last.then_inc(gmm, 1)
                    for j in after_batch(b):
                        down_products(tb * DN + DN0 + j, DN0 + j)
            pe.wait_ge(gbank_free, 2 + DTB * P // BT)
            pe.wait_ge(zeros_ready, 1)
            for b in range(2 * DTB):
                pe.matmul(bank[:, b, :], zeros[:, 0:P], zeros[:, :], start=True, stop=False)
            pe.sem_inc(up_done, 2)
            with pe.Fori(0, ET // UN) as it:
                for e in range(UN):
                    i, slot = it * UN + e, e % 4
                    pe.wait_ge(wlo_ready, i + 1)
                    pe.wait_ge(ulo_ready, i + 5)
                    for tb in range(DTB):
                        lh, ll = (x[:, slot, tb * P:(tb + 1) * P] for x in (w_hi, w_lo))
                        for half in range(2):
                            rh, rl = (x[:, slot, half * S:(half + 1) * S] for x in (uhi, ulo))
                            last = mm3(bank[:, 2 * tb + half, :], lh, ll, rh, rl, False, False)
                    last.then_inc(up_done, 1)
            for b in range(2 * DTB):
                last = pe.matmul(bank[:, b, :], zeros[:, 0:P], zeros[:, :], start=False, stop=True)
            last.then_inc(psum_done, 1)

        def w_done(eng, n):
            stage, c = CHUNKS[n]
            last = {"pool": 7, "v": c * TB + TB - 1}.get(stage, 2 * c + 1)
            eng.wait_ge(tile_ready, TILE_AT[stage, last] + 1)

        @block.scalar
        def _(act):
            def whi_make(n):
                if n >= len(CHUNKS):
                    return
                raw_arrived(act, AT["w", n])
                if n >= 2:
                    w_done(act, n - 2)
                act.activation(whi[:, n % 2], raw_w(n), ACT.Copy).then_inc(hi_ready, 1)

            def tile(kind, i):
                t = TILE_AT[kind, i]
                act.wait_ge(tile_ready, t + 1)
                return bank[:, t % 4, :]

            def root(n, scale):
                act.wait_ge(mean_ready, n + 1)
                if n:
                    act.wait_ge(root_used, 1)
                act.activation(rms1[:, :], bank[:, 6, :], ACT.Sqrt, bias=eps_t[:, :], scale=scale)\
                   .then_inc(root_ready, 1)

            act.wait_ge(const_in, 32)
            act.activation(cact[:, :], chan[:, K_C:K_C + KT], ACT.Silu).then_inc(cact_ready, 1)
            act.wait_ge(xT_in, 16)
            for k in range(KT):
                act.activation(sq1[:, k, :], xT[:, k, :], ACT.Square).then_inc(sq_ready, 1)
            act.wait_ge(ones_ready, 1)
            root(0, 1.0 / D)
            whi_make(0)
            for k in range(KT):
                act.wait_ge(part_ready, k + 1)
                act.activation(hT_hi[:, k, :], tmp1[:, k, :], ACT.Identity, bias=modc[:, k:k + 1])\
                   .then_inc(ahi_ready, 1)
            for n in range(2):
                act.wait_ge(sin_arg, n + 1)
                act.activation((rope_sin, rope_cos)[n][:, :], rope_w[:, 2 + n, :], ACT.Sin)\
                   .then_inc(sin_done, 1)
            act.wait_ge(lam_arg, 1)
            act.activation(lamt[:, 2:4], lamt[:, 0:2], ACT.Exp).then_inc(lam_exp, 1)

            def attention():
                def exps(u):
                    h, qb = UNITS[u]
                    par, n = u % 2, (qb + 1) * P
                    act.wait_ge(max_ready, u + 1)
                    if u >= 2:
                        act.wait_ge(comb_ready, u - 1)
                    for c in range(2):
                        act.activation(prob[:, par, c, 0:n], bank[:, 2 * par + c, 0:n], ACT.Exp,
                                       bias=att_bias[:, par, c:c + 1], scale=HD ** -0.5,
                                       accum_out=att_sum[:, par, c:c + 1]).then_inc(prob_ready, 1)

                def head_out(h):
                    act.wait_ge(pv_ready, TB * (h + 1))
                    act.wait_ge(mean_ready, N_MEAN["o"] + h)
                    act.activation(sqo[:, :], bank[:, 6 + h % 2, :], ACT.Square).then_inc(sq_ready, 1)
                    act.activation(oT[:, h, :], bank[:, 6 + h % 2, :], ACT.Copy).then_inc(o_ready, 1)

                def mean_out(h):
                    act.wait_ge(mean_ready, N_MEAN["o"] + h + 1)
                    act.activation(rms_o[:, (h + 1) % HEADS, :], bank[:, 6 + h % 2, :], ACT.Copy).then_inc(meano_out, 1)

                exps(0)
                exps(1)
                for u, (h, qb) in enumerate(UNITS):
                    act.wait_ge(tr_ready, u + 1)
                    if u >= 2:
                        act.wait_ge(pv_ready, u - 1)
                    act.activation(combT[:, u % 2, 0:(qb + 1) * P], bank[:, 4 + u % 2, 0:(qb + 1) * P],
                                   ACT.Copy).then_inc(trs_ready, 1)
                    if qb == 0 and h:
                        head_out(h - 1)
                    if qb == 2 and h:
                        mean_out(h - 1)
                    if u + 2 < len(UNITS):
                        exps(u + 2)
                head_out(HEADS - 1)
                mean_out(HEADS - 1)
                act.drain()
                for h in range(HEADS):
                    act.activation(rms_o[:, (h + 1) % HEADS, :], rms_o[:, (h + 1) % HEADS, :], ACT.Sqrt, bias=eps_t[:, :], scale=1.0 / P)\
                       .then_inc(root_ready, 1)
                    if h:
                        split_o(h - 1)
                split_o(HEADS - 1)

            def split_o(h):
                act.wait_ge(part_ready, 16 + h + 1)
                act.activation(r1_hi[:, h, :], tmpo[:, h, :], ACT.Copy).then_inc(ahi_ready, 1)

            for n, (stage, c) in enumerate(CHUNKS):
                whi_make(n + 1)
                if stage == "branchA" and c == 0:
                    attention()
                if stage == "xp":
                    if c == 0:
                        act.wait_ge(pads, 1)
                    for m in range(2):
                        act.activation(xpT[:, 2 * c + m, PADW:], tile(stage, 2 * c + m), ACT.Copy)\
                           .then_inc(act_emptied, 1)
                elif stage in ("gateA", "gateB"):
                    dst, col = (mergedP, 0) if stage == "gateA" else (sigB, KT)
                    for m in range(2):
                        i = 2 * c + m
                        act.activation(dst[:, i, :], tile(stage, i), ACT.Sigmoid,
                                       bias=chan[:, K_BGATE + col + i:K_BGATE + col + i + 1])\
                           .then_inc(act_emptied, 1)
                        if stage == "gateA":
                            act.wait_ge(part_ready, 8 + i + 1)
                            act.activation(r1_hi[:, i, :], pool_y[:, i % 2, :], ACT.Copy)\
                               .then_inc(ahi_ready, 1)
                elif stage == "pool":
                    for i in range(8):
                        src = tile(stage, i)
                        act.activation(ya_hi[:, i, :], src, ACT.Identity, bias=0.0,
                                       scale=chan[:, K_PSCALE + i:K_PSCALE + i + 1]).then_inc(ahi_ready, 1)
                elif stage in ("q", "k"):
                    for m in range(2):
                        i = 2 * c + m + (HEADS if stage == "k" else 0)
                        src = tile(stage, 2 * c + m)
                        if i >= 2:
                            act.wait_ge(rot_used, i - 1)
                        act.activation(q_raw[:, i % 2, :], src, ACT.Copy).then_inc(act_emptied, 1)
                elif stage == "v":
                    for tb in range(TB):
                        act.activation(v_t[:, tb, c * CH:(c + 1) * CH], tile(stage, c * TB + tb)[:, 0:CH],
                                       ACT.Copy).then_inc(act_emptied, 1)
                elif stage == "branchA":
                    for m in range(2):
                        i = 2 * c + m
                        act.wait_ge(part_ready, 24 + i + 1)
                        act.activation(hT_hi[:, i, :], tmpo[:, i, :], ACT.Copy).then_inc(ahi_ready, 1)
                elif stage == "out":
                    if c == 3:
                        root(N_MEAN["norm2"], 1.0 / D)
                        for k in range(8):
                            act.activation(x1stage[:, k // 2, (k % 2) * S:(k % 2 + 1) * S],
                                           tile("x1tok", k), ACT.Copy).then_inc(act_emptied, 1)
                        for k in range(KT):
                            act.wait_ge(part_ready, 32 + k + 1)
                            act.activation(r1_hi[:, k, :], h2T[:, k, :], ACT.Identity,
                                           bias=modc[:, 24 + k:25 + k]).then_inc(ahi_ready, 1)
                elif stage == "query":
                    for m in range(2):
                        act.activation(q2T[:, 2 * c + m, :], tile(stage, 2 * c + m), ACT.Copy)\
                           .then_inc(act_emptied, 1)
            for n in range(16):
                tb, g = n // 4, n % 4
                act.activation(s_all[:, tb, 4 * g:4 * g + 4, :].rearrange("p a b -> p (a b)"),
                               tile("score", n), ACT.Copy).then_inc(act_emptied, 1)
            act.sem_inc(gbank_free, 2)
            wait_emptied(act, "gaterow", 1)

            def stage_scores(src):
                act.activation(s_cur[:, :, :].rearrange("p a b -> p (a b)"), src, ACT.Copy)\
                   .then_inc(cur_ready, 1)

            def exponentials(n):
                act.wait_ge(logit_ready, n + 1)
                act.activation(expo[:, :, :], logit[:, :, :], ACT.Exp).then_inc(exp_done, 1)

            for n in range(2):
                act.sem_inc(g_stored[n], 16)
            act.sem_inc(ge_ready, 2)

            def down_hi(j, tb=None):
                slot, use = (j + 1) % DR, (j + DR) // DR if (j + 1) % DR else (j + 1) // DR
                act.wait_ge(draw_in[slot], 16 * use if tb is None else tb * (16 * DN // DR) + 16 * use)
                act.activation(dhi[:, slot].rearrange("p a b -> p (a b)"), draw[:, slot, :], ACT.Copy)\
                   .then_inc(dhi_ready, 1)

            def down_tile(i, j, tb=None):
                act.wait_ge(pre_done, i + 1)
                if j >= 2:
                    act.wait_ge(ge_stored[j % 2], 16 * (j // 2) if tb is None
                                else tb * (16 * DN // 2) + 16 * (j // 2))
                act.activation(ge[:, j % 2, :], bank[:, 6 + j % 2, 0:DT], ACT.Gelu)\
                   .then_inc(ge_ready, 1)
                down_hi(j + DR, tb)
                act.drain()
                act.dma_start(ged[bass.ds(i, 1)].rearrange("a p n -> (a p) n"), ge[:, j % 2, :])\
                   .then_inc(ge_stored[j % 2], 16)

            act.drain()
            for j in range(DR):
                down_hi(j)
            stage_scores(s_all[:, DTB].rearrange("p a b -> p (a b)"))
            for j in range(DN0):
                if j == EXP_AT:
                    exponentials(0)
                    stage_scores(s_all[:, 0].rearrange("p a b -> p (a b)"))
                down_tile(j, j)
            with act.Fori(0, DTB) as tb:
                for j in range(DNA):
                    if j == EXPB_AT:
                        exponentials(tb + 1)
                    down_tile(tb * DN + DN0 + j, DN0 + j, tb)
                act.wait_ge(pickT_ready, tb + 1)
                act.activation(ijT[:, :, :].rearrange("p a b -> p (a b)"), bank[:, 4, 0:2 * P], ACT.Copy)
                act.activation(gT_hi[:, :], bank[:, 4, 2 * P:3 * P], ACT.Copy).then_inc(pickTs_ready, 1)

                def onehot_lo(b):
                    act.wait_ge(eq_ready, tb * (P // BT) + b + 1)
                    for n in range(BT):
                        t0 = b * BT + n
                        last = act.activation(ohI_lo[:, b % 2, n, :], oh_eq[:, b % 2, 0, n, :].bitcast(f32),
                                              ACT.Copy, scale=gT_lo[:, t0:t0 + 1].bitcast(f32))
                    last.then_inc(ohlo_ready, 1)

                onehot_lo(0)
                for b in range(P // BT):
                    n, par, c = tb * (P // BT) + b, b % 2, b * BT // GC
                    if b * BT % GC == 0:
                        act.wait_ge(g_stored[c % 2], tb * (16 * P // GC // 2) + 16 * (c // 2 + 1))
                    act.wait_ge(gmm, n + 3)
                    for q in range(2):
                        t0 = b * BT % GC + 4 * q
                        last = act.activation(
                            gstage[:, c % 2, :, t0:t0 + 4].rearrange("p i t -> p t i"),
                            bank[:, 2 * par + q, :].rearrange("p (t i) -> p t i", t=4), ACT.Copy)
                    last.then_inc(gbank_free, 1)
                    if b + 1 < P // BT:
                        onehot_lo(b + 1)
                    if (b + 1) * BT % GC == 0:
                        act.drain()
                        act.dma_start(gmat[bass.ds(tb * (P // GC) + c, 1)].rearrange("a p i t -> (a p) i t"),
                                      gstage[:, c % 2]).then_inc(g_stored[c % 2], 16)
                    for j in after_batch(b):
                        down_tile(tb * DN + DN0 + j, DN0 + j, tb)
                    if b == NEXT_AT:
                        stage_scores(s_all[:, bass.ds(tb + 1, 1)].rearrange("p c a b -> p (c a b)"))

            def up_hi(count, slot):
                act.wait_ge(uraw_in[slot], count)
                act.activation(uhi[:, slot, :], uraw[:, slot, :], ACT.Copy).then_inc(uhi_ready, 1)

            act.wait_ge(pre3_ready, 1)
            act.activation(gel3[:, :], pre3[:, 0:P], ACT.Gelu).then_inc(gel3_ready, 1)
            act.wait_ge(g_stored[0], 16 + 16 * DT // GC // 2)
            up_hi(16, 0)
            up_hi(16, 1)
            act.wait_ge(g_stored[1], 16 + 16 * DT // GC // 2)
            with act.Fori(0, ET // UN) as it:
                for e in range(UN):
                    i = it * UN + e
                    act.wait_ge(wf_ready, i + 5)
                    act.activation(w_hi[:, e % 4, :], wf[:, e % 2, :], ACT.Copy).then_inc(whi_ready, 1)
                    act.wait_ge(up_done, i + 1)
                    up_hi(it * (16 * UN // 4) + 16 * ((e + 2) // 4 + 1), (e + 2) % 4)
            for tb in (3, 0, 1, 2):
                act.wait_ge(y_ready, (tb + 1) % TB + 1)
                act.activation(junk[:, :], yrow[:, tb, :], ACT.Square, accum_out=fin_ss[:, 0, tb:tb + 1])
                act.drain()
            act.activation(fin_ss[:, 1, :], fin_ss[:, 0, :], ACT.Sqrt, bias=eps_t[:, :], scale=1.0 / D)\
               .then_inc(ss_ready, 1)

        @block.vector
        def _(dve):
            def ada_chunk(j, r):
                n = AT["ada", j, r]
                raw_arrived(dve, n)
                if j >= 2 and r == 0:
                    dve.wait_ge(ada_col, j - 1)
                acc = acc_ada[:, j % 2, :]
                for k in range(2):
                    src = raw[:, n % RAW_SLOTS, k * D:(k + 1) * D]
                    col = cact[:, 2 * r + k:2 * r + k + 1]
                    if r == 0 and k == 0:
                        last = dve.tensor_scalar(acc, src, col, None, ALU.mult)
                    else:
                        last = dve.scalar_tensor_tensor(acc, src, col, acc, ALU.mult, ALU.add)
                    if k == 0:
                        dve.drain()
                last.then_inc(raw_free, 1)
                dve.drain()
                if r == 3:
                    dve.sem_inc(ada_acc, 1)

            def ada_finish(j):
                dve.wait_ge(ada_col, j + 1)
                dve.tensor_tensor(modc[:, j * KT:(j + 1) * KT], bank[:, 7, 0:KT],
                                  chan[:, K_BADA + j * KT:K_BADA + (j + 1) * KT], ALU.add)\
                   .then_inc(ada_done, 1)

            def wlo_make(n):
                if n >= len(CHUNKS):
                    return
                dve.wait_ge(hi_ready, n + 1)
                dve.tensor_tensor(wlo[:, n % 2], raw_w(n), whi[:, n % 2].bitcast(f32), ALU.subtract)\
                   .then_inc(lo_ready, 1)

            def follow(n):
                if n >= len(CHUNKS):
                    return
                wlo_make(n)
                dve.drain()
                dve.sem_inc(raw_free, 1)
                at_ = AT["w", n] + 1
                if at_ < len(STREAM) and STREAM[at_][0] == "ada":
                    _, j, r = STREAM[at_]
                    if r == 0 and j >= 3:
                        ada_finish(j - 1)
                    ada_chunk(j, r)
                    if j == 5 and r == 3:
                        ada_finish(5)

            def tile(kind, i):
                t = TILE_AT[kind, i]
                dve.wait_ge(tile_ready, t + 1)
                return bank[:, t % 4, :]

            def inverse_root(n, dst=rms1[:, :]):
                dve.wait_ge(root_ready, n + 1)
                dve.reciprocal(dst, dst)
                dve.drain()

            def lo_part(dst, src, hi, count, scalar=None, op=ALU.add):
                dve.wait_ge(ahi_ready, count)
                if scalar is None:
                    ins = dve.tensor_tensor(dst, src, hi.bitcast(f32), ALU.subtract)
                else:
                    ins = dve.scalar_tensor_tensor(dst, src, scalar, hi.bitcast(f32), op, ALU.subtract)
                return ins.then_inc(alo_ready, 1)

            dve.memset(ones[:, :], 1.0)
            dve.memset(eps_t[:, :], EPS)
            dve.drain()
            dve.sem_inc(ones_ready, 1)
            dve.wait_ge(cact_ready, 1)
            for j in range(2):
                for r in range(4):
                    ada_chunk(j, r)
            ada_finish(0)
            ada_finish(1)
            dve.drain()
            dve.scalar_tensor_tensor(scaleA[:, :], modc[:, KT:2 * KT], 1.0, chan[:, K_GMIX:K_GMIX + KT],
                                     ALU.add, ALU.mult)
            inverse_root(0)
            for k in range(KT):
                dve.scalar_tensor_tensor(tmp1[:, k, :], xT[:, k, :], scaleA[:, k:k + 1], rms1[:, :],
                                         ALU.mult, ALU.mult).then_inc(part_ready, 1)
            dve.sem_inc(root_used, 1)
            follow(0)
            for k in range(KT):
                lo_part(hT_lo[:, k, :], tmp1[:, k, :], hT_hi[:, k, :], k + 1, modc[:, k:k + 1])
            dve.drain()
            dve.memset(xpT[:, :, 0:PADW], 0.0)
            dve.memset(pool_w[:, :, 0:PADW], 0.0)
            dve.drain()
            dve.sem_inc(pads, 1)
            dve.wait_ge(pos_in, 48)
            ang, turns = rope_w[:, 0, :], rope_w[:, 1, :]
            dve.tensor_copy(turns, pos_i[:, :])
            dve.drain()
            dve.tensor_scalar(ang, turns, cst[:, C_FREQ:C_FREQ + 1], None, ALU.mult)
            dve.drain()
            for n, shift in ((0, 0.0), (1, 0.25)):
                arg = rope_w[:, 2 + n, :]
                dve.tensor_scalar(turns, ang, 1.0 / (2 * np.pi), shift, ALU.mult, ALU.add)
                dve.drain()
                dve.tensor_scalar(turns, turns, MAGIC, None, ALU.add)
                dve.drain()
                dve.tensor_scalar(turns, turns, -MAGIC, None, ALU.add)
                dve.drain()
                dve.scalar_tensor_tensor(arg, turns, -TWO_PI[0], ang, ALU.mult, ALU.add)
                for part in TWO_PI[1:]:
                    dve.drain()
                    dve.scalar_tensor_tensor(arg, turns, -part, arg, ALU.mult, ALU.add)
                dve.drain()
                if n:
                    dve.tensor_scalar(arg, arg, np.pi / 2, None, ALU.add)
                    dve.drain()
                dve.tensor_scalar(arg, arg, PI_BELOW, -PI_BELOW, ALU.min, ALU.max).then_inc(sin_arg, 1)
                dve.drain()
            for n in range(2):
                dve.tensor_tensor(lam_p[:, :], lam_w[:, 2 * n, :], lam_w[:, 2 * n + 1, :], ALU.mult)
                dve.drain()
                dve.tensor_reduce(lamt[:, n:n + 1], lam_p[:, :], AX.X, ALU.add)
                dve.drain()
            dve.sem_inc(lam_arg, 1)
            dve.wait_ge(lam_exp, 1)
            dve.tensor_tensor(neglam[:, :], lamt[:, 3:4], lamt[:, 2:3], ALU.subtract)
            dve.drain()
            dve.tensor_scalar(neglam[:, :], neglam[:, :], -LAM_INIT, None, ALU.add)

            def pooling(i):
                w = WINDOWS[i // 2]
                if i == 0:
                    wait_emptied(dve, "xp", 7)
                x = xpT[:, i, :]
                src, n = x, 1
                while n < w:
                    dst = pool_w[:, (n.bit_length() - 1) % 2, :]
                    dve.tensor_tensor(dst[:, PADW:], src[:, PADW:], src[:, PADW - n:PADW + S - n], ALU.add)
                    dve.drain()
                    src, n = dst, 2 * n
                y = pool_y[:, i % 2, :]
                if i >= 2:
                    dve.wait_ge(ahi_ready, 8 + i - 1)
                dve.scalar_tensor_tensor(y, src[:, PADW:], 1.0 / w, x[:, PADW:], ALU.mult, ALU.subtract)
                dve.tensor_tensor(pool_e[:, 0:w - 1], src[:, PADW:PADW + w - 1],
                                  cst[:, C_INV:C_INV + w - 1], ALU.mult)
                dve.drain()
                dve.tensor_tensor(y[:, 0:w - 1], pool_e[:, 0:w - 1], x[:, PADW:PADW + w - 1], ALU.subtract)\
                   .then_inc(part_ready, 1)
                dve.drain()
                lo_part(r1_lo[:, i, :], y, r1_hi[:, i, :], 8 + i + 1)

            def attention():
                def maxima(u):
                    h, qb = UNITS[u]
                    par, n = u % 2, (qb + 1) * P
                    dve.wait_ge(sc_ready, u + 1)
                    sc = bank[:, 2 * par:2 * par + 2, 0:n]
                    dve.tensor_tensor(sc[:, :, qb * P:n], sc[:, :, qb * P:n],
                                      mask.unsqueeze(1).broadcast_to([P, 2, P]), ALU.add)
                    dve.drain()
                    dve.tensor_reduce(att_max[:, par, :], sc, AX.X, ALU.max)
                    dve.drain()
                    dve.tensor_scalar(att_bias[:, par, :], att_max[:, par, :], -(HD ** -0.5), None, ALU.mult)\
                       .then_inc(max_ready, 1)

                dve.tensor_scalar(gain_o[:, :], chan[:, K_SUBLN:K_SUBLN + HEADS], 1.0 - LAM_INIT, None,
                                  ALU.mult)
                maxima(0)
                maxima(1)
                for u, (h, qb) in enumerate(UNITS):
                    par, n = u % 2, (qb + 1) * P
                    dve.wait_ge(prob_ready, 2 * (u + 1))
                    dve.reciprocal(att_rec[:, par, :], att_sum[:, par, :])
                    dve.drain()
                    dve.tensor_tensor(att_neg[:, par:par + 1], att_rec[:, par, 1:2], neglam[:, :], ALU.mult)
                    dve.drain()
                    if u >= 2:
                        dve.wait_ge(tr_ready, u - 1)
                    dve.tensor_scalar(comb[:, par, 0:n], prob[:, par, 1, 0:n], att_neg[:, par:par + 1],
                                      None, ALU.mult)
                    dve.drain()
                    dve.scalar_tensor_tensor(comb[:, par, 0:n], prob[:, par, 0, 0:n],
                                             att_rec[:, par, 0:1], comb[:, par, 0:n],
                                             ALU.mult, ALU.add).then_inc(comb_ready, 1)
                    if u + 2 < len(UNITS):
                        maxima(u + 2)
                for h in range(HEADS):
                    inverse_root(N_MEAN["o"] + h, rms_o[:, (h + 1) % HEADS, :])
                    dve.scalar_tensor_tensor(tmpo[:, h, :], oT[:, h, :], gain_o[:, h:h + 1],
                                             rms_o[:, (h + 1) % HEADS, :], ALU.mult, ALU.mult).then_inc(part_ready, 1)
                for h in range(HEADS):
                    lo_part(r1_lo[:, h, :], tmpo[:, h, :], r1_hi[:, h, :], 24 + h + 1)

            for n, (stage, c) in enumerate(CHUNKS):
                if n + 1 < len(CHUNKS):
                    follow(n + 1)
                if stage == "branchA" and c == 0:
                    attention()
                if stage == "gateA":
                    for m in range(2):
                        pooling(2 * c + m)
                elif stage == "pool":
                    for i in range(8):
                        src = tile(stage, i)
                        lo_part(ya_lo[:, i, :], src, ya_hi[:, i, :], 16 + i + 1,
                                chan[:, K_PSCALE + i:K_PSCALE + i + 1], ALU.mult)
                        dve.drain()
                        dve.sem_inc(dve_emptied, 1)
                elif stage == "branchP":
                    for m in range(2):
                        i = 2 * c + m
                        src = tile(stage, i)
                        wait_emptied(dve, "gateA", i)
                        dve.tensor_tensor(mergedP[:, i, :], src, mergedP[:, i, :], ALU.mult)\
                           .then_inc(dve_emptied, 1)
                elif stage in ("q", "k") or (stage == "v" and c == 0):
                    done = 2 * (n - FIRST["q"])
                    for r in range(max(0, done - 2), done):
                        dve.wait_ge(rot_ready, r + 1)
                        if r == 0:
                            dve.wait_ge(sin_done, 2)
                        dst = (qT if r < HEADS else kT)[:, r % HEADS, :]
                        dve.tensor_tensor(q_tmp[:, 0, :], q_raw[:, r % 2, :], rope_cos[:, :], ALU.mult)
                        dve.tensor_tensor(q_tmp[:, 1, :], bank[:, 4 + r % 2, :], rope_sin[:, :], ALU.mult)
                        dve.drain()
                        dve.tensor_tensor(dst, q_tmp[:, 0, :], q_tmp[:, 1, :], ALU.add)\
                           .then_inc(rot_used, 1)
                        dve.drain()
                elif stage == "branchA":
                    for m in range(2):
                        i = 2 * c + m
                        src = tile(stage, i)
                        dve.tensor_tensor(tmpo[:, i, :], src, sigB[:, i, :], ALU.mult)\
                           .then_inc(dve_emptied, 1)
                        dve.drain()
                        dve.tensor_tensor(tmpo[:, i, :], tmpo[:, i, :], mergedP[:, i, :], ALU.add)\
                           .then_inc(part_ready, 1)
                        dve.drain()
                        lo_part(hT_lo[:, i, :], tmpo[:, i, :], hT_hi[:, i, :], 32 + i + 1)
                elif stage == "out":
                    if c == 0:
                        dve.wait_ge(xR_in, 16)
                    for m in range(2):
                        i = 2 * c + m
                        src = tile(stage, i)
                        dve.scalar_tensor_tensor(x1T[:, i, :], src, modc[:, 16 + i:17 + i], xR[:, i, :],
                                                 ALU.mult, ALU.add).then_inc(dve_emptied, 1)
                        dve.drain()
                        dst = sq2[:, min(i, 1), :]
                        dve.tensor_tensor(dst, x1T[:, i, :], x1T[:, i, :], ALU.mult)
                        dve.drain()
                        if i:
                            dve.tensor_tensor(sq2[:, 0, :], sq2[:, 0, :], dst, ALU.add)
                            dve.drain()
                        if i == KT - 1:
                            dve.sem_inc(x1sq_ready, 1)
                    if c == 3:
                        dve.scalar_tensor_tensor(scaleF[:, :], modc[:, 32:40], 1.0,
                                                 chan[:, K_GFFN:K_GFFN + KT], ALU.add, ALU.mult)
                        inverse_root(N_MEAN["norm2"])
                        for k in range(KT):
                            dve.scalar_tensor_tensor(h2T[:, k, :], x1T[:, k, :], scaleF[:, k:k + 1],
                                                     rms1[:, :], ALU.mult, ALU.mult).then_inc(part_ready, 1)
                        for k in range(KT):
                            lo_part(r1_lo[:, k, :], h2T[:, k, :], r1_hi[:, k, :], 40 + k + 1,
                                    modc[:, 24 + k:25 + k])
                        for k in range(KT):
                            dve.tensor_scalar(h2T[:, k, :], h2T[:, k, :], modc[:, 24 + k:25 + k], None,
                                              ALU.add).then_inc(h2_ready, 1)
            for n in range(2):
                dve.tensor_copy(h2row[:, n * S:(n + 1) * S], tile("h2tok", n)).then_inc(dve_emptied, 1)
            for n in range(2):
                src = tile("gaterow", n)
                if n == 0:
                    dve.wait_ge(row_in, 16)
                dve.tensor_tensor(gate_row[:, n * S:(n + 1) * S], src, bias_row[:, n * S:(n + 1) * S],
                                  ALU.add).then_inc(dve_emptied, 1)
            dve.memset(idx3[:, P:P + UN], 0)
            iota = cst[:, C_IOTA:C_IOTA + P]
            grid = [P, PH, TOPK, TOPK]

            def top16(vals, at_, src, left):
                rows_ = range(len(src))
                for n in rows_:
                    dve.max(vals[n][:, 0:8], src[n])
                dve.drain()
                for n in rows_:
                    dve.max_index(at_[n][:, 0:8], vals[n][:, 0:8], src[n])
                    dve.match_replace(left[n], vals[n][:, 0:8], src[n], NEG)
                dve.drain()
                for n in rows_:
                    dve.max(vals[n][:, 8:16], left[n])
                dve.drain()
                for n in rows_:
                    dve.max_index(at_[n][:, 8:16], vals[n][:, 8:16], left[n])
                dve.drain()

            def route(n):
                hp = [(h, half) for h in range(PH) for half in range(2)]
                top16([top_v[:, h, x] for h, x in hp], [top_i[:, h, x] for h, x in hp],
                      [s_cur[:, 2 * h + x] for h, x in hp], [s_left[:, 2 * h + x] for h, x in hp])
                dve.tensor_copy(top_f[:, :, :, :], top_i[:, :, :, :])
                dve.tensor_tensor(cand[:, :, :, :], top_v[:, :, 0].unsqueeze(3).broadcast_to(grid),
                                  top_v[:, :, 1].unsqueeze(2).broadcast_to(grid), ALU.add)
                dve.drain()
                top16([best[:, h] for h in range(PH)], [best_at[:, h] for h in range(PH)],
                      [cand[:, h].rearrange("p a b -> p (a b)") for h in range(PH)],
                      [cand_left[:, h] for h in range(PH)])
                dve.tensor_tensor(logit[:, :, :], best[:, :, :],
                                  best[:, :, 0:1].broadcast_to([P, PH, TOPK]), ALU.subtract)\
                   .then_inc(logit_ready, 1)
                dve.tensor_scalar(best_ab[:, 0], best_at[:, :, :], 4, None, ALU.logical_shift_right)
                dve.tensor_scalar(best_ab[:, 1], best_at[:, :, :], TOPK - 1, None, ALU.bitwise_and)
                dve.drain()
                dve.tensor_copy(best_f[:, :, :, :], best_ab[:, :, :, :])
                dve.drain()
                for x in range(2):
                    dve.tensor_tensor(onehot[:, :], best_f[:, x].unsqueeze(3).broadcast_to(grid),
                                      iota[:, 0:TOPK].unsqueeze(1).unsqueeze(1).broadcast_to(grid),
                                      ALU.is_equal)
                    dve.drain()
                    dve.tensor_tensor(onehot[:, :], onehot[:, :],
                                      top_f[:, :, x].unsqueeze(2).broadcast_to(grid), ALU.mult)
                    dve.drain()
                    dve.tensor_reduce(picked[:, x, :].rearrange("p (a b) -> p a b", a=PH), onehot[:, :],
                                      AX.X, ALU.add)
                    dve.drain()
                dve.wait_ge(exp_done, n + 1)
                dve.tensor_reduce(expsum[:, :], expo[:, :, :], AX.X, ALU.add)
                dve.drain()
                dve.reciprocal(expsum[:, :], expsum[:, :])
                dve.drain()
                return dve.tensor_tensor(picked[:, 2, :].rearrange("p (a b) -> p a b", a=PH),
                                         expo[:, :, :], expsum[:, :].unsqueeze(2)
                                         .broadcast_to([P, PH, TOPK]), ALU.mult)

            dve.wait_ge(cur_ready, 1)
            route(0)
            dve.drain()
            dve.scalar_tensor_tensor(idx3[:, 0:P], picked[:, 0, :], float(NKEYS), picked[:, 1, :],
                                     ALU.mult, ALU.add)
            dve.tensor_copy(share3[:, :], picked[:, 2, :])
            dve.drain()
            dve.sem_inc(idx_ready, 1)
            dve.sem_inc(dot_done, DROWS)
            dve.sem_inc(ulo_ready, 4)
            with dve.Fori(0, DTB) as tb:
                dve.wait_ge(cur_ready, tb + 2)
                dve.sem_inc(dve_step, 1)
                route(tb + 1).then_inc(picked_ready, 1)
                dve.wait_ge(pickTs_ready, tb + 1)
                dve.tensor_tensor(gT_lo[:, :], bank[:, 4, 2 * P:3 * P], gT_hi[:, :].bitcast(f32),
                                  ALU.subtract)
                dve.drain()
                for b in range(P // BT):
                    par, t0 = b % 2, b * BT
                    pair = [P, 2, BT, P]
                    dve.wait_ge(gmm, tb * (P // BT) + b + 1)
                    dve.tensor_tensor(oh_eq[:, par], ijT[:, :, t0:t0 + BT].unsqueeze(3).broadcast_to(pair),
                                      iota.unsqueeze(1).unsqueeze(1).broadcast_to(pair), ALU.is_equal)\
                       .then_inc(eq_ready, 1)
                    dve.drain()
                    dve.tensor_tensor(ohI_hi[:, par], oh_eq[:, par, 0].bitcast(f32),
                                      gT_hi[:, t0:t0 + BT].bitcast(f32).unsqueeze(2)
                                      .broadcast_to([P, BT, P]), ALU.mult).then_inc(ohhi_ready, 1)
                    for k in rows_of_batch(b):
                        dve.wait_ge(d_in[k % DROWS], tb * (16 * ROWS // DROWS) + 16 * (k // DROWS + 1))
                        dve.tensor_tensor_reduce(out=dot_junk[:, :], in0=d_ring[k % DROWS][:, :],
                                                 in1=h2row[:, :], scale=1.0, scalar=0.0, op0=ALU.mult,
                                                 op1=ALU.add, accum_out=pre_s[:, k:k + 1])\
                           .then_inc(dot_done, 1)
                        dve.drain()
                dve.tensor_copy(pre3[:, bass.ds(tb * ROWS, ROWS)], pre_s[:, :])
                dve.drain()
            dve.sem_inc(pre3_ready, 1)
            dve.sem_inc(rows_free, 1)
            dve.wait_ge(pre_done, ET)
            dve.memset(zeros[:, :].bitcast(f32), 0.0)
            dve.memset(accum[:, :], 0.0)
            dve.drain()
            for s_, n in ((zeros_ready, 1), (wf_ready, 4), (g_free, 2), (sum_done, 8)):
                dve.sem_inc(s_, n)

            def up_lo(n, slot):
                dve.wait_ge(uhi_ready, n + 1)
                dve.tensor_tensor(ulo[:, slot, :], uraw[:, slot, :], uhi[:, slot, :].bitcast(f32),
                                  ALU.subtract).then_inc(ulo_ready, 1)

            up_lo(0, 0)
            dve.wait_ge(gel3_ready, 1)
            dve.tensor_tensor(wexp[:, :], gel3[:, :], share3[:, :], ALU.mult)
            dve.drain()
            with dve.Fori(0, ET // UN) as it:
                dve.tensor_copy(wexp_s[:, :], wexp[:, bass.ds(it * UN, UN)])
                dve.drain()
                for e in range(UN):
                    i = it * UN + e
                    if e % GG == 0:
                        dve.wait_ge(g_in[e // GG], 16 * it + 16)
                    dve.wait_ge(ge_in[e % 4], it * (16 * UN // 4) + 16 * (e // 4 + 1))
                    dve.tensor_tensor(wf[:, e % 2, :].rearrange("p (c t) -> p c t", t=GC),
                                      gein[:, e % 4, :].rearrange("p (c t) -> p c t", t=GC),
                                      gtile[:, e // GG, :, (e % GG) * GC:(e % GG + 1) * GC], ALU.mult)\
                       .then_inc(wf_ready, 1)
                    dve.wait_ge(u_in[e % 8], it * (16 * UN // 8) + 16 * (e // 8 + 1))
                    dve.scalar_tensor_tensor(accum[:, :], u_ring[:, e % 8, :], wexp_s[:, e:e + 1],
                                             accum[:, :], ALU.mult, ALU.add).then_inc(sum_done, 1)
                    dve.wait_ge(whi_ready, i + 1)
                    dve.tensor_tensor(w_lo[:, e % 4, :], wf[:, e % 2, :], w_hi[:, e % 4, :].bitcast(f32),
                                      ALU.subtract).then_inc(wlo_ready, 1)
                    up_lo(i + 1, (e + 1) % 4)
                    dve.drain()
                    if e % GG == GG - 1:
                        dve.sem_inc(g_free, 1)
            dve.drain()
            dve.wait_ge(x1b_in, 48)
            dve.wait_ge(psum_done, 1)
            for tb in (3, 0, 1, 2):
                src = accum[:, :] if tb == 3 else bank[:, 2 * tb:2 * tb + 2, :].rearrange("p a b -> p (a b)")
                dve.tensor_tensor(yrow[:, tb, :], src, gate_row[:, :], ALU.mult)
                dve.drain()
                dve.tensor_tensor(yrow[:, tb, :], yrow[:, tb, :], x1tok[:, tb, :], ALU.add)\
                   .then_inc(y_ready, 1)
            dve.wait_ge(ss_ready, 1)
            dve.reciprocal(fin_ss[:, 2, :], fin_ss[:, 1, :])
            dve.drain()
            for tb in range(TB):
                dve.scalar_tensor_tensor(yrow[:, tb, :], yrow[:, tb, :], fin_ss[:, 2, tb:tb + 1],
                                         gain_row[:, :], ALU.mult, ALU.mult).then_inc(out_ready, 1)

        @block.gpsimd
        def _(pool):
            pool.sem_inc(dlo_ready, DR)
            wait_emptied(pool, "score", 15)
            pool.wait_ge(gate_stored, 16)

            def down_lo(i, j):
                slot = (j + 1) % DR
                pool.wait_ge(dhi_ready, i + 1)
                pool.tensor_tensor(dlo[slot][:, :, :].rearrange("p a b -> p (a b)"), draw[:, slot, :],
                                   dhi[:, slot].rearrange("p a b -> p (a b)").bitcast(f32), ALU.subtract)\
                    .then_inc(dlo_ready, 1)

            for i in range(DN0 + DR):
                down_lo(i, i)
            with pool.Fori(0, DTB) as tb:
                for j in range(DNA):
                    down_lo(tb * DN + DN0 + DR + j, DN0 + DR + j)
                pool.wait_ge(idx_ready, 1)
                pool.wait_ge(dot_done, tb * ROWS + DROWS)
                pool.sem_inc(pool_step, 1)
                pool.tensor_copy(idxd[:, :], idx3[:, bass.ds(tb * ROWS, ROWS)]).then_inc(idxd_ready, 1)
                pool.wait_ge(idxd_ready, tb + 1)
                pool.sem_inc(pool_step, 1)
                pool.wait_ge(picked_ready, tb + 1)

                def gather(k):
                    pool.wait_ge(dot_done, tb * ROWS + k + 1)
                    pool.sem_inc(pool_step, 1)
                    pool.indirect_dma_start(
                        out=d_ring[k % DROWS][:, :], out_offset=None, in_=down,
                        in_offset=bass.IndirectOffsetOnAxis(ap=idxd[:, k:k + 1], axis=0))\
                        .then_inc(d_in[k % DROWS], 16)

                for k in range(DROWS):
                    gather(k)
                for b in range(P // BT):
                    for k in rows_of_batch(b):
                        if k + DROWS < ROWS:
                            gather(k + DROWS)
                    for j in after_batch(b):
                        down_lo(tb * DN + DN0 + DR + j, DN0 + DR + j)
            pool.wait_ge(rows_free, 1)
            pool.wait_ge(pre_done, ET)
            pool.wait_ge(sum_done, 8)
            pool.sem_inc(pool_step, 1)
            pool.tensor_copy(idxc[:, :], idx3[:, 0:UN]).then_inc(idxc_ready, 1)
            with pool.Fori(0, ET // UN) as it:
                pool.wait_ge(idxc_ready, it + 1)
                pool.sem_inc(pool_step, 1)
                for e in range(UN):
                    slot = e % 8
                    pool.wait_ge(sum_done, it * UN + e + 1)
                    pool.sem_inc(pool_step, 1)
                    pool.indirect_dma_start(
                        out=u_ring[:, slot, :], out_offset=None, in_=up,
                        in_offset=bass.IndirectOffsetOnAxis(ap=idxc[:, e:e + 1], axis=0))\
                        .then_inc(u_in[slot], 16)
                for slot in range(8):
                    pool.wait_ge(u_in[slot], it * (16 * UN // 8) + 16 * (UN // 8))
                pool.sem_inc(pool_step, 1)
                pool.tensor_copy(idxc[:, :], idx3[:, bass.ds((it + 1) * UN, UN)]).then_inc(idxc_ready, 1)


def constants():
    c = np.zeros((P, C_W), np.float32)
    c[:, C_ID:C_ID + P] = np.eye(P)
    inv = (500000.0 ** (-np.arange(0, ROT, 2) / ROT)).astype(np.float32)
    for p in range(P):
        r = p % HD
        if r < ROT // 2:
            c[p + ROT // 2, C_ROT + p] = -1.0
        elif r < ROT:
            c[p - ROT // 2, C_ROT + p] = 1.0
        if r < ROT:
            c[p, C_FREQ] = inv[r % (ROT // 2)]
    c[:, C_MASK:C_MASK + P] = np.where(np.arange(P)[:, None] >= np.arange(P)[None, :], 0.0, MASKED)
    c[:, C_INV:C_INV + 16] = 1.0 / np.arange(1, 17)
    c[:, C_IOTA:C_IOTA + P] = np.arange(P)
    return c


def kernel(**inputs):
    import concourse.bacc as bacc
    from concourse.bass_utils import run_bass_kernel_spmd

    a = {k: np.asarray(v) for k, v in inputs.items()}

    def chunks(w):
        n = w.shape[1]
        return np.ascontiguousarray(w.reshape(KT, P, n // CH, CH).transpose(2, 1, 0, 3).reshape(n // CH, P, KT * CH))

    def columns(v):
        return v.reshape(-1, P).T

    w_in, w_gate = a["w_in"][0], a["w_gate"][0]
    arrays = {
        "consts": constants(),
        "chans": np.ascontiguousarray(np.concatenate(
            [columns(a[k].reshape(-1)) for k in ("c", "b_ada", "b_gate", "pool_scale", "norm_mix_gain",
                                                 "norm_ffn_gain", "attn_subln_gain")], axis=1)),
        "rows": np.ascontiguousarray(np.broadcast_to(np.concatenate(
            [a["final_norm_gain"], a["b_ada"][0, 5 * D:], a["lambda_q1"][0], a["lambda_k1"][0],
             a["lambda_q2"][0], a["lambda_k2"][0]])[None, :], (P, 2 * D + 4 * HD))),
        "xT": np.ascontiguousarray(a["x"][0].T.reshape(KT, P, S).transpose(1, 0, 2)),
        "pos": np.ascontiguousarray(np.broadcast_to(a["positions"], (P, S))),
        "subk": np.ascontiguousarray(a["peer_sub_keys"][0].transpose(2, 0, 1)),
        "ada": np.ascontiguousarray(a["w_ada"][0].reshape(4, 2, P, 6, D).transpose(3, 0, 2, 1, 4)
                                    .reshape(6, 4, P, 2 * D)),
        "w_xp": chunks(w_in[:, 3 * D:]), "w_q": chunks(w_in[:, :D]), "w_k": chunks(w_in[:, D:2 * D]),
        "w_v": chunks(w_in[:, 2 * D:3 * D]), "w_gateA": chunks(w_gate[:, :D]),
        "w_gateB": chunks(w_gate[:, D:]),
        "w_pool": np.ascontiguousarray(a["pool_w"][0].reshape(4, 2, P, CH).transpose(2, 0, 1, 3)
                                       .reshape(1, P, KT * CH)),
        "w_branchP": chunks(a["w_branch_pool"][0]), "w_branchA": chunks(a["w_branch_attn"][0]),
        "w_out": chunks(a["w_out"][0]), "w_query": chunks(a["peer_w_query"][0]),
        "downT": np.ascontiguousarray(a["peer_down"][0].reshape(ET, P, KT, P).transpose(0, 3, 2, 1)
                                      .reshape(ET, P, D)),
        "down": np.ascontiguousarray(a["peer_down"][0]), "up": np.ascontiguousarray(a["peer_up"][0]),
    }
    nc = bacc.Bacc("TRN2", target_bir_lowering=False, num_devices=1)
    t = {k: nc.dram_tensor("in_" + k, v.shape, mybir.dt.from_np(v.dtype), kind="ExternalInput").ap()
         for k, v in arrays.items()}
    gmat = nc.dram_tensor("gmat", (DT // GC, P, ET, GC), mybir.dt.float32, kind="Internal").ap()
    ged = nc.dram_tensor("ged", (ET, P, DT), mybir.dt.float32, kind="Internal").ap()
    gated = nc.dram_tensor("gated", (P, D), mybir.dt.float32, kind="Internal").ap()
    x1d = nc.dram_tensor("x1d", (P, TB, D), mybir.dt.float32, kind="Internal").ap()
    out = nc.dram_tensor("out", (TB, P, D), mybir.dt.float32, kind="ExternalOutput").ap()
    wdram = {s: t["w_" + s] for s, _ in STAGES}
    layer(nc, t["consts"], t["chans"], t["rows"], t["xT"], t["pos"], t["subk"], t["ada"], wdram,
          t["downT"], t["down"], t["up"], gmat, ged, x1d, gated, out)
    r = run_bass_kernel_spmd(nc, [{"in_" + k: v for k, v in arrays.items()}], core_ids=[0])
    return r.results[0]["out"].reshape(1, S, D)
```
